# Optimizing a Trainium2 kernel written in Bass

```python
import math
import jax
import jax.numpy as jnp
from jax import lax
import numpy as np

D_MODEL = 1024
BATCH = 1
SEQ = 1024
DEPTH = 2

N_MIXERS = 2
N_SWA_LAYERS = (DEPTH + 1) // 2
N_DIFF_LAYERS = DEPTH // 2

HEAD_DIM = 64
QBLK = 128

SWA_HEADS = D_MODEL // HEAD_DIM
SWA_KV_HEADS = SWA_HEADS // 4
SWA_GROUP = SWA_HEADS // SWA_KV_HEADS
WINDOW = 128
KBLK = QBLK + 2 * WINDOW
SWA_QKV_WIDTH = (SWA_HEADS + 2 * SWA_KV_HEADS) * HEAD_DIM

DIFF_HEADS = D_MODEL // (2 * HEAD_DIM)
DIFF_VDIM = 2 * HEAD_DIM
DIFF_QKV_WIDTH = 2 * DIFF_HEADS * HEAD_DIM * 2 + DIFF_HEADS * DIFF_VDIM

N_GROUPS = 4
EXPERTS_PER_GROUP = 8
N_EXPERTS = N_GROUPS * EXPERTS_PER_GROUP
TOP_K = 2
D_EXPERT = D_MODEL // 2
MOE_BLK = 128

NORM_EPS = 1e-6
SUBLN_EPS = 1e-5

kernel_name = "hybrid_swa_diffattn_hmoe_encoder"

def rmsnorm(x, g, eps=NORM_EPS):
    xf = x.astype(jnp.float32)
    y = xf * lax.rsqrt(jnp.mean(xf * xf, axis=-1, keepdims=True) + eps)
    return y.astype(x.dtype) * g

def alibi_slopes(n_heads):
    h = jnp.arange(1, n_heads + 1, dtype=jnp.float32)
    return jnp.exp2(-8.0 * h / n_heads)

def lambda_init_fn(layer_idx):
    return 0.8 - 0.6 * math.exp(-0.3 * layer_idx)

def windowed_gqa_attention(h, w_qkv, w_o, sink):
    b, s, _ = h.shape
    nb = s // QBLK
    qkv = h @ w_qkv
    q = qkv[..., :SWA_HEADS * HEAD_DIM]
    k = qkv[..., SWA_HEADS * HEAD_DIM:(SWA_HEADS + SWA_KV_HEADS) * HEAD_DIM]
    v = qkv[..., (SWA_HEADS + SWA_KV_HEADS) * HEAD_DIM:]
    q = q.reshape(b, s, SWA_KV_HEADS, SWA_GROUP, HEAD_DIM) * (HEAD_DIM ** -0.5)
    k = k.reshape(b, s, SWA_KV_HEADS, HEAD_DIM)
    v = v.reshape(b, s, SWA_KV_HEADS, HEAD_DIM)
    pad = ((0, 0), (WINDOW, WINDOW), (0, 0), (0, 0))
    kp = jnp.pad(k, pad)
    vp = jnp.pad(v, pad)
    qb = q.reshape(b, nb, QBLK, SWA_KV_HEADS, SWA_GROUP, HEAD_DIM).transpose(1, 0, 2, 3, 4, 5)
    slopes = alibi_slopes(SWA_HEADS).reshape(SWA_KV_HEADS, SWA_GROUP)[:, :, None, None]
    sink_l = sink.astype(jnp.float32).reshape(SWA_KV_HEADS, SWA_GROUP)[:, :, None, None]

    def block(args):
        qi, i = args
        start = i * QBLK
        kb = lax.dynamic_slice_in_dim(kp, start, KBLK, axis=1)
        vb = lax.dynamic_slice_in_dim(vp, start, KBLK, axis=1)
        qpos = start + jnp.arange(QBLK)
        kpos = start - WINDOW + jnp.arange(KBLK)
        dist = jnp.abs(qpos[:, None] - kpos[None, :])
        valid = (kpos[None, :] >= 0) & (kpos[None, :] < s) & (dist <= WINDOW)
        logits = jnp.einsum('bqkgd,bskd->bkgqs', qi, kb).astype(jnp.float32)
        logits = logits - slopes * dist.astype(jnp.float32)
        logits = jnp.where(valid, logits, -jnp.inf)
        m = jnp.maximum(jnp.max(logits, axis=-1, keepdims=True), sink_l)
        p = jnp.exp(logits - m)
        denom = jnp.sum(p, axis=-1, keepdims=True) + jnp.exp(sink_l - m)
        probs = (p / denom).astype(vb.dtype)
        return jnp.einsum('bkgqs,bskd->bqkgd', probs, vb)

    out = lax.map(block, (qb, jnp.arange(nb)))
    out = out.transpose(1, 0, 2, 3, 4, 5).reshape(b, s, SWA_HEADS * HEAD_DIM)
    return out @ w_o

def differential_attention(h, w_qkv, w_o, lam, subln_g, lambda_init):
    b, s, _ = h.shape
    nb = s // QBLK
    qk_w = 2 * DIFF_HEADS * HEAD_DIM
    qkv = h @ w_qkv
    q = qkv[..., :qk_w].reshape(b, s, DIFF_HEADS, 2, HEAD_DIM) * (HEAD_DIM ** -0.5)
    k = qkv[..., qk_w:2 * qk_w].reshape(b, s, DIFF_HEADS, 2, HEAD_DIM)
    v = qkv[..., 2 * qk_w:].reshape(b, s, DIFF_HEADS, DIFF_VDIM)
    lamf = lam.astype(jnp.float32)
    lam_full = (jnp.exp(jnp.sum(lamf[0] * lamf[1])) - jnp.exp(jnp.sum(lamf[2] * lamf[3]))
                + lambda_init)
    slopes = alibi_slopes(DIFF_HEADS)[None, :, None, None, None]
    kpos = jnp.arange(s)
    qb = q.reshape(b, nb, QBLK, DIFF_HEADS, 2, HEAD_DIM).transpose(1, 0, 2, 3, 4, 5)

    def block(args):
        qi, i = args
        qpos = i * QBLK + jnp.arange(QBLK)
        dist = jnp.abs(qpos[:, None] - kpos[None, :]).astype(jnp.float32)
        logits = jnp.einsum('bqhcd,bshcd->bhcqs', qi, k).astype(jnp.float32) - slopes * dist
        a = jax.nn.softmax(logits, axis=-1)
        wmap = a[:, :, 0] - lam_full * a[:, :, 1]
        return jnp.einsum('bhqs,bshe->bqhe', wmap.astype(v.dtype), v)

    o = lax.map(block, (qb, jnp.arange(nb)))
    o = o.transpose(1, 0, 2, 3, 4).reshape(b, s, DIFF_HEADS, DIFF_VDIM)
    o = rmsnorm(o, subln_g, eps=SUBLN_EPS) * (1.0 - lambda_init)
    return o.reshape(b, s, DIFF_HEADS * DIFF_VDIM) @ w_o

def hierarchical_moe(h, w_group, b_group, w_router, b_router, w_gate, w_up, w_down):
    b, s, d = h.shape
    x2 = h.reshape(b * s, d)
    n = x2.shape[0]
    lg = (x2 @ w_group + b_group).astype(jnp.float32)
    pg_all = jax.nn.softmax(lg, axis=-1)
    g = jnp.argmax(lg, axis=-1)
    pg = jnp.take_along_axis(pg_all, g[:, None], axis=1)[:, 0]
    le = (x2 @ w_router + b_router).astype(jnp.float32).reshape(n, N_GROUPS, EXPERTS_PER_GROUP)
    le = jnp.take_along_axis(le, g[:, None, None], axis=1)[:, 0]
    pe = jax.nn.softmax(le, axis=-1)
    top_p, top_i = lax.top_k(pe, TOP_K)
    top_p = top_p / jnp.sum(top_p, axis=-1, keepdims=True)
    weights = pg[:, None] * top_p
    eid = g[:, None] * EXPERTS_PER_GROUP + top_i

    flat_e = eid.reshape(-1)
    flat_w = weights.reshape(-1)
    flat_t = jnp.arange(n * TOP_K) // TOP_K
    order = jnp.argsort(flat_e)
    se, st, sw = flat_e[order], flat_t[order], flat_w[order]
    counts = jnp.zeros((N_EXPERTS,), jnp.int32).at[flat_e].add(1)
    padded = ((counts + MOE_BLK - 1) // MOE_BLK) * MOE_BLK
    start = jnp.cumsum(counts) - counts
    pend = jnp.cumsum(padded)
    pstart = pend - padded
    dest = pstart[se] + (jnp.arange(n * TOP_K) - start[se])
    cap = n * TOP_K + N_EXPERTS * MOE_BLK
    n_blocks = cap // MOE_BLK
    slot_tok = jnp.zeros((cap,), jnp.int32).at[dest].set(st)
    slot_w = jnp.zeros((cap,), x2.dtype).at[dest].set(sw.astype(x2.dtype))
    block_e = jnp.minimum(jnp.searchsorted(pend, jnp.arange(n_blocks) * MOE_BLK, side='right'),
                          N_EXPERTS - 1)
    xs = x2[slot_tok].reshape(n_blocks, MOE_BLK, d)

    def expert_block(args):
        xb, e = args
        hid = jax.nn.silu(xb @ w_gate[e]) * (xb @ w_up[e])
        return hid @ w_down[e]

    ys = lax.map(expert_block, (xs, block_e)).reshape(cap, d)
    out = jnp.zeros_like(x2).at[slot_tok].add(ys * slot_w[:, None])
    return out.reshape(b, s, d)

def setup_inputs(seed: int = 0) -> dict:
    key = jax.random.key(seed)
    ks = jax.random.split(key, 20)
    f32 = jnp.float32
    nrm = lambda k, shape, scale: jax.random.normal(k, shape, f32) * scale
    return {
        "x": jax.random.normal(ks[0], (BATCH, SEQ, D_MODEL), f32),
        "norm_mix": 1.0 + nrm(ks[1], (DEPTH, D_MODEL), 0.02),
        "norm_ffn": 1.0 + nrm(ks[2], (DEPTH, D_MODEL), 0.02),
        "swa_w_qkv": nrm(ks[3], (N_SWA_LAYERS, D_MODEL, SWA_QKV_WIDTH), D_MODEL ** -0.5),
        "swa_w_o": nrm(ks[4], (N_SWA_LAYERS, SWA_HEADS * HEAD_DIM, D_MODEL), (SWA_HEADS * HEAD_DIM) ** -0.5),
        "swa_sink": nrm(ks[5], (N_SWA_LAYERS, SWA_HEADS), 0.5),
        "diff_w_qkv": nrm(ks[6], (N_DIFF_LAYERS, D_MODEL, DIFF_QKV_WIDTH), D_MODEL ** -0.5),
        "diff_w_o": nrm(ks[7], (N_DIFF_LAYERS, DIFF_HEADS * DIFF_VDIM, D_MODEL), (DIFF_HEADS * DIFF_VDIM) ** -0.5),
        "diff_lambda": nrm(ks[8], (N_DIFF_LAYERS, 4, HEAD_DIM), 0.1),
        "diff_subln": 1.0 + nrm(ks[9], (N_DIFF_LAYERS, DIFF_VDIM), 0.02),
        "moe_w_group": nrm(ks[10], (DEPTH, D_MODEL, N_GROUPS), D_MODEL ** -0.5),
        "moe_b_group": nrm(ks[11], (DEPTH, N_GROUPS), 0.01),
        "moe_w_router": nrm(ks[12], (DEPTH, D_MODEL, N_EXPERTS), D_MODEL ** -0.5),
        "moe_b_router": nrm(ks[13], (DEPTH, N_EXPERTS), 0.01),
        "moe_w_gate": nrm(ks[14], (DEPTH, N_EXPERTS, D_MODEL, D_EXPERT), D_MODEL ** -0.5),
        "moe_w_up": nrm(ks[15], (DEPTH, N_EXPERTS, D_MODEL, D_EXPERT), D_MODEL ** -0.5),
        "moe_w_down": nrm(ks[16], (DEPTH, N_EXPERTS, D_EXPERT, D_MODEL), D_EXPERT ** -0.5),
        "final_norm": 1.0 + nrm(ks[17], (D_MODEL,), 0.02),
    }

def reference(x, norm_mix, norm_ffn, swa_w_qkv, swa_w_o, swa_sink, diff_w_qkv, diff_w_o,
              diff_lambda, diff_subln, moe_w_group, moe_b_group, moe_w_router, moe_b_router,
              moe_w_gate, moe_w_up, moe_w_down, final_norm):
    for i in range(DEPTH):
        hn = rmsnorm(x, norm_mix[i])
        j = i // N_MIXERS
        if i % N_MIXERS == 0:
            x = x + windowed_gqa_attention(hn, swa_w_qkv[j], swa_w_o[j], swa_sink[j])
        else:
            x = x + differential_attention(hn, diff_w_qkv[j], diff_w_o[j], diff_lambda[j],
                                           diff_subln[j], lambda_init_fn(i))
        x = x + hierarchical_moe(rmsnorm(x, norm_ffn[i]), moe_w_group[i], moe_b_group[i],
                                 moe_w_router[i], moe_b_router[i], moe_w_gate[i],
                                 moe_w_up[i], moe_w_down[i])
    return rmsnorm(x, final_norm)


_drawn_inputs = setup_inputs


def setup_inputs(seed=0):
    import zlib

    import numpy as np

    out = dict(_drawn_inputs(seed))
    spreads = {}
    factors = {}
    for name, (base, spread) in spreads.items():
        noise = np.random.default_rng([zlib.crc32(name.encode()), seed]).standard_normal(out[name].shape)
        drawn = base * np.exp(spread * noise) if base else spread * noise
        out[name] = jnp.asarray(drawn.astype(out[name].dtype))
    for name, factor in factors.items():
        out[name] = (out[name] * factor).astype(out[name].dtype)
    return out
```

```python
import math
from contextlib import ExitStack

import concourse.bass as bass
from concourse import mybir

F32 = mybir.dt.float32
F32R = mybir.dt.float32r
I32 = mybir.dt.int32
ALU = mybir.AluOpType
ACT = mybir.ActivationFunctionType
AX = mybir.AxisListType.X

P = 128
T = 1024
D = 1024
NT = T // P
KD = D // P
HALF = 512
HEAD = 64
Q_SCALE = HEAD ** -0.5
NORM_EPS = 1e-6
SUBLN_EPS = 1e-5
MASKED = -1e30
HALVES = (slice(0, 64), slice(64, 128))

GROUPS = 4
PER_GROUP = 8
EXPERTS = GROUPS * PER_GROUP
HIDDEN = 512
KH = HIDDEN // P
TOP_K = 2
CAP = 96
SPARE = T * TOP_K // CAP
ROWS = EXPERTS + SPARE
COLS = ROWS + 2
STEPS = T // CAP


class Step:

    def __init__(self, eng, sem, base=0):
        self.eng, self.sem, self.base, self.n = eng, sem, base, 0

    def __call__(self, instruction):
        self.n += 1
        instruction.then_inc(self.sem, 1)
        self.eng.wait_ge(self.sem, self.base + self.n)


def wait_count(eng, sem, count):
    if not (isinstance(count, int) and count == 0):
        eng.wait_ge(sem, count)


def wait_apart(eng, sem, count, passed):
    eng.wait_ge(sem, count)
    eng.sem_inc(passed, 1)


class Trunk:
    def __init__(self, nc, stack):
        self.nc, self.stack, self.used = nc, stack, []

    def sem(self, name):
        handle = self.nc.alloc_semaphore(name=name)
        self.used.append(handle)
        return handle

    def clear_semaphores(self):
        numbers = sorted(h.num for h in self.used)
        spans = []
        for n in numbers:
            if spans and spans[-1][1] == n:
                spans[-1][1] = n + 1
            else:
                spans.append([n, n + 1])
        with self.nc.Block() as block:
            @block.gpsimd
            def _(pool):
                for a, b in spans:
                    pool.sem_clear(range(a, b))
        for h in self.used:
            self.nc.release_semaphore(h)
        self.used = []


def setup(t, x):
    nc = t.nc
    keep = t.stack.enter_context
    t.x = keep(nc.sbuf_tensor("x_res", [P, NT, D], F32))
    t.ident = keep(nc.sbuf_tensor("ident", [P, P], F32))
    t.zero_col = keep(nc.sbuf_tensor("zero_col", [P, 1], F32))
    made, loaded = t.sem("const_made"), t.sem("x_loaded")
    with nc.Block() as block:
        @block.sync
        def _(sp):
            for tt in range(NT):
                sp.dma_start(t.x[:, tt, :], x[0, tt * P:(tt + 1) * P, :]).then_inc(loaded, 16)
            sp.wait_ge(loaded, 16 * NT)

        @block.gpsimd
        def _(pool):
            pool.memset(t.ident[:, :], 0.0).then_inc(made, 1)
            pool.memset(t.zero_col[:, :], 0.0)
            pool.wait_ge(made, 1)
            pool.affine_select(out=t.ident[:, :], in_=t.ident[:, :], compare_op=ALU.not_equal, fill=1.0,
                               base=0, pattern=[[-1, P]], channel_multiplier=1).then_inc(made, 1)


class Norm:

    def __init__(self, t, name, gain, sb, ps, rows_dram=None):
        nc = t.nc
        self.t, self.gain, self.rows_dram = t, gain, rows_dram
        self.gain_b = sb(f"{name}_gain", [P, D], F32)
        self.junk_a = sb(f"{name}_junk_a", [P, D], F32)
        self.hn = sb(f"{name}_hn", [P, 2, D], F32)
        self.ssq = sb(f"{name}_ssq", [P, NT], F32)
        self.rms = sb(f"{name}_rms", [P, NT], F32)
        self.rstd = sb(f"{name}_rstd", [P, NT], F32)
        self.hnT = sb(f"{name}_hnT", [P, KD, T], F32)
        self.banks = ps
        s = lambda what: t.sem(f"{name}_{what}")
        self.gain_loaded, self.act_sq, self.dve_sq = s("gain_loaded"), s("act_sq"), s("dve_sq")
        self.ms_ready, self.rms_ready, self.chain = s("ms_ready"), s("rms_ready"), s("chain")
        self.hn_ready, self.turned = s("hn_ready"), s("turned")
        self.act_copied, self.dve_copied = s("act_copied"), s("dve_copied")
        self.rows_stored = (s("even_rows_stored"), s("odd_rows_stored"))

    def sync_load(self, sp):
        sp.dma_start(self.gain_b[:, :], self.gain.broadcast_to((P, D))).then_inc(self.gain_loaded, 16)

    def sync_store(self, sp):
        for tt in range(NT):
            sp.wait_ge(self.hn_ready, tt + 1)
            sp.dma_start(self.rows_dram[tt * P:(tt + 1) * P, :], self.hn[:, tt % 2, :]).then_inc(self.rows_stored[tt % 2], 16)
        for stored in self.rows_stored:
            sp.wait_ge(stored, 16 * NT // 2)

    def scalar(self, act):
        for tt in range(0, NT, 2):
            if tt:
                act.wait_ge(self.act_sq, tt // 2)
            act.activation(self.junk_a[:, :], self.t.x[:, tt, :], ACT.Square, bias=self.t.zero_col[:, :],
                           accum_out=self.ssq[:, tt:tt + 1]).then_inc(self.act_sq, 1)
        act.wait_ge(self.ms_ready, 1)
        act.activation(self.rms[:, :], self.ssq[:, :], ACT.Sqrt, bias=self.t.zero_col[:, :]).then_inc(self.rms_ready, 1)
        for tt in range(NT):
            act.wait_ge(self.turned, 2 * tt + 1)
            act.copy(self.hnT[:, 0:KD // 2, tt * P:(tt + 1) * P], self.banks[:, 2 * (tt % 2), :]
                     .rearrange("p (k n) -> p k n", k=4)).then_inc(self.act_copied, 1)

    def vector(self, dve):
        for tt in range(1, NT, 2):
            if tt > 1:
                dve.wait_ge(self.dve_sq, tt // 2)
            dve.tensor_tensor_reduce(self.hn[:, 0, :], self.t.x[:, tt, :], self.t.x[:, tt, :], 1.0, 0.0,
                                     ALU.mult, ALU.add, self.ssq[:, tt:tt + 1]).then_inc(self.dve_sq, 1)
        dve.wait_ge(self.act_sq, NT // 2)
        dve.wait_ge(self.dve_sq, NT // 2)
        dve.tensor_scalar(self.ssq[:, :], self.ssq[:, :], 1.0 / D, NORM_EPS, ALU.mult, ALU.add)\
           .then_inc(self.ms_ready, 1)
        dve.wait_ge(self.rms_ready, 1)
        dve.reciprocal(self.rstd[:, :], self.rms[:, :]).then_inc(self.chain, 1)
        dve.wait_ge(self.chain, 1)
        dve.wait_ge(self.gain_loaded, 16)

        def copy_half(tt):
            dve.wait_ge(self.turned, 2 * tt + 2)
            dve.tensor_copy(self.hnT[:, KD // 2:KD, tt * P:(tt + 1) * P], self.banks[:, 2 * (tt % 2) + 1, :]
                            .rearrange("p (k n) -> p k n", k=4)).then_inc(self.dve_copied, 1)

        for tt in range(NT):
            if tt >= 2:
                dve.wait_ge(self.turned, 2 * (tt - 1))
                if self.rows_dram is not None:
                    dve.wait_ge(self.rows_stored[tt % 2], 16 * (tt // 2))
            dve.scalar_tensor_tensor(
                out=self.hn[:, tt % 2, :].rearrange("q (k p) -> q p k", k=KD),
                in0=self.t.x[:, tt, :].rearrange("q (p k) -> q p k", k=KD), scalar=self.rstd[:, tt:tt + 1],
                in1=self.gain_b[:, :].rearrange("q (p k) -> q p k", k=KD), op0=ALU.mult, op1=ALU.mult)\
               .then_inc(self.hn_ready, 1)
            if tt >= 1:
                copy_half(tt - 1)
        copy_half(NT - 1)

    def tensor(self, pe):
        for tt in range(NT):
            pe.wait_ge(self.hn_ready, tt + 1)
            for b, copied in enumerate((self.act_copied, self.dve_copied)):
                if tt >= 2:
                    pe.wait_ge(copied, tt - 1)
                for k in range(4):
                    kk = 4 * b + k
                    last = pe.transpose(self.banks[:, 2 * (tt % 2) + b, k * P:(k + 1) * P],
                                        self.hn[:, tt % 2, kk * P:(kk + 1) * P], self.t.ident[:, :])
                last.then_inc(self.turned, 1)

    def ready(self, eng):
        eng.wait_ge(self.act_copied, NT)
        eng.wait_ge(self.dve_copied, NT)


class OutProjection:

    def __init__(self, t, name, w_o, oT, w_sb, banks, rows):
        self.t, self.w_o, self.oT, self.w_sb, self.banks, self.rows = t, w_o, oT, w_sb, banks, rows
        s = lambda what: t.sem(f"{name}_{what}")
        self.loaded, self.done, self.added = s("wo_loaded"), s("wo_done"), s("wo_added")

    def sync_load(self, sp):
        sp.dma_start(self.w_sb[:, :, :], self.w_o.rearrange("(k p) n -> p k n", p=P)).then_inc(self.loaded, 16)

    def tensor(self, pe, tt, oT=None):
        oT = self.oT[:, :, tt * P:(tt + 1) * P] if oT is None else oT
        for n in range(2):
            bank = 2 * (tt % 2) + n
            if tt >= 2:
                pe.wait_ge(self.added, 2 * (tt - 2) + n + 1)
            for k in range(KD):
                last = pe.matmul(self.banks[:, bank, :], oT[:, k, :],
                                 self.w_sb[:, k, n * HALF:(n + 1) * HALF], start=(k == 0), stop=(k == KD - 1))
            last.then_inc(self.done, 1)

    def vector(self, dve, tt):
        for n in range(2):
            dve.wait_ge(self.done, 2 * tt + n + 1)
            xs = self.t.x[:, tt, n * HALF:(n + 1) * HALF]
            dve.tensor_tensor(xs, self.banks[:, 2 * (tt % 2) + n, :], xs, ALU.add).then_inc(self.added, 1)


def windowed_attention(t, gain, w_qkv, w_o, sink):
    nc = t.nc
    KV = 4
    QH = 4
    NQ = KV * QH
    WIN = 3 * P
    W_COLS = QH * HEAD + 2 * HEAD
    blocks = [(max(i - 1, 0), min(i + 1, NT - 1)) for i in range(NT)]
    tiles = [b - a + 1 for a, b in blocks]
    before = [sum(tiles[:i]) for i in range(NT)]
    TILES = sum(tiles)
    with ExitStack() as ctx:
        sb = lambda *a: ctx.enter_context(nc.sbuf_tensor(*a))
        S = ctx.enter_context(nc.psum_tensor("a0_S", [P, 4, HALF], F32))
        TB = ctx.enter_context(nc.psum_tensor("a0_T", [P, 2, HALF], F32))
        O = ctx.enter_context(nc.psum_tensor("a0_O", [P, 2, HALF], F32))
        norm = Norm(t, "a0n", gain, sb, S)
        w_sb = sb("a0_w", [P, KD, W_COLS], F32)
        q_parts = sb("a0_q_parts", [P, QH, T], F32R)
        k_hi, k_lo = sb("a0_k_hi", [P, T], F32R), sb("a0_k_lo", [P, T], F32R)
        kvT = sb("a0_kvT", [P, T], F32)
        v_rows = sb("a0_v_rows", [P, NT, 2, HEAD], F32)
        probs = sb("a0_probs", [P, 2, QH, WIN], F32)
        pT = sb("a0_pT", [P, 2, 3, QH * P], F32)
        bias = sb("a0_bias", [P, QH, WIN], F32)
        dist = sb("a0_dist", [P, WIN], F32)
        zero_rows = sb("a0_zero_rows", [CAP, D], F32)
        far = sb("a0_far", [P, WIN], F32)
        sinks = sb("a0_sinks", [P, NQ], F32)
        sink4 = sb("a0_sink4", [P, QH], F32)
        top4 = sb("a0_top4", [P, 2, QH], F32)
        neg4 = sb("a0_neg4", [P, 2, QH], F32)
        snk4 = sb("a0_snk4", [P, 2, QH], F32)
        sum4 = sb("a0_sum4", [P, 2, QH], F32)
        exs4 = sb("a0_exs4", [P, 2, QH], F32)
        inv4 = sb("a0_inv4", [P, 2, QH], F32)
        oT = sb("a0_oT", [P, KD, T], F32)
        out_proj = OutProjection(t, "a0o", w_o, oT, norm.hnT, S, None)

        w_loaded, sink_loaded = t.sem("a0_w_loaded"), t.sem("a0_sink_loaded")
        proj_done, hi_ready, parts_ready = t.sem("a0_proj_done"), t.sem("a0_hi_ready"), t.sem("a0_parts_ready")
        v_turned, v_rows_ready = t.sem("a0_v_turned"), t.sem("a0_v_rows_ready")
        scores, scores_seen, biased = t.sem("a0_scores"), t.sem("a0_scores_seen"), t.sem("a0_biased")
        stats, exp_done, probs_ready = t.sem("a0_stats"), t.sem("a0_exp_done"), t.sem("a0_probs_ready")
        p_turned, pT_ready = t.sem("a0_p_turned"), t.sem("a0_pT_ready")
        pv_done, oT_ready = t.sem("a0_pv_done"), t.sem("a0_oT_ready")
        spare_zeroed = t.sem("spare_zeroed")
        dve_own, prep, zeroed, iota_done = t.sem("a0_dve_own"), t.sem("a0_prep"), t.sem("a0_zeroed"), t.sem("a0_iota")

        with nc.Block() as block:
            @block.sync
            def _(sp):
                norm.sync_load(sp)
                sp.dma_start(sinks[:, :], sink.broadcast_to((P, NQ))).then_inc(sink_loaded, 16)

                def load_weights(g):
                    for at, n, col in ((0, QH * HEAD, g * (QH * HEAD)), (QH * HEAD, HEAD, NQ * HEAD + g * HEAD),
                                       (QH * HEAD + HEAD, HEAD, (NQ + KV) * HEAD + g * HEAD)):
                        sp.dma_start(w_sb[:, :, at:at + n],
                                     w_qkv.rearrange("(p k) n -> p k n", k=KD)[:, :, bass.ds(col, n)])\
                          .then_inc(w_loaded, 16)

                load_weights(0)
                with sp.Fori(1, KV) as g:
                    sp.wait_ge(proj_done, 6 * g)
                    load_weights(g)
                sp.wait_ge(proj_done, 6 * KV)
                out_proj.sync_load(sp)
                sp.wait_ge(zeroed, 1)
                spare_rows = t.dram[2].rearrange("(r c) n -> r c n", c=CAP)[EXPERTS:ROWS]
                sp.dma_start(spare_rows.rearrange("r c n -> c r n"), zero_rows[:, :].unsqueeze(1)
                             .broadcast_to((CAP, SPARE, D))).then_inc(spare_zeroed, 16)
                sp.wait_ge(spare_zeroed, 16)

            @block.gpsimd
            def _(pool):
                pool.iota(dist[:, :].bitcast(I32), pattern=[[-1, WIN]], base=P, channel_multiplier=1).then_inc(iota_done, 1)
                pool.memset(zero_rows[:, :], 0.0).then_inc(zeroed, 1)

            @block.scalar
            def _(act):
                norm.scalar(act)
                with act.Fori(0, KV) as g:
                    for o in range(6):
                        act.wait_ge(proj_done, 6 * g + o + 1)
                        j, n = divmod(o, 2)
                        cols = slice(n * HALF, (n + 1) * HALF)
                        if j < 2:
                            for e, part in enumerate(HALVES):
                                last = act.mul(q_parts[part, 2 * j + e, cols], S[part, o % 4, :], Q_SCALE)
                            last.then_inc(hi_ready, 1)
                        else:
                            for there in HALVES:
                                act.copy(k_hi[there, cols], S[0:64, o % 4, :])
                            act.copy(kvT[:, cols], S[:, o % 4, :]).then_inc(hi_ready, 1)

                    def exponentials(i):
                        n = 8 * g + i
                        act.wait_ge(stats, n + 1)
                        for h in range(QH):
                            row = probs[:, i % 2, h, 0:tiles[i] * P]
                            act.activation(row, row, ACT.Exp, bias=neg4[:, i % 2, h:h + 1],
                                           accum_out=sum4[:, i % 2, h:h + 1])
                        act.activation(exs4[:, i % 2, :], snk4[:, i % 2, :], ACT.Exp, bias=t.zero_col[:, :])\
                           .then_inc(exp_done, 1)

                    exponentials(0)
                    for i in range(NT):
                        if i + 1 < NT:
                            exponentials(i + 1)
                        n = 8 * g + i
                        if i >= 2:
                            act.wait_ge(pv_done, n - 1)
                        for j in range(tiles[i]):
                            c = TILES * g + before[i] + j
                            act.wait_ge(p_turned, c + 1)
                            act.copy(pT[:, i % 2, j, :], TB[:, (before[i] + j) % 2, :]).then_inc(pT_ready, 1)

            @block.vector
            def _(dve):
                own = Step(dve, prep)
                dve.wait_ge(iota_done, 1)
                own(dve.tensor_copy(far[:, :], dist[:, :].bitcast(I32)))
                own(dve.tensor_scalar(dist[:, :], far[:, :], -1.0, None, ALU.mult))
                own(dve.tensor_tensor(dist[:, :], dist[:, :], far[:, :], ALU.max))
                own(dve.tensor_scalar(far[:, :], dist[:, :], float(P), MASKED, ALU.is_gt, ALU.mult))
                for h in range(QH):
                    last = dve.scalar_tensor_tensor(out=bias[:, h, :], in0=dist[:, :], scalar=-2.0 ** (-8.0 * (h + 1) / NQ),
                                                    in1=far[:, :], op0=ALU.mult, op1=ALU.add)
                own(last)
                norm.vector(dve)
                dve.wait_ge(sink_loaded, 16)
                OWN = 4 + 5 * NT
                with dve.Fori(0, KV) as g:
                    own = Step(dve, dve_own, OWN * g)
                    own(dve.tensor_copy(sink4[:, :], sinks[:, bass.ds(g * QH, QH)]))
                    for o in range(6):
                        dve.wait_ge(hi_ready, 6 * g + o + 1)
                        j, n = divmod(o, 2)
                        cols = slice(n * HALF, (n + 1) * HALF)
                        for e, part in enumerate(HALVES):
                            if j < 2:
                                q = q_parts[:, 2 * j + e, cols]
                                last = dve.scalar_tensor_tensor(out=q[HALVES[1 - e]], in0=S[part, o % 4, :], scalar=Q_SCALE,
                                                                in1=q[part].bitcast(F32), op0=ALU.mult, op1=ALU.subtract)
                            else:
                                last = dve.tensor_tensor(k_lo[part, cols], S[0:64, o % 4, :],
                                                         k_hi[0:64, cols].bitcast(F32), ALU.subtract)
                        last.then_inc(parts_ready, 1)
                    for b in range(2):
                        dve.wait_ge(v_turned, 2 * g + b + 1)
                        source = TB[:, b, :].rearrange("p (a c) -> p a c", c=P)[:, :, HEAD:P]
                        for copy in range(2):
                            last = dve.tensor_copy(v_rows[:, 4 * b:4 * b + 4, copy, :], source)
                        last.then_inc(v_rows_ready, 1)

                    def masked_scores(i):
                        n = 8 * g + i
                        first = P if i == 0 else 0
                        width = tiles[i] * P
                        if i >= 2:
                            dve.wait_ge(p_turned, TILES * g + before[i - 1])
                        for h in range(QH):
                            wait_apart(dve, scores, 4 * n + h + 1, scores_seen)
                            dve.tensor_tensor_reduce(probs[:, i % 2, h, 0:width], S[:, h, 0:width],
                                                     bias[:, h, first:first + width], 1.0, MASKED,
                                                     ALU.add, ALU.max, top4[:, i % 2, h:h + 1]).then_inc(biased, 1)
                        dve.wait_ge(biased, 4 * n + 4)
                        own(dve.tensor_tensor(top4[:, i % 2, :], top4[:, i % 2, :], sink4[:, :], ALU.max))
                        own(dve.tensor_scalar(neg4[:, i % 2, :], top4[:, i % 2, :], -1.0, None, ALU.mult))
                        dve.tensor_tensor(snk4[:, i % 2, :], sink4[:, :], top4[:, i % 2, :], ALU.subtract).then_inc(stats, 1)

                    def normalise(i):
                        n = 8 * g + i
                        dve.wait_ge(exp_done, n + 1)
                        own(dve.tensor_tensor(sum4[:, i % 2, :], sum4[:, i % 2, :], exs4[:, i % 2, :], ALU.add))
                        own(dve.reciprocal(inv4[:, i % 2, :], sum4[:, i % 2, :]))
                        for h in range(QH):
                            row = probs[:, i % 2, h, 0:tiles[i] * P]
                            last = dve.tensor_scalar(row, row, inv4[:, i % 2, h:h + 1], None, ALU.mult)
                        last.then_inc(probs_ready, 1)

                    def heads_out(i):
                        dve.wait_ge(pv_done, 8 * g + i + 1)
                        out = O[:, i % 2, :].rearrange("p (h n) -> p h n", h=QH)
                        for e, part in enumerate((slice(0, 64), slice(64, 128))):
                            last = dve.tensor_copy(oT[part, bass.ds(2 * g, 2), i * P:(i + 1) * P], out[part, e:QH:2, :])
                        last.then_inc(oT_ready, 1)

                    masked_scores(0)
                    for i in range(NT):
                        if i + 1 < NT:
                            masked_scores(i + 1)
                        normalise(i)
                        if i >= 1:
                            heads_out(i - 1)
                    heads_out(NT - 1)
                    own(dve.tensor_scalar(bias[:, :, :], bias[:, :, :], 2.0 ** (-8.0 * QH / NQ), None, ALU.mult))
                    while own.n < OWN:
                        own(dve.tensor_copy(exs4[:, 0, 0:1], sink4[:, 0:1]))
                    assert own.n == OWN
                for tt in range(NT):
                    out_proj.vector(dve, tt)

            @block.tensor
            def _(pe):
                norm.tensor(pe)
                norm.ready(pe)
                with pe.Fori(0, KV) as g:
                    pe.wait_ge(w_loaded, 48 * g + 48)
                    for o in range(6):
                        j, n = divmod(o, 2)
                        if o >= 4:
                            pe.wait_ge(parts_ready, 6 * g + o - 3)
                        for k in range(KD):
                            last = pe.matmul(S[:, o % 4, :], w_sb[:, k, j * P:(j + 1) * P],
                                             norm.hnT[:, k, n * HALF:(n + 1) * HALF], start=(k == 0), stop=(k == KD - 1))
                        last.then_inc(proj_done, 1)
                    for b in range(2):
                        pe.wait_ge(hi_ready, 6 * g + 5 + b)
                        for a in range(4):
                            last = pe.transpose(TB[:, b, a * P:(a + 1) * P], kvT[:, (4 * b + a) * P:(4 * b + a + 1) * P],
                                                t.ident[:, :])
                        last.then_inc(v_turned, 1)
                    pe.wait_ge(parts_ready, 6 * g + 6)
                    pe.wait_ge(v_rows_ready, 2 * g + 2)

                    def head_scores(i):
                        n = 8 * g + i
                        a, b = blocks[i]
                        for h in range(QH):
                            if i >= 1:
                                pe.wait_ge(biased, 4 * (n - 1) + h + 1)
                            for k_part in (k_hi, k_lo):
                                last = pe.matmul(S[:, h, 0:tiles[i] * P], q_parts[:, h, i * P:(i + 1) * P],
                                                 k_part[:, a * P:(b + 1) * P], start=(k_part is k_hi), stop=(k_part is k_lo))
                            last.then_inc(scores, 1)

                    def product(i):
                        n = 8 * g + i
                        pe.wait_ge(probs_ready, n + 1)

                        def turn(j):
                            c = TILES * g + before[i] + j
                            if before[i] + j >= 2:
                                pe.wait_ge(pT_ready, c - 1)
                            for h in range(QH):
                                last = pe.transpose(TB[:, (before[i] + j) % 2, h * P:(h + 1) * P],
                                                    probs[:, i % 2, h, j * P:(j + 1) * P], t.ident[:, :])
                            last.then_inc(p_turned, 1)

                        def times_v(j):
                            c = TILES * g + before[i] + j
                            pe.wait_ge(pT_ready, c + 1)
                            return pe.matmul(O[:, i % 2, :],
                                             v_rows[:, blocks[i][0] + j, :, :].rearrange("p a b -> p (a b)"),
                                             pT[:, i % 2, j, :], start=(j == 0), stop=(j == tiles[i] - 1))

                        turn(0)
                        turn(1)
                        if i >= 2:
                            pe.wait_ge(oT_ready, n - 1)
                        times_v(0)
                        if tiles[i] == 3:
                            turn(2)
                            times_v(1)
                        times_v(tiles[i] - 1).then_inc(pv_done, 1)

                    head_scores(0)
                    head_scores(1)
                    for i in range(NT):
                        if i + 2 < NT:
                            head_scores(i + 2)
                        product(i)
                pe.wait_ge(oT_ready, KV * NT)
                pe.wait_ge(out_proj.loaded, 16)
                for tt in range(NT):
                    out_proj.tensor(pe, tt)


def route(t, name, gain, w_group, b_group, w_router, b_router, moe):
    nc = t.nc
    NL = GROUPS + EXPERTS
    with ExitStack() as ctx:
        sb = lambda *a: ctx.enter_context(nc.sbuf_tensor(*a))
        ps = lambda *a: ctx.enter_context(nc.psum_tensor(*a))
        turn_banks = ps(f"{name}_T", [P, 4, HALF], F32)
        L_ps = ps(f"{name}_L", [P, 2, HALF], F32)
        R_ps = ps(f"{name}_R", [P, HALF], F32)
        C_ps = ps(f"{name}_C", [P, HALF], F32)
        norm = Norm(t, f"{name}n", gain, sb, turn_banks, moe.hn_rows)
        w_sb = sb(f"{name}_w", [P, KD, NL], F32)
        b_sb = sb(f"{name}_b", [NL, 1], F32)
        lT = sb(f"{name}_lT", [NL, T], F32)
        lg = sb(f"{name}_lg", [P, NT, NL], F32)
        below = sb(f"{name}_below", [P, P], F32)
        ones = sb(f"{name}_ones", [P, P], F32)
        count_i = sb(f"{name}_count_i", [P, 64], I32)
        count_up = sb(f"{name}_count_up", [P, 64], F32)
        count_dn = sb(f"{name}_count_dn", [P, 64], F32)
        token_i = sb(f"{name}_token_i", [P, NT], I32)
        table0 = sb(f"{name}_table0", [CAP, COLS], I32)
        v = lambda what, *shape: sb(f"{name}_{what}", [P, *shape], F32)
        gm, gh, gs = v("gm", NT), v("gh", NT, GROUPS), v("gs", NT, GROUPS)
        gd, gsum, pg = v("gd", NT, GROUPS), v("gsum", NT), v("pg", NT)
        le = v("le", NT, EXPERTS)
        top = v("top", 2, NT)
        seen = v("seen", NT, EXPERTS)
        code = v("code", 2, NT)
        hot = v("hot", 2, NT * EXPERTS)
        hots = v("hots", NT * EXPERTS)
        diff, ex, den = v("diff", NT), v("ex", NT), v("den", NT)
        tot = v("tot", NT, EXPERTS)
        base = v("base", NT + 1, EXPERTS)
        pos = v("pos", NT * EXPERTS)
        pick = v("pick", 2, NT * EXPERTS)
        place, extra0, more = v("place", 2 * NT), v("extra0", 2 * NT), v("more", 2 * NT)
        over = v("over", EXPERTS * STEPS)
        spare, run_a, run_b, first = v("spare", EXPERTS), v("run_a", EXPERTS), v("run_b", EXPERTS), v("first", EXPERTS)
        stepped = v("stepped", 2 * NT * STEPS)
        expert, row, slot, slot_of_row = (v(what, 2 * NT) for what in ("expert", "row", "slot", "slot_of_row"))
        owner_cmp, ctl_f = v("owner_cmp", COLS * EXPERTS), v("ctl_f", COLS + 1)
        steps_of = v("steps_of", STEPS)
        slot_i = sb(f"{name}_slot_i", [P, 2 * NT], I32)

        s = lambda what: t.sem(f"{name}_{what}")
        w_loaded, made, consts, lT_done, lT_ready = s("w_loaded"), s("made"), s("consts"), s("lT_done"), s("lT_ready")
        lg_done, own_s, act_in, act_out = s("lg_done"), s("own"), s("act_in"), s("act_out")
        hot_ready, counted, slots_ready = s("hot_ready"), s("counted"), s("slots_ready")
        zero_made, zeroed, scattered, table_loaded = s("zero_made"), s("zeroed"), s("scattered"), s("table_loaded")

        with nc.Block() as block:
            @block.sync
            def _(sp):
                norm.sync_load(sp)
                wide = dict(allow_slow_non_contiguous=True)
                sp.dma_start(w_sb[:, :, 0:GROUPS], w_group.rearrange("(p k) n -> p k n", k=KD)).then_inc(w_loaded, 16)
                sp.dma_start(w_sb[:, :, GROUPS:NL], w_router.rearrange("(p k) n -> p k n", k=KD)).then_inc(w_loaded, 16)
                sp.dma_start(b_sb[0:GROUPS, :], b_group.unsqueeze(1), **wide).then_inc(w_loaded, 16)
                sp.dma_start(b_sb[GROUPS:NL, :], b_router.unsqueeze(1), **wide).then_inc(w_loaded, 16)
                sp.wait_ge(zero_made, 1)
                sp.dma_start(moe.table_dram.rearrange("(c r) o -> c (r o)", c=CAP), table0[:, :]).then_inc(zeroed, 16)
                moe.first_weights(sp)
                norm.sync_store(sp)
                sp.wait_ge(scattered, 16 * 2 * NT)
                sp.dma_start(moe.table[:, :], moe.table_dram.rearrange("(c r) o -> c (r o)", c=CAP)).then_inc(table_loaded, 16)
                sp.wait_ge(table_loaded, 16)

            @block.gpsimd
            def _(pool):
                pool.memset(table0[:, :], 0).then_inc(zero_made, 1)
                pool.memset(ones[:, :], 1.0).then_inc(made, 1)
                pool.iota(count_i[:, :], pattern=[[1, 64]], base=0, channel_multiplier=0).then_inc(made, 1)
                pool.iota(token_i[:, :], pattern=[[P, NT]], base=0, channel_multiplier=1).then_inc(made, 1)
                pool.wait_ge(made, 1)
                pool.affine_select(out=below[:, :], in_=ones[:, :], compare_op=ALU.is_gt, fill=0.0, base=0,
                                   pattern=[[1, P]], channel_multiplier=-1).then_inc(made, 1)
                pool.wait_ge(zeroed, 16)
                pool.wait_ge(made, 4)
                pool.wait_ge(slots_ready, 1)
                for c in range(2 * NT):
                    pool.indirect_dma_start(out=moe.table_dram, out_offset=bass.IndirectOffsetOnAxis(slot_i[:, c:c + 1], 0),
                                            in_=token_i[:, c % NT:c % NT + 1], in_offset=None).then_inc(scattered, 16)

            @block.scalar
            def _(act):
                norm.scalar(act)
                act.wait_ge(w_loaded, 64)
                for n in range(2):
                    act.wait_ge(lT_done, n + 1)
                    act.activation(lT[:, n * HALF:(n + 1) * HALF], L_ps[0:NL, n, :], ACT.Identity, bias=b_sb[:, :])\
                       .then_inc(lT_ready, 1)
                act.wait_ge(act_in, 1)
                act.activation(gd[:, :, :], gd[:, :, :], ACT.Exp, bias=t.zero_col[:, :]).then_inc(act_out, 1)
                act.wait_ge(act_in, 2)
                act.activation(ex[:, :], diff[:, :], ACT.Exp, bias=t.zero_col[:, :]).then_inc(act_out, 1)

            @block.tensor
            def _(pe):
                norm.tensor(pe)
                norm.ready(pe)
                pe.wait_ge(w_loaded, 64)
                for n in range(2):
                    for k in range(KD):
                        last = pe.matmul(L_ps[0:NL, n, :], w_sb[:, k, :], norm.hnT[:, k, n * HALF:(n + 1) * HALF],
                                         start=(k == 0), stop=(k == KD - 1))
                    last.then_inc(lT_done, 1)
                for n in range(2):
                    pe.wait_ge(lT_ready, n + 1)
                    for tt in range(4 * n, 4 * n + 4):
                        last = pe.transpose(R_ps[:, tt * NL:(tt + 1) * NL], lT[:, tt * P:(tt + 1) * P], t.ident[0:NL, 0:NL])
                last.then_inc(lg_done, 1)
                pe.wait_ge(hot_ready, 1)
                pe.wait_ge(made, 4)
                pe.matmul(C_ps[:, 0:256], below[:, :], hots[:, :], start=True, stop=True)
                pe.matmul(C_ps[:, 256:512], ones[:, :], hots[:, :], start=True, stop=True).then_inc(counted, 1)

            @block.vector
            def _(dve):
                norm.vector(dve)
                own = Step(dve, own_s)
                tt_, ts_, red = dve.tensor_tensor, dve.tensor_scalar, dve.tensor_reduce
                dve.wait_ge(made, 4)
                own(dve.tensor_copy(count_up[:, :], count_i[:, :]))
                own(ts_(count_dn[:, :], count_up[:, :], -1.0, 64.0, ALU.mult, ALU.add))
                own(ts_(steps_of[:, :], count_up[:, 1:STEPS + 1], float(CAP), None, ALU.mult))
                dve.wait_ge(lg_done, 1)
                own(dve.tensor_copy(lg[:, :, :], R_ps[:, 0:NT * NL].rearrange("p (a b) -> p a b", b=NL)))
                groups = lg[:, :, 0:GROUPS]
                over_g = lambda a: a.unsqueeze(2).broadcast_to((P, NT, GROUPS))
                over_e = lambda a: a.unsqueeze(2).broadcast_to((P, NT, EXPERTS))
                tiled = lambda a, n: a.unsqueeze(1).broadcast_to((P, NT, n))
                own(red(gm[:, :], groups, AX, ALU.max))
                tt_(gd[:, :, :], groups, over_g(gm[:, :]), ALU.subtract).then_inc(act_in, 1)
                own(tt_(gh[:, :, :], groups, over_g(gm[:, :]), ALU.is_equal))
                own(tt_(gs[:, :, :], gh[:, :, :], tiled(count_dn[:, 0:GROUPS], GROUPS), ALU.mult))
                own(red(gm[:, :], gs[:, :, :], AX, ALU.max))
                own(tt_(gh[:, :, :], gs[:, :, :], over_g(gm[:, :]), ALU.is_equal))
                own(ts_(gh[:, :, :], gh[:, :, :], -1.0, -MASKED, ALU.add, ALU.mult))
                own(tt_(le[:, :, :].rearrange("p a (g e) -> p a g e", g=GROUPS),
                        lg[:, :, GROUPS:NL].rearrange("p a (g e) -> p a g e", g=GROUPS),
                        gh[:, :, :].unsqueeze(3).broadcast_to((P, NT, GROUPS, PER_GROUP)), ALU.add))
                flat = lambda a: a[:, :, :].rearrange("p a b -> p (a b)")
                for c in range(TOP_K):
                    own(red(top[:, c, :], le[:, :, :], AX, ALU.max))
                    own(tt_(seen[:, :, :], le[:, :, :], over_e(top[:, c, :]), ALU.is_equal))
                    own(tt_(seen[:, :, :], seen[:, :, :], tiled(count_dn[:, 0:EXPERTS], EXPERTS), ALU.mult))
                    own(red(code[:, c, :], seen[:, :, :], AX, ALU.max))
                    own(tt_(hot[:, c, :].rearrange("p (a b) -> p a b", b=EXPERTS), seen[:, :, :], over_e(code[:, c, :]),
                            ALU.is_equal))
                    if c == 0:
                        own(dve.scalar_tensor_tensor(out=flat(le), in0=hot[:, 0, :], scalar=2 * MASKED, in1=flat(le),
                                                     op0=ALU.mult, op1=ALU.add))
                tt_(hots[:, :], hot[:, 0, :], hot[:, 1, :], ALU.add).then_inc(hot_ready, 1)
                tt_(diff[:, :], top[:, 1, :], top[:, 0, :], ALU.subtract).then_inc(act_in, 1)
                own(ts_(expert[:, :], code[:, :, :].rearrange("p a b -> p (a b)"), -1.0, 64.0, ALU.mult, ALU.add))
                own(dve.memset(base[:, 0, :], 0.0))
                dve.wait_ge(act_out, 2)
                own(red(gsum[:, :], gd[:, :, :], AX, ALU.add))
                own(dve.reciprocal(pg[:, :], gsum[:, :]))
                own(ts_(den[:, :], ex[:, :], 1.0, None, ALU.add))
                own(dve.reciprocal(den[:, :], den[:, :]))
                own(tt_(moe.weight[:, 0, :], pg[:, :], den[:, :], ALU.mult))
                own(tt_(moe.weight[:, 1, :], moe.weight[:, 0, :], ex[:, :], ALU.mult))
                dve.wait_ge(counted, 1)
                own(dve.tensor_copy(flat(tot), C_ps[:, 256:512]))
                for a in range(NT):
                    own(tt_(base[:, a + 1, :], base[:, a, :], tot[:, a, :], ALU.add))
                own(tt_(pos[:, :], C_ps[:, 0:256], base[:, 0:NT, :].rearrange("p a b -> p (a b)"), ALU.add))
                twice = lambda a: a.unsqueeze(1).broadcast_to((P, 2, NT * EXPERTS))
                by_expert = pick[:, :, :].rearrange("p c (a b) -> p (c a) b", b=EXPERTS)
                own(tt_(pick[:, :, :], hot[:, :, :], twice(pos[:, :]), ALU.mult))
                own(red(place[:, :], by_expert, AX, ALU.add))
                total = base[:, NT, :]
                grid = over[:, :].rearrange("p (e j) -> p e j", j=STEPS)
                own(tt_(grid, total.unsqueeze(2).broadcast_to((P, EXPERTS, STEPS)),
                        steps_of[:, :].unsqueeze(1).broadcast_to((P, EXPERTS, STEPS)), ALU.is_gt))
                own(red(spare[:, :], grid, AX, ALU.add))
                source, target, shift = spare, run_a, 1
                while shift < EXPERTS:
                    own(dve.tensor_copy(target[:, 0:shift], source[:, 0:shift]))
                    own(tt_(target[:, shift:], source[:, shift:], source[:, 0:EXPERTS - shift], ALU.add))
                    source, target = target, (run_b if target is run_a else run_a)
                    shift *= 2
                running = source
                own(tt_(first[:, :], running[:, :], spare[:, :], ALU.subtract))
                own(tt_(pick[:, :, :].rearrange("p c (a b) -> p (c a) b", b=EXPERTS),
                        hot[:, :, :].rearrange("p c (a b) -> p (c a) b", b=EXPERTS),
                        first[:, :].unsqueeze(1).broadcast_to((P, 2 * NT, EXPERTS)), ALU.mult))
                own(red(extra0[:, :], by_expert, AX, ALU.add))
                ladder = stepped[:, :].rearrange("p (c j) -> p c j", j=STEPS)
                own(tt_(ladder, place[:, :].unsqueeze(2).broadcast_to((P, 2 * NT, STEPS)),
                        steps_of[:, :].unsqueeze(1).broadcast_to((P, 2 * NT, STEPS)), ALU.is_ge))
                own(red(more[:, :], ladder, AX, ALU.add))
                own(dve.scalar_tensor_tensor(out=place[:, :], in0=more[:, :], scalar=-float(CAP), in1=place[:, :],
                                             op0=ALU.mult, op1=ALU.add))
                own(tt_(row[:, :], extra0[:, :], more[:, :], ALU.add))
                own(ts_(row[:, :], row[:, :], float(EXPERTS - 1), None, ALU.add))
                own(tt_(row[:, :], row[:, :], expert[:, :], ALU.subtract))
                own(ts_(more[:, :], more[:, :], 0.0, None, ALU.is_gt))
                own(tt_(row[:, :], row[:, :], more[:, :], ALU.mult))
                own(tt_(row[:, :], row[:, :], expert[:, :], ALU.add))
                own(dve.scalar_tensor_tensor(out=slot[:, :], in0=place[:, :], scalar=float(COLS), in1=row[:, :],
                                             op0=ALU.mult, op1=ALU.add))
                dve.tensor_copy(slot_i[:, :], slot[:, :]).then_inc(slots_ready, 1)
                own(dve.scalar_tensor_tensor(out=slot_of_row[:, :], in0=row[:, :], scalar=float(CAP), in1=place[:, :],
                                             op0=ALU.mult, op1=ALU.add))
                own(dve.tensor_copy(moe.out_slot[:, :], slot_of_row[:, :]))
                own(ts_(ctl_f[:, 0:1], running[:, EXPERTS - 1:EXPERTS], float(EXPERTS - 3), None, ALU.add))
                own(dve.tensor_copy(ctl_f[:, 1:1 + EXPERTS], count_up[:, 0:EXPERTS]))
                owners = owner_cmp[:, 0:(COLS - EXPERTS) * EXPERTS].rearrange("p (b e) -> p b e", e=EXPERTS)
                own(tt_(owners, running[:, :].unsqueeze(1).broadcast_to((P, COLS - EXPERTS, EXPERTS)),
                        count_up[:, 0:COLS - EXPERTS].unsqueeze(2).broadcast_to((P, COLS - EXPERTS, EXPERTS)), ALU.is_le))
                own(red(ctl_f[:, 1 + EXPERTS:1 + COLS], owners, AX, ALU.add))
                own(ts_(ctl_f[:, 1 + EXPERTS:1 + COLS], ctl_f[:, 1 + EXPERTS:1 + COLS], float(EXPERTS - 1), None, ALU.min))
                own(dve.tensor_copy(moe.control[:, :], ctl_f[0:1, :]))



def differential_attention(t, gain, w_qkv, w_o, lam, subln, lambda_init):
    nc = t.nc
    HEADS = 8
    VD = 2 * HEAD
    QK = HEADS * 2 * HEAD
    SPAN = 2 * T - P
    with ExitStack() as ctx:
        sb = lambda *a: ctx.enter_context(nc.sbuf_tensor(*a))
        S = ctx.enter_context(nc.psum_tensor("a1_S", [P, 4, HALF], F32))
        TB = ctx.enter_context(nc.psum_tensor("a1_T", [P, 2, HALF], F32))
        O = ctx.enter_context(nc.psum_tensor("a1_O", [P, 2, HALF], F32))
        norm = Norm(t, "a1n", gain, sb, S)
        w_sb = sb("a1_w", [P, KD, 3 * P], F32)
        q_parts, k_hi, k_lo = (sb(f"a1_{n}", [P, 2, T], F32R) for n in ("q_parts", "k_hi", "k_lo"))
        v_rows = sb("a1_v_rows", [P, NT, VD], F32)
        probs = sb("a1_probs", [P, 2, 2, T], F32)
        mixed = sb("a1_mixed", [P, 2, T], F32)
        mixT = sb("a1_mixT", [P, 2, KD * P], F32)
        bias = sb("a1_bias", [P, SPAN], F32)
        o_rows = sb("a1_o_rows", [P, NT, HEADS, VD], F32)
        square = sb("a1_square", [P, HEADS * VD], F32)
        lam_b = sb("a1_lam", [P, 4, HEAD], F32)
        lam_2 = sb("a1_lam_2", [P, 2, HEAD], F32)
        lam_s = sb("a1_lam_s", [P, 2], F32)
        lam_neg = sb("a1_lam_neg", [P, 1], F32)
        sub_g = sb("a1_sub_g", [P, 1], F32)
        top2, neg2, sum2 = (sb(f"a1_{n}", [P, 2, 2], F32) for n in ("top2", "neg2", "sum2"))
        inv2 = sb("a1_inv2", [P, 4, 2], F32)
        ratio = sb("a1_ratio", [P, 2], F32)
        o_ss, o_rms, o_rstd = (sb(f"a1_{n}", [P, NT, HEADS], F32) for n in ("o_ss", "o_rms", "o_rstd"))
        out_proj = OutProjection(t, "a1o", w_o, None, norm.hnT, S, None)

        w_loaded, lam_loaded = t.sem("a1_w_loaded"), t.sem("a1_lam_loaded")
        proj_done, hi_ready, parts_ready, v_ready = (t.sem(f"a1_{n}") for n in ("proj_done", "hi_ready", "parts_ready", "v_ready"))
        scores, scores_seen, biased = t.sem("a1_scores"), t.sem("a1_scores_seen"), t.sem("a1_biased")
        stats, exp_done, mixed_ready = t.sem("a1_stats"), t.sem("a1_exp_done"), t.sem("a1_mixed_ready")
        m_turned, mixT_ready, pv_done, o_ready = t.sem("a1_m_turned"), t.sem("a1_mixT_ready"), t.sem("a1_pv_done"), t.sem("a1_o_ready")
        dve_own, prep, iota_done = t.sem("a1_dve_own"), t.sem("a1_prep"), t.sem("a1_iota")
        lam_in, lam_out = t.sem("a1_lam_in"), t.sem("a1_lam_out")
        rms_in, rms_out, scaled, o_turned, oT_ready = (t.sem(f"a1_{n}") for n in ("rms_in", "rms_out", "scaled", "o_turned", "oT_ready"))

        with nc.Block() as block:
            @block.sync
            def _(sp):
                norm.sync_load(sp)
                sp.dma_start(lam_b[:, :, :], lam.unsqueeze(0).broadcast_to((P, 4, HEAD))).then_inc(lam_loaded, 16)
                sp.dma_start(sub_g[:, :], subln.unsqueeze(1), allow_slow_non_contiguous=True).then_inc(lam_loaded, 16)

                def load_weights(h):
                    for at, col in ((0, h * P), (P, QK + h * P), (2 * P, 2 * QK + h * P)):
                        sp.dma_start(w_sb[:, :, at:at + P],
                                     w_qkv.rearrange("(p k) n -> p k n", k=KD)[:, :, bass.ds(col, P)])\
                          .then_inc(w_loaded, 16)

                load_weights(0)
                with sp.Fori(1, HEADS) as h:
                    sp.wait_ge(proj_done, 6 * h)
                    load_weights(h)
                sp.wait_ge(proj_done, 6 * HEADS)
                out_proj.sync_load(sp)

            @block.gpsimd
            def _(pool):
                pool.iota(bias[:, :].bitcast(I32), pattern=[[-1, SPAN]], base=T - P, channel_multiplier=1).then_inc(iota_done, 1)

            @block.scalar
            def _(act):
                norm.scalar(act)
                act.wait_ge(lam_in, 1)
                act.activation(lam_s[:, :], lam_s[:, :], ACT.Exp, bias=t.zero_col[:, :]).then_inc(lam_out, 1)
                with act.Fori(0, HEADS) as h:
                    for o in range(6):
                        act.wait_ge(proj_done, 6 * h + o + 1)
                        j, n = divmod(o, 2)
                        cols = slice(n * HALF, (n + 1) * HALF)
                        if j == 0:
                            for c, part in enumerate(HALVES):
                                last = act.mul(q_parts[part, c, cols], S[part, o % 4, :], Q_SCALE)
                            last.then_inc(hi_ready, 1)
                        elif j == 1:
                            for c, part in enumerate(HALVES):
                                for there in HALVES:
                                    last = act.copy(k_hi[there, c, cols], S[part, o % 4, :])
                            last.then_inc(hi_ready, 1)
                        else:
                            act.copy(v_rows[:, 4 * n:4 * n + 4, :], S[:, o % 4, :].rearrange("p (a b) -> p a b", b=VD))\
                               .then_inc(v_ready, 1)

                    def exponentials(i):
                        n = NT * h + i
                        act.wait_ge(stats, n + 1)
                        for c in range(2):
                            row = probs[:, i % 2, c, :]
                            last = act.activation(row, row, ACT.Exp, bias=neg2[:, i % 2, c:c + 1],
                                                  accum_out=sum2[:, i % 2, c:c + 1])
                        last.then_inc(exp_done, 1)

                    exponentials(0)
                    for i in range(NT):
                        if i + 1 < NT:
                            exponentials(i + 1)
                        n = NT * h + i
                        if i >= 2:
                            act.wait_ge(pv_done, n - 1)
                        for b in range(2):
                            act.wait_ge(m_turned, 2 * n + b + 1)
                            act.copy(mixT[:, i % 2, b * HALF:(b + 1) * HALF], TB[:, b, :]).then_inc(mixT_ready, 1)
                act.wait_ge(rms_in, 1)
                act.activation(o_rms[:, :, :], o_ss[:, :, :], ACT.Sqrt, bias=t.zero_col[:, :]).then_inc(rms_out, 1)
                for tt in range(NT):
                    for b in range(2):
                        act.wait_ge(o_turned, 2 * tt + b + 1)
                        if tt >= 2:
                            act.wait_ge(out_proj.done, 2 * (tt - 1))
                        act.activation(mixT[:, tt % 2, b * HALF:(b + 1) * HALF], TB[:, b, :], ACT.Copy,
                                       scale=sub_g[:, :]).then_inc(oT_ready, 1)

            @block.vector
            def _(dve):
                own = Step(dve, prep)
                dve.wait_ge(iota_done, 1)
                wide = probs[:, 0, :, :].rearrange("p a b -> p (a b)")[:, 0:SPAN]
                own(dve.tensor_copy(wide, bias[:, :].bitcast(I32)))
                own(dve.tensor_scalar(bias[:, :], wide, -1.0, None, ALU.mult))
                own(dve.tensor_tensor(bias[:, :], bias[:, :], wide, ALU.max))
                own(dve.tensor_scalar(bias[:, :], bias[:, :], -2.0 ** (-8.0 / HEADS), None, ALU.mult))
                dve.wait_ge(lam_loaded, 32)
                own(dve.tensor_tensor(lam_2[:, :, :], lam_b[:, 0:4:2, :], lam_b[:, 1:4:2, :], ALU.mult))
                own(dve.tensor_reduce(lam_s[:, :], lam_2[:, :, :], AX, ALU.add))
                own(dve.tensor_scalar(sub_g[:, :], sub_g[:, :], 1.0 - lambda_init, None, ALU.mult))
                dve.tensor_copy(lam_neg[:, :], lam_s[:, 0:1]).then_inc(lam_in, 1)
                norm.vector(dve)
                dve.wait_ge(lam_out, 1)
                own(dve.tensor_tensor(lam_neg[:, :], lam_s[:, 1:2], lam_s[:, 0:1], ALU.subtract))
                own(dve.tensor_scalar(lam_neg[:, :], lam_neg[:, :], -lambda_init, None, ALU.add))
                prepared = own.n
                OWN = 2 * NT + 1
                with dve.Fori(0, HEADS) as h:
                    own = Step(dve, dve_own, OWN * h)
                    for o in range(4):
                        dve.wait_ge(hi_ready, 4 * h + o + 1)
                        j, n = divmod(o, 2)
                        cols = slice(n * HALF, (n + 1) * HALF)
                        for c, part in enumerate(HALVES):
                            if j == 0:
                                last = dve.scalar_tensor_tensor(out=q_parts[HALVES[1 - c], c, cols], in0=S[part, o, :],
                                                                scalar=Q_SCALE, in1=q_parts[part, c, cols].bitcast(F32),
                                                                op0=ALU.mult, op1=ALU.subtract)
                            else:
                                for there in HALVES:
                                    last = dve.tensor_tensor(k_lo[there, c, cols], S[part, o, :],
                                                             k_hi[part, c, cols].bitcast(F32), ALU.subtract)
                        last.then_inc(parts_ready, 1)

                    def biased_scores(i):
                        n = NT * h + i
                        if i >= 2:
                            dve.wait_ge(mixed_ready, n - 1)
                        for c in range(2):
                            wait_apart(dve, scores, 2 * n + c + 1, scores_seen)
                            at = T - P - i * P
                            dve.tensor_tensor_reduce(probs[:, i % 2, c, :].rearrange("p (a b) -> p a b", a=2),
                                                     S[:, 2 * c:2 * c + 2, :],
                                                     bias[:, at:at + T].rearrange("p (a b) -> p a b", a=2), 1.0, MASKED,
                                                     ALU.add, ALU.max, top2[:, i % 2, c:c + 1]).then_inc(biased, 1)
                        dve.wait_ge(biased, 2 * n + 2)
                        dve.tensor_scalar(neg2[:, i % 2, :], top2[:, i % 2, :], -1.0, None, ALU.mult).then_inc(stats, 1)

                    def mix(i):
                        n = NT * h + i
                        dve.wait_ge(exp_done, n + 1)
                        own(dve.reciprocal(inv2[:, i % 4, :], sum2[:, i % 2, :]))
                        own(dve.scalar_tensor_tensor(out=ratio[:, i % 2:i % 2 + 1], in0=inv2[:, i % 4, 1:2],
                                                     scalar=lam_neg[:, :], in1=sum2[:, i % 2, 0:1],
                                                     op0=ALU.mult, op1=ALU.mult))
                        if i >= 2:
                            dve.wait_ge(m_turned, 2 * (n - 1))
                        dve.scalar_tensor_tensor(out=mixed[:, i % 2, :], in0=probs[:, i % 2, 1, :],
                                                 scalar=ratio[:, i % 2:i % 2 + 1], in1=probs[:, i % 2, 0, :],
                                                 op0=ALU.mult, op1=ALU.add).then_inc(mixed_ready, 1)

                    def head_out(i):
                        dve.wait_ge(pv_done, NT * h + i + 1)
                        dve.tensor_scalar(o_rows[:, i, bass.ds(h, 1), :].rearrange("p a b -> p (a b)"), O[:, i % 2, 0:VD],
                                          inv2[:, i % 4, 0:1], None, ALU.mult).then_inc(o_ready, 1)

                    biased_scores(0)
                    for i in range(NT):
                        if i + 1 < NT:
                            biased_scores(i + 1)
                        if i >= 2:
                            head_out(i - 2)
                        mix(i)
                    head_out(NT - 2)
                    head_out(NT - 1)
                    own(dve.tensor_scalar(bias[:, :], bias[:, :], 2.0 ** (-8.0 / HEADS), None, ALU.mult))
                    assert own.n == OWN
                own = Step(dve, prep, prepared)
                dve.wait_ge(o_ready, NT * HEADS)
                for tt in range(NT):
                    own(dve.tensor_tensor(square[:, :], o_rows[:, tt, :, :].rearrange("p a b -> p (a b)"),
                                          o_rows[:, tt, :, :].rearrange("p a b -> p (a b)"), ALU.mult))
                    own(dve.tensor_reduce(o_ss[:, tt, :], square[:, :].rearrange("p (a b) -> p a b", b=VD), AX, ALU.add))
                dve.tensor_scalar(o_ss[:, :, :], o_ss[:, :, :], 1.0 / VD, SUBLN_EPS, ALU.mult, ALU.add).then_inc(rms_in, 1)
                dve.wait_ge(rms_out, 1)
                own(dve.reciprocal(o_rstd[:, :, :], o_rms[:, :, :]))

                def scale(tt):
                    dve.tensor_tensor(o_rows[:, tt, :, :], o_rows[:, tt, :, :],
                                      o_rstd[:, tt, :].unsqueeze(2).broadcast_to((P, HEADS, VD)), ALU.mult).then_inc(scaled, 1)
                scale(0)
                for tt in range(NT):
                    if tt + 1 < NT:
                        scale(tt + 1)
                    out_proj.vector(dve, tt)

            @block.tensor
            def _(pe):
                norm.tensor(pe)
                norm.ready(pe)
                with pe.Fori(0, HEADS) as h:
                    pe.wait_ge(w_loaded, 48 * h + 48)
                    for o in range(6):
                        j, n = divmod(o, 2)
                        if o >= 4:
                            pe.wait_ge(parts_ready, 4 * h + o - 3)
                        if j < 2:
                            for k in range(KD):
                                last = pe.matmul(S[:, o % 4, :], w_sb[:, k, j * P:(j + 1) * P],
                                                 norm.hnT[:, k, n * HALF:(n + 1) * HALF], start=(k == 0), stop=(k == KD - 1))
                        else:
                            for a in range(4):
                                tt = 4 * n + a
                                for k in range(KD):
                                    last = pe.matmul(S[:, o % 4, a * P:(a + 1) * P], norm.hnT[:, k, tt * P:(tt + 1) * P],
                                                     w_sb[:, k, 2 * P:3 * P], start=(k == 0), stop=(k == KD - 1))
                        last.then_inc(proj_done, 1)
                    pe.wait_ge(parts_ready, 4 * h + 4)
                    pe.wait_ge(v_ready, 2 * h + 2)

                    def head_scores(i):
                        n = NT * h + i
                        for c in range(2):
                            if i >= 1:
                                pe.wait_ge(biased, 2 * (n - 1) + c + 1)
                            for b in range(2):
                                for k_part in (k_hi, k_lo):
                                    last = pe.matmul(S[:, 2 * c + b, :], q_parts[:, c, i * P:(i + 1) * P],
                                                     k_part[:, c, b * HALF:(b + 1) * HALF],
                                                     start=(k_part is k_hi), stop=(k_part is k_lo))
                            last.then_inc(scores, 1)

                    def product(i):
                        n = NT * h + i
                        pe.wait_ge(mixed_ready, n + 1)
                        for b in range(2):
                            if i >= 1:
                                pe.wait_ge(mixT_ready, 2 * (n - 1) + b + 1)
                            for a in range(4):
                                k = 4 * b + a
                                last = pe.transpose(TB[:, b, a * P:(a + 1) * P], mixed[:, i % 2, k * P:(k + 1) * P],
                                                    t.ident[:, :])
                            last.then_inc(m_turned, 1)
                        if i >= 2:
                            pe.wait_ge(o_ready, n - 1)
                        for k in range(KD):
                            if k % 4 == 0:
                                pe.wait_ge(mixT_ready, 2 * n + k // 4 + 1)
                            last = pe.matmul(O[:, i % 2, 0:VD], mixT[:, i % 2, k * P:(k + 1) * P], v_rows[:, k, :],
                                             start=(k == 0), stop=(k == KD - 1))
                        last.then_inc(pv_done, 1)

                    head_scores(0)
                    head_scores(1)
                    for i in range(NT):
                        if i + 2 < NT:
                            head_scores(i + 2)
                        product(i)
                pe.wait_ge(out_proj.loaded, 16)
                for tt in range(NT):
                    pe.wait_ge(scaled, tt + 1)
                    for b in range(2):
                        if tt >= 1:
                            pe.wait_ge(oT_ready, 2 * (tt - 1) + b + 1)
                        for a in range(4):
                            last = pe.transpose(TB[:, b, a * P:(a + 1) * P], o_rows[:, tt, 4 * b + a, :], t.ident[:, :])
                        last.then_inc(o_turned, 1)
                    pe.wait_ge(oT_ready, 2 * tt + 2)
                    out_proj.tensor(pe, tt, mixT[:, tt % 2, :].rearrange("p (k n) -> p k n", k=KD))


def final_norm(t, gain, out):
    nc = t.nc
    with ExitStack() as ctx:
        sb = lambda *a: ctx.enter_context(nc.sbuf_tensor(*a))
        gain_b = sb("f_gain", [P, D], F32)
        junk_a, junk_d = sb("f_junk_a", [P, D], F32), sb("f_junk_d", [P, D], F32)
        rows = sb("f_rows", [P, NT, D], F32)
        ssq, rms, rstd = sb("f_ssq", [P, NT], F32), sb("f_rms", [P, NT], F32), sb("f_rstd", [P, NT], F32)
        gain_loaded, act_sq, dve_sq, ms_ready = (t.sem(f"f_{n}") for n in ("gain_loaded", "act_sq", "dve_sq", "ms_ready"))
        rms_ready, chain, ready, stored = (t.sem(f"f_{n}") for n in ("rms_ready", "chain", "ready", "stored"))
        with nc.Block() as block:
            @block.sync
            def _(sp):
                sp.dma_start(gain_b[:, :], gain.broadcast_to((P, D))).then_inc(gain_loaded, 16)
                for tt in range(NT):
                    sp.wait_ge(ready, tt + 1)
                    sp.dma_start(out[0, tt * P:(tt + 1) * P, :], rows[:, tt, :]).then_inc(stored, 16)
                sp.wait_ge(stored, 16 * NT)

            @block.scalar
            def _(act):
                for tt in range(0, NT, 2):
                    if tt:
                        act.wait_ge(act_sq, tt // 2)
                    act.activation(junk_a[:, :], t.x[:, tt, :], ACT.Square, bias=t.zero_col[:, :],
                                   accum_out=ssq[:, tt:tt + 1]).then_inc(act_sq, 1)
                act.wait_ge(ms_ready, 1)
                act.activation(rms[:, :], ssq[:, :], ACT.Sqrt, bias=t.zero_col[:, :]).then_inc(rms_ready, 1)

            @block.vector
            def _(dve):
                for tt in range(1, NT, 2):
                    if tt > 1:
                        dve.wait_ge(dve_sq, tt // 2)
                    dve.tensor_tensor_reduce(junk_d[:, :], t.x[:, tt, :], t.x[:, tt, :], 1.0, 0.0,
                                             ALU.mult, ALU.add, ssq[:, tt:tt + 1]).then_inc(dve_sq, 1)
                dve.wait_ge(act_sq, NT // 2)
                dve.wait_ge(dve_sq, NT // 2)
                dve.tensor_scalar(ssq[:, :], ssq[:, :], 1.0 / D, NORM_EPS, ALU.mult, ALU.add).then_inc(ms_ready, 1)
                dve.wait_ge(rms_ready, 1)
                dve.reciprocal(rstd[:, :], rms[:, :]).then_inc(chain, 1)
                dve.wait_ge(chain, 1)
                dve.wait_ge(gain_loaded, 16)
                for tt in range(NT):
                    dve.scalar_tensor_tensor(out=rows[:, tt, :], in0=t.x[:, tt, :], scalar=rstd[:, tt:tt + 1],
                                             in1=gain_b[:, :], op0=ALU.mult, op1=ALU.mult).then_inc(ready, 1)


class Experts:

    def __init__(self, t, name, w_gate, w_up, w_down, dram, ctx):
        nc = t.nc
        sb = lambda *a: ctx.enter_context(nc.sbuf_tensor(*a))
        self.t, self.name = t, name
        self.weights = (w_gate, w_up, w_down)
        self.hn_rows, self.table_dram, self.out_rows = dram
        self.raw = [sb(f"{name}_raw_{w}", [P, KD * HIDDEN], F32) for w in ("gate", "up", "down")]
        self.table = sb(f"{name}_table", [CAP, COLS], I32)
        self.weight = sb(f"{name}_weight", [P, 2, NT], F32)
        self.out_slot = sb(f"{name}_out_slot", [P, 2 * NT], I32)
        self.control = sb(f"{name}_control", [1, COLS + 1], I32)
        s = lambda what: t.sem(f"{name}_{what}")
        self.raw_loaded = [s(f"{w}_loaded") for w in ("gate", "up", "down")]

    def load(self, sp, w, expert):
        k = KH if w == 2 else KD
        sp.dma_start(self.raw[w][:, :], self.weights[w][expert].rearrange("(p k) n -> p (k n)", k=k)
                     if isinstance(expert, int) else
                     self.weights[w][bass.ds(expert, 1)].rearrange("e (p k) n -> p (e k n)", k=k))\
          .then_inc(self.raw_loaded[w], 16)

    def first_weights(self, sp):
        for w in range(3):
            self.load(sp, w, 0)

    def run(self):
        t, nc, name = self.t, self.t.nc, self.name
        W = KD * HIDDEN
        PIECE = W // 2
        with ExitStack() as ctx:
            sb = lambda *a: ctx.enter_context(nc.sbuf_tensor(*a))
            ps = lambda *a: ctx.enter_context(nc.psum_tensor(*a))
            hi = [sb(f"{name}_hi_{w}", [P, W], F32R) for w in ("gate", "up", "down")]
            lo = [sb(f"{name}_lo_{w}", [P, W], F32R) for w in ("gate", "up", "down")]
            pick = sb(f"{name}_pick", [CAP, 1], I32)
            xg = sb(f"{name}_xg", [CAP, D], F32)
            x_hi, x_lo = sb(f"{name}_x_hi", [P, KD * CAP], F32R), sb(f"{name}_x_lo", [P, KD * CAP], F32R)
            gated = sb(f"{name}_gated", [CAP, HIDDEN], F32)
            hid = sb(f"{name}_hid", [CAP, HIDDEN], F32)
            h_hi, h_lo = sb(f"{name}_h_hi", [P, KH * CAP], F32R), sb(f"{name}_h_lo", [P, KH * CAP], F32R)
            y = sb(f"{name}_y", [CAP, D], F32)
            G, U, HT = ps(f"{name}_G", [P, HALF], F32), ps(f"{name}_U", [P, HALF], F32), ps(f"{name}_HT", [P, HALF], F32)
            Y, XT = ps(f"{name}_Y", [P, 2, HALF], F32), ps(f"{name}_XT", [P, 2, HALF], F32)
            s = lambda what: t.sem(f"{name}_{what}")
            hi_done = [s(f"{w}_hi") for w in ("gate", "up", "down")]
            lo_done = [s(f"{w}_lo") for w in ("gate", "up", "down")]
            gate_done, up_done, down_done = s("gate_done"), s("up_done"), s("down_done")
            picked, gathered, x_turned, x_hi_done, x_lo_done = s("picked"), s("gathered"), s("x_turned"), s("x_hi"), s("x_lo")
            gated_done, hid_done, h_turned, h_hi_done, h_lo_done = s("gated"), s("hid"), s("h_turned"), s("h_hi"), s("h_lo")
            pick_seen = s("pick_seen")
            y_act, y_dve, y_stored = s("y_act"), s("y_dve"), s("y_stored")

            def steady_blocks(eng):
                return eng.value_load(self.control[0:1, 0:1], min_val=EXPERTS - 3, max_val=ROWS - 3)

            def in_turn(eng, step):
                last = steady_blocks(eng) + 2
                step(0, True, False)
                step(1, False, False)
                with eng.Fori(2, last) as b:
                    step(b, False, False)
                step(last, False, True)
                return last

            with nc.Block() as block:
                @block.sync
                def _(sp):
                    def load(w, b, expert):
                        sp.wait_ge(hi_done[w], 2 * b)
                        sp.wait_ge(lo_done[w], 2 * b)
                        self.load(sp, w, expert)

                    def expert_of(b):
                        return sp.value_load(self.control[0:1, bass.ds(b + 1, 1)], min_val=0, max_val=EXPERTS - 1)

                    last = steady_blocks(sp) + 2
                    for w in range(2):
                        load(w, 1, 1)
                    with sp.Fori(1, last) as b:
                        following, expert = expert_of(b + 1), expert_of(b)
                        for w in range(2):
                            load(w, b + 1, following)
                        load(2, b, expert)
                    load(2, last, expert_of(last))

                @block.gpsimd
                def _(pool):
                    def gather(b, first):
                        if not first:
                            pool.wait_ge(x_turned, b)
                        pool.tensor_copy(pick[:, :], self.table[:, b:b + 1] if first else self.table[:, bass.ds(b, 1)])\
                            .then_inc(picked, 1)
                        wait_apart(pool, picked, b + 1, pick_seen)
                        pool.indirect_dma_start(out=xg[:, :], out_offset=None, in_=self.hn_rows,
                                                in_offset=bass.IndirectOffsetOnAxis(pick[:, :], 0)).then_inc(gathered, 16)

                    def store(b):
                        pool.wait_ge(y_act, b + 1)
                        pool.wait_ge(y_dve, b + 1)
                        rows = self.out_rows.rearrange("(r c) n -> r c n", c=CAP)
                        pool.dma_start(rows[b] if isinstance(b, int) else rows[bass.ds(b, 1)].rearrange("r c n -> (r c) n"),
                                       y[:, :]).then_inc(y_stored, 16)

                    def step(b, first, last):
                        if not last:
                            gather(b + 1, False)
                        if not first:
                            store(b - 1)
                    gather(0, True)
                    last = in_turn(pool, step)
                    store(last)
                    pool.wait_ge(y_stored, 16 * (last + 1))

                def times(pe, out, left, right, K, n, N):
                    (l_hi, l_lo), (r_hi, r_lo) = left, right
                    for k in range(K):
                        rows = slice(k * CAP, (k + 1) * CAP)
                        cols = slice(k * N + n * HALF, k * N + (n + 1) * HALF)
                        pe.matmul(out, l_hi[:, rows], r_hi[:, cols], start=(k == 0), stop=False)
                        pe.matmul(out, l_lo[:, rows], r_hi[:, cols], start=False, stop=False)
                        last = pe.matmul(out, l_hi[:, rows], r_lo[:, cols], start=False, stop=(k == K - 1))
                    return last

                @block.tensor
                def _(pe):
                    def turn_x(b):
                        pe.wait_ge(gathered, 16 * (b + 1))
                        wait_count(pe, x_lo_done, 2 * b)
                        for half in range(2):
                            for k in range(4):
                                kk = 4 * half + k
                                last = pe.transpose(XT[:, half, k * CAP:(k + 1) * CAP], xg[:, kk * P:(kk + 1) * P],
                                                    t.ident[0:CAP, 0:CAP])
                        last.then_inc(x_turned, 1)

                    def turn_h(b):
                        pe.wait_ge(hid_done, b + 1)
                        wait_count(pe, h_lo_done, b)
                        for k in range(KH):
                            last = pe.transpose(HT[:, k * CAP:(k + 1) * CAP], hid[:, k * P:(k + 1) * P],
                                                t.ident[0:CAP, 0:CAP])
                        last.then_inc(h_turned, 1)

                    def down(b):
                        pe.wait_ge(h_lo_done, b + 1)
                        pe.wait_ge(lo_done[2], 2 * b + 2)
                        wait_count(pe, y_act, b)
                        wait_count(pe, y_dve, b)
                        for n in range(2):
                            times(pe, Y[0:CAP, n, :], (h_hi, h_lo), (hi[2], lo[2]), KH, n, D).then_inc(down_done, 1)

                    def step(b, first, last):
                        pe.wait_ge(x_lo_done, 2 * b + 2)
                        pe.wait_ge(lo_done[0], 2 * b + 2)
                        if not first:
                            pe.wait_ge(gated_done, b)
                        times(pe, G[0:CAP, :], (x_hi, x_lo), (hi[0], lo[0]), KD, 0, HIDDEN).then_inc(gate_done, 1)
                        if not first:
                            turn_h(b - 1)
                        pe.wait_ge(lo_done[1], 2 * b + 2)
                        if not first:
                            pe.wait_ge(hid_done, b)
                        times(pe, U[0:CAP, :], (x_hi, x_lo), (hi[1], lo[1]), KD, 0, HIDDEN).then_inc(up_done, 1)
                        if not last:
                            turn_x(b + 1)
                        if not first:
                            down(b - 1)
                    turn_x(0)
                    last = in_turn(pe, step)
                    turn_h(last)
                    down(last)

                @block.scalar
                def _(act):
                    def split(w, b, piece):
                        if piece == 0:
                            act.wait_ge(self.raw_loaded[w], 16 * (b + 1))
                            wait_count(act, *((gate_done, b), (up_done, b), (down_done, 2 * b))[w])
                        cut = slice(piece * PIECE, (piece + 1) * PIECE)
                        act.copy(hi[w][:, cut], self.raw[w][:, cut]).then_inc(hi_done[w], 1)

                    def x_part(b):
                        act.wait_ge(x_turned, b + 1)
                        for half in range(2):
                            act.copy(x_hi[:, half * 4 * CAP:(half + 1) * 4 * CAP], XT[:, half, 0:4 * CAP]).then_inc(x_hi_done, 1)

                    def step(b, first, last):
                        act.wait_ge(gate_done, b + 1)
                        wait_count(act, hid_done, b)
                        act.activation(gated[:, :], G[0:CAP, :], ACT.Silu, bias=t.zero_col[0:CAP, :]).then_inc(gated_done, 1)
                        if not first:
                            act.wait_ge(h_turned, b)
                            act.copy(h_hi[:, :], HT[:, 0:KH * CAP]).then_inc(h_hi_done, 1)
                        if not last:
                            split(0, b + 1, 0)
                            split(0, b + 1, 1)
                            x_part(b + 1)
                            split(1, b + 1, 0)
                            split(1, b + 1, 1)
                        if not first:
                            act.wait_ge(down_done, 2 * b - 1)
                            wait_count(act, y_stored, 16 * (b - 1))
                            act.copy(y[:, 0:HALF], Y[0:CAP, 0, :]).then_inc(y_act, 1)
                        split(2, b, 0)
                        split(2, b, 1)

                    x_part(0)
                    for w in range(2):
                        split(w, 0, 0)
                        split(w, 0, 1)
                    last = in_turn(act, step)
                    act.wait_ge(h_turned, last + 1)
                    act.copy(h_hi[:, :], HT[:, 0:KH * CAP]).then_inc(h_hi_done, 1)
                    act.wait_ge(down_done, 2 * last + 1)
                    act.wait_ge(y_stored, 16 * last)
                    act.copy(y[:, 0:HALF], Y[0:CAP, 0, :]).then_inc(y_act, 1)

                @block.vector
                def _(dve):
                    def split(w, b, piece):
                        dve.wait_ge(hi_done[w], 2 * b + piece + 1)
                        cut = slice(piece * PIECE, (piece + 1) * PIECE)
                        dve.tensor_tensor(lo[w][:, cut], self.raw[w][:, cut], hi[w][:, cut].bitcast(F32), ALU.subtract)\
                           .then_inc(lo_done[w], 1)

                    def x_part(b):
                        for half in range(2):
                            dve.wait_ge(x_hi_done, 2 * b + half + 1)
                            cut = slice(half * 4 * CAP, (half + 1) * 4 * CAP)
                            dve.tensor_tensor(x_lo[:, cut], XT[:, half, 0:4 * CAP], x_hi[:, cut].bitcast(F32), ALU.subtract)\
                               .then_inc(x_lo_done, 1)

                    def h_part(b):
                        dve.wait_ge(h_hi_done, b + 1)
                        dve.tensor_tensor(h_lo[:, :], HT[:, 0:KH * CAP], h_hi[:, :].bitcast(F32), ALU.subtract)\
                           .then_inc(h_lo_done, 1)

                    def y_part(b):
                        dve.wait_ge(down_done, 2 * b + 2)
                        wait_count(dve, y_stored, 16 * b)
                        dve.tensor_copy(y[:, HALF:D], Y[0:CAP, 1, :]).then_inc(y_dve, 1)

                    def step(b, first, last):
                        if not first:
                            h_part(b - 1)
                        if not last:
                            split(0, b + 1, 0)
                            split(0, b + 1, 1)
                        dve.wait_ge(up_done, b + 1)
                        dve.tensor_tensor(hid[:, :].rearrange("q (k p) -> q p k", k=KH), gated[:, :]
                                          .rearrange("q (p k) -> q p k", k=KH), U[0:CAP, :]
                                          .rearrange("q (p k) -> q p k", k=KH), ALU.mult).then_inc(hid_done, 1)
                        if not last:
                            x_part(b + 1)
                            split(1, b + 1, 0)
                            split(1, b + 1, 1)
                        if not first:
                            y_part(b - 1)
                        split(2, b, 0)
                        split(2, b, 1)

                    x_part(0)
                    for w in range(2):
                        split(w, 0, 0)
                        split(w, 0, 1)
                    last = in_turn(dve, step)
                    h_part(last)
                    y_part(last)


    def combine(self):
        t, nc, name = self.t, self.t.nc, self.name
        BUFS = 8
        with ExitStack() as ctx:
            rows = ctx.enter_context(nc.sbuf_tensor(f"{name}_rows", [P, BUFS, D], F32))
            gathered = [t.sem(f"{name}_back_{i}") for i in range(BUFS)]
            added = t.sem(f"{name}_added")
            with nc.Block() as block:
                @block.gpsimd
                def _(pool):
                    for m in range(2 * NT):
                        tt, c = divmod(m, 2)
                        if m >= BUFS:
                            pool.wait_ge(added, m - BUFS + 1)
                        pool.indirect_dma_start(out=rows[:, m % BUFS, :], out_offset=None, in_=self.out_rows,
                                                in_offset=bass.IndirectOffsetOnAxis(
                                                    self.out_slot[:, c * NT + tt:c * NT + tt + 1], 0))\
                            .then_inc(gathered[m % BUFS], 16)

                @block.vector
                def _(dve):
                    for m in range(2 * NT):
                        tt, c = divmod(m, 2)
                        dve.wait_ge(gathered[m % BUFS], 16 * (m // BUFS + 1))
                        if c:
                            dve.wait_ge(added, m)
                        dve.scalar_tensor_tensor(out=t.x[:, tt, :], in0=rows[:, m % BUFS, :],
                                                 scalar=self.weight[:, c, tt:tt + 1], in1=t.x[:, tt, :],
                                                 op0=ALU.mult, op1=ALU.add).then_inc(added, 1)


def mixture(t, name, args, layer):
    with ExitStack() as ctx:
        moe = Experts(t, name, args["moe_w_gate"][layer], args["moe_w_up"][layer], args["moe_w_down"][layer],
                      t.dram, ctx)
        route(t, f"{name}r", args["norm_ffn"][layer:layer + 1, :], args["moe_w_group"][layer],
              args["moe_b_group"][layer], args["moe_w_router"][layer], args["moe_b_router"][layer], moe)
        moe.run()
        moe.combine()


def program(nc, args, out, stages=99):
    with ExitStack() as stack:
        t = Trunk(nc, stack)
        dram = lambda n, shape, dt: nc.dram_tensor(n, shape, dt, kind="Internal").ap()
        t.dram = (dram("hn_rows", (T, D), F32), dram("slot_table", (CAP * COLS, 1), I32),
                  dram("out_rows", (ROWS * CAP, D), F32))
        setup(t, args["x"])
        if stages >= 1:
            windowed_attention(t, args["norm_mix"][0:1, :], args["swa_w_qkv"][0], args["swa_w_o"][0],
                               args["swa_sink"][0:1, :])
        if stages >= 2:
            mixture(t, "m0", args, 0)
            t.clear_semaphores()
        if stages >= 3:
            differential_attention(t, args["norm_mix"][1:2, :], args["diff_w_qkv"][0], args["diff_w_o"][0],
                                   args["diff_lambda"][0], args["diff_subln"][0], 0.8 - 0.6 * math.exp(-0.3))
        if stages >= 4:
            mixture(t, "m1", args, 1)
        if stages >= 5:
            return final_norm(t, args["final_norm"].unsqueeze(0), out)
        stored = t.sem("out_stored")
        with nc.Block() as block:
            @block.sync
            def _(sp):
                for tt in range(NT):
                    sp.dma_start(out[0, tt * P:(tt + 1) * P, :], t.x[:, tt, :]).then_inc(stored, 16)
                sp.wait_ge(stored, 16 * NT)


_INS = ("x", "norm_mix", "norm_ffn", "swa_w_qkv", "swa_w_o", "swa_sink", "diff_w_qkv", "diff_w_o", "diff_lambda",
        "diff_subln", "moe_w_group", "moe_b_group", "moe_w_router", "moe_b_router", "moe_w_gate", "moe_w_up",
        "moe_w_down", "final_norm")


def kernel(**inputs):
    import numpy as np
    import concourse.bacc as bacc
    from concourse.bass_utils import run_bass_kernel_spmd

    nc = bacc.Bacc("TRN2", target_bir_lowering=False, num_devices=1)
    arrays, args = {}, {}
    for name in _INS:
        a = np.ascontiguousarray(inputs[name])
        arrays[f"in_{name}_dram"] = a
        args[name] = nc.dram_tensor(f"in_{name}_dram", a.shape, mybir.dt.from_np(a.dtype), kind="ExternalInput").ap()
    out = nc.dram_tensor("out_0_dram", (1, T, D), F32, kind="ExternalOutput").ap()
    program(nc, args, out)
    r = run_bass_kernel_spmd(nc, [arrays], core_ids=[0])
    return r.results[0]["out_0_dram"]
```

```python
import math
from contextlib import ExitStack

import concourse.bass as bass
from concourse import mybir

F32 = mybir.dt.float32
F32R = mybir.dt.float32r
I32 = mybir.dt.int32
ALU = mybir.AluOpType
ACT = mybir.ActivationFunctionType
AX = mybir.AxisListType.X

P = 128
T = 1024
D = 1024
NT = T // P
KD = D // P
HALF = 512
HEAD = 64
Q_SCALE = HEAD ** -0.5
NORM_EPS = 1e-6
SUBLN_EPS = 1e-5
MASKED = -1e30
HALVES = (slice(0, 64), slice(64, 128))

GROUPS = 4
PER_GROUP = 8
EXPERTS = GROUPS * PER_GROUP
HIDDEN = 512
KH = HIDDEN // P
TOP_K = 2
CAP = 96
SPARE = T * TOP_K // CAP
ROWS = EXPERTS + SPARE
COLS = ROWS + 2
STEPS = T // CAP
PIECE = KD * HIDDEN // 2


class Step:

    def __init__(self, eng, sem, base=0):
        self.eng, self.sem, self.base, self.n = eng, sem, base, 0

    def __call__(self, instruction):
        self.n += 1
        instruction.then_inc(self.sem, 1)
        self.eng.wait_ge(self.sem, self.base + self.n)


def wait_count(eng, sem, count):
    if not (isinstance(count, int) and count == 0):
        eng.wait_ge(sem, count)


def wait_apart(eng, sem, count, passed):
    eng.wait_ge(sem, count)
    eng.sem_inc(passed, 1)


class Trunk:
    def __init__(self, nc, stack):
        self.nc, self.stack, self.used = nc, stack, []

    def sem(self, name):
        handle = self.nc.alloc_semaphore(name=name)
        self.used.append(handle)
        return handle

    def clear_semaphores(self):
        numbers = sorted(h.num for h in self.used)
        spans = []
        for n in numbers:
            if spans and spans[-1][1] == n:
                spans[-1][1] = n + 1
            else:
                spans.append([n, n + 1])
        with self.nc.Block() as block:
            @block.gpsimd
            def _(pool):
                for a, b in spans:
                    pool.sem_clear(range(a, b))
        for h in self.used:
            self.nc.release_semaphore(h)
        self.used = []


def setup(t, x):
    nc = t.nc
    keep = t.stack.enter_context
    t.x = keep(nc.sbuf_tensor("x_res", [P, NT, D], F32))
    t.ident = keep(nc.sbuf_tensor("ident", [P, P], F32))
    t.zero_col = keep(nc.sbuf_tensor("zero_col", [P, 1], F32))
    t.eps_col = keep(nc.sbuf_tensor("eps_col", [P, 1], F32))
    t.weight = keep(nc.sbuf_tensor("choice_weight", [P, 2, NT], F32))
    t.out_slot = keep(nc.sbuf_tensor("choice_slot", [P, 2 * NT], I32))
    made, t.x_loaded = t.sem("const_made"), [t.sem(f"x_loaded_{i}") for i in range(NT // 2)]
    with nc.Block() as block:
        @block.sync
        def _(sp):
            for i, loaded in enumerate(t.x_loaded):
                sp.dma_start(t.x[:, 2 * i:2 * i + 2, :], x[0, 2 * i * P:2 * (i + 1) * P, :]
                             .rearrange("(a p) n -> p a n", p=P)).then_inc(loaded, 16)

        @block.gpsimd
        def _(pool):
            pool.memset(t.ident[:, :], 0.0).then_inc(made, 1)
            pool.memset(t.zero_col[:, :], 0.0)
            pool.memset(t.eps_col[:, :], NORM_EPS)
            pool.wait_ge(made, 1)
            pool.affine_select(out=t.ident[:, :], in_=t.ident[:, :], compare_op=ALU.not_equal, fill=1.0,
                               base=0, pattern=[[-1, P]], channel_multiplier=1).then_inc(made, 1)


class Resident:

    def complete(self, eng, tt):
        pass

    def add(self, dve, tt):
        pass


class Loaded(Resident):

    def __init__(self, t):
        self.t = t

    def complete(self, eng, tt):
        eng.wait_ge(self.t.x_loaded[tt // 2], 16)


class Combined:

    def __init__(self, t, name, out_rows, buffers):
        self.t, self.out_rows, self.buffers = t, out_rows, buffers
        self.gathered = [t.sem(f"{name}_back_{i}") for i in range(len(buffers))]
        self.added = t.sem(f"{name}_added")

    def gather(self, pool):
        bufs = len(self.buffers)
        for m in range(2 * NT):
            tt, c = divmod(m, 2)
            if m >= bufs:
                pool.wait_ge(self.added, m - bufs + 1)
            pool.indirect_dma_start(out=self.buffers[m % bufs], out_offset=None, in_=self.out_rows,
                                    in_offset=bass.IndirectOffsetOnAxis(self.t.out_slot[:, c * NT + tt:c * NT + tt + 1], 0))\
                .then_inc(self.gathered[m % bufs], 16)

    def add(self, dve, tt):
        bufs = len(self.buffers)
        for c in range(TOP_K):
            m = 2 * tt + c
            dve.wait_ge(self.gathered[m % bufs], 16 * (m // bufs + 1))
            if c:
                dve.wait_ge(self.added, m)
            dve.scalar_tensor_tensor(out=self.t.x[:, tt, :], in0=self.buffers[m % bufs],
                                     scalar=self.t.weight[:, c, tt:tt + 1], in1=self.t.x[:, tt, :],
                                     op0=ALU.mult, op1=ALU.add).then_inc(self.added, 1)

    def complete(self, eng, tt):
        eng.wait_ge(self.added, 2 * (tt + 1))


class Norm:

    def __init__(self, t, name, gain, sb, banks, source, tiles_T=NT, rows_dram=None, bufs=2):
        self.t, self.gain, self.banks, self.source, self.rows_dram = t, gain, banks, source, rows_dram
        self.tiles_T, self.bufs = tiles_T, bufs
        self.gain_b = sb(f"{name}_gain", [P, D], F32)
        self.junk = sb(f"{name}_junk", [P, D], F32)
        self.hn = sb(f"{name}_hn", [P, bufs, D], F32)
        self.ssq = sb(f"{name}_ssq", [P, NT], F32)
        self.rms = sb(f"{name}_rms", [P, NT], F32)
        self.rstd = sb(f"{name}_rstd", [P, NT], F32)
        self.hnT = sb(f"{name}_hnT", [P, KD, tiles_T * P], F32)
        s = lambda what: t.sem(f"{name}_{what}")
        self.gain_loaded, self.squared, self.rms_ready, self.chain = s("gain_loaded"), s("squared"), s("rms_ready"), s("chain")
        self.hn_ready, self.turned, self.copied, self.used = s("hn_ready"), s("turned"), s("copied"), s("used")
        self.rows_stored = [s(f"rows_stored_{i}") for i in range(bufs)] if rows_dram is not None else []

    def tile_T(self, tt):
        at = tt % self.tiles_T
        return self.hnT[:, :, at * P:(at + 1) * P]

    def sync_load(self, sp):
        sp.dma_start(self.gain_b[:, :], self.gain.broadcast_to((P, D))).then_inc(self.gain_loaded, 16)

    def sync_store(self, sp):
        for tt in range(NT):
            sp.wait_ge(self.hn_ready, tt + 1)
            sp.dma_start(self.rows_dram[tt * P:(tt + 1) * P, :], self.hn[:, tt % self.bufs, :])\
              .then_inc(self.rows_stored[tt % self.bufs], 16)

    def sync_stored(self, sp):
        for stored in self.rows_stored:
            sp.wait_ge(stored, 16 * NT // self.bufs)

    def scalar(self, act):
        for tt in range(NT + 2):
            if tt < NT:
                self.source.complete(act, tt)
                if tt:
                    act.wait_ge(self.squared, tt)
                act.activation(self.junk[:, :], self.t.x[:, tt, :], ACT.Square, bias=self.t.zero_col[:, :],
                               accum_out=self.ssq[:, tt:tt + 1]).then_inc(self.squared, 1)
                act.wait_ge(self.squared, tt + 1)
                act.activation(self.rms[:, tt:tt + 1], self.ssq[:, tt:tt + 1], ACT.Sqrt, bias=self.t.eps_col[:, :],
                               scale=1.0 / D).then_inc(self.rms_ready, 1)
            if tt >= 2:
                done = tt - 2
                act.wait_ge(self.turned, done + 1)
                if done >= self.tiles_T:
                    act.wait_ge(self.used, done - self.tiles_T + 1)
                act.copy(self.tile_T(done), self.banks[:, 2 * (done % 2):2 * (done % 2) + 2, :]
                         .rearrange("p b (k n) -> p (b k) n", k=4)).then_inc(self.copied, 1)

    def vector(self, dve):
        self.source.add(dve, 0)
        for tt in range(NT):
            if tt + 1 < NT:
                self.source.add(dve, tt + 1)
            dve.wait_ge(self.rms_ready, tt + 1)
            dve.reciprocal(self.rstd[:, tt:tt + 1], self.rms[:, tt:tt + 1]).then_inc(self.chain, 1)
            if tt == 0:
                dve.wait_ge(self.gain_loaded, 16)
            else:
                if tt >= self.bufs:
                    dve.wait_ge(self.turned, tt - self.bufs + 1)
                    if self.rows_dram is not None:
                        dve.wait_ge(self.rows_stored[tt % self.bufs], 16 * (tt // self.bufs))
            dve.wait_ge(self.chain, tt + 1)
            dve.scalar_tensor_tensor(
                out=self.hn[:, tt % self.bufs, :].rearrange("q (k p) -> q p k", k=KD),
                in0=self.t.x[:, tt, :].rearrange("q (p k) -> q p k", k=KD), scalar=self.rstd[:, tt:tt + 1],
                in1=self.gain_b[:, :].rearrange("q (p k) -> q p k", k=KD), op0=ALU.mult, op1=ALU.mult)\
               .then_inc(self.hn_ready, 1)

    def turn(self, pe, tt):
        pe.wait_ge(self.hn_ready, tt + 1)
        if tt >= 2:
            pe.wait_ge(self.copied, tt - 1)
        for k in range(KD):
            last = pe.transpose(self.banks[:, 2 * (tt % 2) + k // 4, k % 4 * P:(k % 4 + 1) * P],
                                self.hn[:, tt % self.bufs, k * P:(k + 1) * P], self.t.ident[:, :])
        last.then_inc(self.turned, 1)

    def tensor(self, pe):
        for tt in range(NT):
            self.turn(pe, tt)
        pe.wait_ge(self.copied, NT)


class OutProjection:

    def __init__(self, t, name, w_o, oT, w_sb, banks, rows):
        self.t, self.w_o, self.oT, self.w_sb, self.banks, self.rows = t, w_o, oT, w_sb, banks, rows
        s = lambda what: t.sem(f"{name}_{what}")
        self.loaded, self.done, self.added = s("wo_loaded"), s("wo_done"), s("wo_added")

    def sync_load(self, sp):
        sp.dma_start(self.w_sb[:, :, :], self.w_o.rearrange("(k p) n -> p k n", p=P)).then_inc(self.loaded, 16)

    def tensor(self, pe, tt, oT=None):
        oT = self.oT[:, :, tt * P:(tt + 1) * P] if oT is None else oT
        for n in range(2):
            bank = 2 * (tt % 2) + n
            if tt >= 2:
                pe.wait_ge(self.added, 2 * (tt - 2) + n + 1)
            for k in range(KD):
                last = pe.matmul(self.banks[:, bank, :], oT[:, k, :],
                                 self.w_sb[:, k, n * HALF:(n + 1) * HALF], start=(k == 0), stop=(k == KD - 1))
            last.then_inc(self.done, 1)

    def vector(self, dve, tt):
        for n in range(2):
            dve.wait_ge(self.done, 2 * tt + n + 1)
            xs = self.t.x[:, tt, n * HALF:(n + 1) * HALF]
            dve.tensor_tensor(xs, self.banks[:, 2 * (tt % 2) + n, :], xs, ALU.add).then_inc(self.added, 1)


def windowed_attention(t, gain, w_qkv, w_o, sink):
    nc = t.nc
    KV = 4
    QH = 4
    NQ = KV * QH
    WIN = 3 * P
    W_COLS = QH * HEAD + 2 * HEAD
    blocks = [(max(i - 1, 0), min(i + 1, NT - 1)) for i in range(NT)]
    tiles = [b - a + 1 for a, b in blocks]
    before = [sum(tiles[:i]) for i in range(NT)]
    TILES = sum(tiles)
    with ExitStack() as ctx:
        sb = lambda *a: ctx.enter_context(nc.sbuf_tensor(*a))
        S = ctx.enter_context(nc.psum_tensor("a0_S", [P, 4, HALF], F32))
        TB = ctx.enter_context(nc.psum_tensor("a0_T", [P, 2, HALF], F32))
        O = ctx.enter_context(nc.psum_tensor("a0_O", [P, 2, HALF], F32))
        norm = Norm(t, "a0n", gain, sb, S, Loaded(t))
        w_sb = sb("a0_w", [P, KD, W_COLS], F32)
        q_parts = sb("a0_q_parts", [P, QH, T], F32R)
        k_hi, k_lo = sb("a0_k_hi", [P, T], F32R), sb("a0_k_lo", [P, T], F32R)
        kvT = sb("a0_kvT", [P, T], F32)
        v_rows = sb("a0_v_rows", [P, NT, 2, HEAD], F32)
        probs = sb("a0_probs", [P, 2, QH, WIN], F32)
        pT = sb("a0_pT", [P, 2, 3, QH * P], F32)
        bias = sb("a0_bias", [P, QH, WIN], F32)
        dist = sb("a0_dist", [P, WIN], F32)
        zero_rows = sb("a0_zero_rows", [CAP, D], F32)
        far = sb("a0_far", [P, WIN], F32)
        sinks = sb("a0_sinks", [P, NQ], F32)
        sink4 = sb("a0_sink4", [P, QH], F32)
        top4 = sb("a0_top4", [P, 2, QH], F32)
        neg4 = sb("a0_neg4", [P, 2, QH], F32)
        snk4 = sb("a0_snk4", [P, 2, QH], F32)
        sum4 = sb("a0_sum4", [P, 2, QH], F32)
        exs4 = sb("a0_exs4", [P, 2, QH], F32)
        inv4 = sb("a0_inv4", [P, 2, QH], F32)
        oT = sb("a0_oT", [P, KD, T], F32)
        out_proj = OutProjection(t, "a0o", w_o, oT, norm.hnT, S, None)

        w_loaded, sink_loaded = t.sem("a0_w_loaded"), t.sem("a0_sink_loaded")
        proj_done, hi_ready, parts_ready = t.sem("a0_proj_done"), t.sem("a0_hi_ready"), t.sem("a0_parts_ready")
        v_turned, v_rows_ready = t.sem("a0_v_turned"), t.sem("a0_v_rows_ready")
        scores, scores_seen, biased = t.sem("a0_scores"), t.sem("a0_scores_seen"), t.sem("a0_biased")
        stats, exp_done, probs_ready = t.sem("a0_stats"), t.sem("a0_exp_done"), t.sem("a0_probs_ready")
        p_turned, pT_ready = t.sem("a0_p_turned"), t.sem("a0_pT_ready")
        pv_done, oT_ready = t.sem("a0_pv_done"), t.sem("a0_oT_ready")
        spare_zeroed = t.sem("spare_zeroed")
        dve_own, prep, zeroed, iota_done = t.sem("a0_dve_own"), t.sem("a0_prep"), t.sem("a0_zeroed"), t.sem("a0_iota")

        with nc.Block() as block:
            @block.sync
            def _(sp):
                norm.sync_load(sp)
                sp.dma_start(sinks[:, :], sink.broadcast_to((P, NQ))).then_inc(sink_loaded, 16)

                def load_weights(g):
                    for at, n, col in ((0, QH * HEAD, g * (QH * HEAD)), (QH * HEAD, HEAD, NQ * HEAD + g * HEAD),
                                       (QH * HEAD + HEAD, HEAD, (NQ + KV) * HEAD + g * HEAD)):
                        sp.dma_start(w_sb[:, :, at:at + n],
                                     w_qkv.rearrange("(p k) n -> p k n", k=KD)[:, :, bass.ds(col, n)])\
                          .then_inc(w_loaded, 16)

                load_weights(0)
                with sp.Fori(1, KV) as g:
                    sp.wait_ge(proj_done, 6 * g)
                    load_weights(g)
                sp.wait_ge(proj_done, 6 * KV)
                out_proj.sync_load(sp)
                sp.wait_ge(zeroed, 1)
                spare_rows = t.dram[1].rearrange("(r c) n -> r c n", c=CAP)[EXPERTS:ROWS]
                sp.dma_start(spare_rows.rearrange("r c n -> c r n"), zero_rows[:, :].unsqueeze(1)
                             .broadcast_to((CAP, SPARE, D))).then_inc(spare_zeroed, 16)
                sp.wait_ge(spare_zeroed, 16)

            @block.gpsimd
            def _(pool):
                pool.iota(dist[:, :].bitcast(I32), pattern=[[-1, WIN]], base=P, channel_multiplier=1).then_inc(iota_done, 1)
                pool.memset(zero_rows[:, :], 0.0).then_inc(zeroed, 1)

            @block.scalar
            def _(act):
                norm.scalar(act)
                with act.Fori(0, KV) as g:
                    for o in range(6):
                        act.wait_ge(proj_done, 6 * g + o + 1)
                        j, n = divmod(o, 2)
                        cols = slice(n * HALF, (n + 1) * HALF)
                        if j < 2:
                            for e, part in enumerate(HALVES):
                                last = act.mul(q_parts[part, 2 * j + e, cols], S[part, o % 4, :], Q_SCALE)
                            last.then_inc(hi_ready, 1)
                        else:
                            for there in HALVES:
                                act.copy(k_hi[there, cols], S[0:64, o % 4, :])
                            act.copy(kvT[:, cols], S[:, o % 4, :]).then_inc(hi_ready, 1)

                    def exponentials(i):
                        n = 8 * g + i
                        act.wait_ge(stats, n + 1)
                        for h in range(QH):
                            row = probs[:, i % 2, h, 0:tiles[i] * P]
                            act.activation(row, row, ACT.Exp, bias=neg4[:, i % 2, h:h + 1],
                                           accum_out=sum4[:, i % 2, h:h + 1])
                        act.activation(exs4[:, i % 2, :], snk4[:, i % 2, :], ACT.Exp, bias=t.zero_col[:, :])\
                           .then_inc(exp_done, 1)

                    exponentials(0)
                    for i in range(NT):
                        if i + 1 < NT:
                            exponentials(i + 1)
                        n = 8 * g + i
                        if i >= 2:
                            act.wait_ge(pv_done, n - 1)
                        for j in range(tiles[i]):
                            c = TILES * g + before[i] + j
                            act.wait_ge(p_turned, c + 1)
                            act.copy(pT[:, i % 2, j, :], TB[:, (before[i] + j) % 2, :]).then_inc(pT_ready, 1)

            @block.vector
            def _(dve):
                norm.vector(dve)
                own = Step(dve, prep)
                dve.wait_ge(iota_done, 1)
                own(dve.tensor_copy(far[:, :], dist[:, :].bitcast(I32)))
                own(dve.tensor_scalar(dist[:, :], far[:, :], -1.0, None, ALU.mult))
                own(dve.tensor_tensor(dist[:, :], dist[:, :], far[:, :], ALU.max))
                own(dve.tensor_scalar(far[:, :], dist[:, :], float(P), MASKED, ALU.is_gt, ALU.mult))
                for h in range(QH):
                    last = dve.scalar_tensor_tensor(out=bias[:, h, :], in0=dist[:, :], scalar=-2.0 ** (-8.0 * (h + 1) / NQ),
                                                    in1=far[:, :], op0=ALU.mult, op1=ALU.add)
                own(last)
                dve.wait_ge(sink_loaded, 16)
                OWN = 4 + 5 * NT
                with dve.Fori(0, KV) as g:
                    own = Step(dve, dve_own, OWN * g)
                    own(dve.tensor_copy(sink4[:, :], sinks[:, bass.ds(g * QH, QH)]))
                    for o in range(6):
                        dve.wait_ge(hi_ready, 6 * g + o + 1)
                        j, n = divmod(o, 2)
                        cols = slice(n * HALF, (n + 1) * HALF)
                        for e, part in enumerate(HALVES):
                            if j < 2:
                                q = q_parts[:, 2 * j + e, cols]
                                last = dve.scalar_tensor_tensor(out=q[HALVES[1 - e]], in0=S[part, o % 4, :], scalar=Q_SCALE,
                                                                in1=q[part].bitcast(F32), op0=ALU.mult, op1=ALU.subtract)
                            else:
                                last = dve.tensor_tensor(k_lo[part, cols], S[0:64, o % 4, :],
                                                         k_hi[0:64, cols].bitcast(F32), ALU.subtract)
                        last.then_inc(parts_ready, 1)
                    for b in range(2):
                        dve.wait_ge(v_turned, 2 * g + b + 1)
                        source = TB[:, b, :].rearrange("p (a c) -> p a c", c=P)[:, :, HEAD:P]
                        for copy in range(2):
                            last = dve.tensor_copy(v_rows[:, 4 * b:4 * b + 4, copy, :], source)
                        last.then_inc(v_rows_ready, 1)

                    def masked_scores(i):
                        n = 8 * g + i
                        first = P if i == 0 else 0
                        width = tiles[i] * P
                        if i >= 2:
                            dve.wait_ge(p_turned, TILES * g + before[i - 1])
                        for h in range(QH):
                            wait_apart(dve, scores, 4 * n + h + 1, scores_seen)
                            dve.tensor_tensor_reduce(probs[:, i % 2, h, 0:width], S[:, h, 0:width],
                                                     bias[:, h, first:first + width], 1.0, MASKED,
                                                     ALU.add, ALU.max, top4[:, i % 2, h:h + 1]).then_inc(biased, 1)
                        dve.wait_ge(biased, 4 * n + 4)
                        own(dve.tensor_tensor(top4[:, i % 2, :], top4[:, i % 2, :], sink4[:, :], ALU.max))
                        own(dve.tensor_scalar(neg4[:, i % 2, :], top4[:, i % 2, :], -1.0, None, ALU.mult))
                        dve.tensor_tensor(snk4[:, i % 2, :], sink4[:, :], top4[:, i % 2, :], ALU.subtract).then_inc(stats, 1)

                    def normalise(i):
                        n = 8 * g + i
                        dve.wait_ge(exp_done, n + 1)
                        own(dve.tensor_tensor(sum4[:, i % 2, :], sum4[:, i % 2, :], exs4[:, i % 2, :], ALU.add))
                        own(dve.reciprocal(inv4[:, i % 2, :], sum4[:, i % 2, :]))
                        for h in range(QH):
                            row = probs[:, i % 2, h, 0:tiles[i] * P]
                            last = dve.tensor_scalar(row, row, inv4[:, i % 2, h:h + 1], None, ALU.mult)
                        last.then_inc(probs_ready, 1)

                    def heads_out(i):
                        dve.wait_ge(pv_done, 8 * g + i + 1)
                        out = O[:, i % 2, :].rearrange("p (h n) -> p h n", h=QH)
                        for e, part in enumerate((slice(0, 64), slice(64, 128))):
                            last = dve.tensor_copy(oT[part, bass.ds(2 * g, 2), i * P:(i + 1) * P], out[part, e:QH:2, :])
                        last.then_inc(oT_ready, 1)

                    masked_scores(0)
                    for i in range(NT):
                        if i + 1 < NT:
                            masked_scores(i + 1)
                        normalise(i)
                        if i >= 1:
                            heads_out(i - 1)
                    heads_out(NT - 1)
                    own(dve.tensor_scalar(bias[:, :, :], bias[:, :, :], 2.0 ** (-8.0 * QH / NQ), None, ALU.mult))
                    while own.n < OWN:
                        own(dve.tensor_copy(exs4[:, 0, 0:1], sink4[:, 0:1]))
                    assert own.n == OWN
                for tt in range(NT):
                    out_proj.vector(dve, tt)

            @block.tensor
            def _(pe):
                norm.tensor(pe)
                with pe.Fori(0, KV) as g:
                    pe.wait_ge(w_loaded, 48 * g + 48)
                    for o in range(6):
                        j, n = divmod(o, 2)
                        if o >= 4:
                            pe.wait_ge(parts_ready, 6 * g + o - 3)
                        for k in range(KD):
                            last = pe.matmul(S[:, o % 4, :], w_sb[:, k, j * P:(j + 1) * P],
                                             norm.hnT[:, k, n * HALF:(n + 1) * HALF], start=(k == 0), stop=(k == KD - 1))
                        last.then_inc(proj_done, 1)
                    for b in range(2):
                        pe.wait_ge(hi_ready, 6 * g + 5 + b)
                        for a in range(4):
                            last = pe.transpose(TB[:, b, a * P:(a + 1) * P], kvT[:, (4 * b + a) * P:(4 * b + a + 1) * P],
                                                t.ident[:, :])
                        last.then_inc(v_turned, 1)
                    pe.wait_ge(parts_ready, 6 * g + 6)
                    pe.wait_ge(v_rows_ready, 2 * g + 2)

                    def head_scores(i):
                        n = 8 * g + i
                        a, b = blocks[i]
                        for h in range(QH):
                            if i >= 1:
                                pe.wait_ge(biased, 4 * (n - 1) + h + 1)
                            for k_part in (k_hi, k_lo):
                                last = pe.matmul(S[:, h, 0:tiles[i] * P], q_parts[:, h, i * P:(i + 1) * P],
                                                 k_part[:, a * P:(b + 1) * P], start=(k_part is k_hi), stop=(k_part is k_lo))
                            last.then_inc(scores, 1)

                    def product(i):
                        n = 8 * g + i
                        pe.wait_ge(probs_ready, n + 1)

                        def turn(j):
                            c = TILES * g + before[i] + j
                            if before[i] + j >= 2:
                                pe.wait_ge(pT_ready, c - 1)
                            for h in range(QH):
                                last = pe.transpose(TB[:, (before[i] + j) % 2, h * P:(h + 1) * P],
                                                    probs[:, i % 2, h, j * P:(j + 1) * P], t.ident[:, :])
                            last.then_inc(p_turned, 1)

                        def times_v(j):
                            c = TILES * g + before[i] + j
                            pe.wait_ge(pT_ready, c + 1)
                            return pe.matmul(O[:, i % 2, :],
                                             v_rows[:, blocks[i][0] + j, :, :].rearrange("p a b -> p (a b)"),
                                             pT[:, i % 2, j, :], start=(j == 0), stop=(j == tiles[i] - 1))

                        turn(0)
                        turn(1)
                        if i >= 2:
                            pe.wait_ge(oT_ready, n - 1)
                        times_v(0)
                        if tiles[i] == 3:
                            turn(2)
                            times_v(1)
                        times_v(tiles[i] - 1).then_inc(pv_done, 1)

                    head_scores(0)
                    head_scores(1)
                    for i in range(NT):
                        if i + 2 < NT:
                            head_scores(i + 2)
                        product(i)
                pe.wait_ge(oT_ready, KV * NT)
                pe.wait_ge(out_proj.loaded, 16)
                for tt in range(NT):
                    out_proj.tensor(pe, tt)


def route(t, name, gain, w_group, b_group, w_router, b_router, moe):
    nc = t.nc
    NL = GROUPS + EXPERTS
    with ExitStack() as ctx:
        sb = lambda *a: ctx.enter_context(nc.sbuf_tensor(*a))
        ps = lambda *a: ctx.enter_context(nc.psum_tensor(*a))
        turn_banks = ps(f"{name}_T", [P, 4, HALF], F32)
        L_ps = ps(f"{name}_L", [P, 2, HALF], F32)
        R_ps = ps(f"{name}_R", [P, HALF], F32)
        C_ps = ps(f"{name}_C", [P, HALF], F32)
        table_ps = L_ps[0:CAP, 0, 0:CAP]
        norm = Norm(t, f"{name}n", gain, sb, turn_banks, Resident(), 2, moe.hn_rows, 4)
        w_sb = sb(f"{name}_w", [P, KD, NL], F32)
        b_sb = sb(f"{name}_b", [NL, 1], F32)
        lT = norm.junk
        lg = sb(f"{name}_lg", [P, NT, NL], F32)
        below = sb(f"{name}_below", [P, P], F32)
        ones = sb(f"{name}_ones", [P, P], F32)
        count_i = sb(f"{name}_count_i", [P, CAP], I32)
        count_up = sb(f"{name}_count_up", [P, CAP], F32)
        count_dn = sb(f"{name}_count_dn", [P, CAP], F32)
        token_i = sb(f"{name}_token_i", [P, NT], I32)
        token = sb(f"{name}_token", [P, NT], F32)
        place_hot = norm.hnT[:, :, :].rearrange("p a b -> p (a b)")[:, 0:2 * NT * CAP].rearrange("p (c n) -> p c n", n=CAP)
        row_hot = sb(f"{name}_row_hot", [P, 2 * NT, CAP], F32)
        v = lambda what, *shape: sb(f"{name}_{what}", [P, *shape], F32)
        gm, gh, gs = v("gm", NT), v("gh", NT, GROUPS), v("gs", NT, GROUPS)
        gd, gsum, pg = v("gd", NT, GROUPS), v("gsum", NT), v("pg", NT)
        le = v("le", NT, EXPERTS)
        top = v("top", 2, NT)
        seen = v("seen", NT, EXPERTS)
        code = v("code", 2, NT)
        hot = v("hot", 2, NT * EXPERTS)
        hots = v("hots", NT * EXPERTS)
        diff, ex, den = v("diff", NT), v("ex", NT), v("den", NT)
        tot = v("tot", NT, EXPERTS)
        base = v("base", NT + 1, EXPERTS)
        pos = v("pos", NT * EXPERTS)
        pick = v("pick", 2, NT * EXPERTS)
        place, extra0, more = v("place", 2 * NT), v("extra0", 2 * NT), v("more", 2 * NT)
        over = v("over", EXPERTS * STEPS)
        spare, run_a, run_b, first = v("spare", EXPERTS), v("run_a", EXPERTS), v("run_b", EXPERTS), v("first", EXPERTS)
        stepped = v("stepped", 2 * NT * STEPS)
        expert, row, slot_of_row = (v(what, 2 * NT) for what in ("expert", "row", "slot_of_row"))
        owner_cmp, ctl_f = v("owner_cmp", (COLS - EXPERTS) * EXPERTS), v("ctl_f", COLS + 1)
        steps_of = v("steps_of", STEPS)

        s = lambda what: t.sem(f"{name}_{what}")
        w_loaded, made, lT_ready = s("w_loaded"), s("made"), s("lT_ready")
        lg_done, own_s, act_in, act_out = s("lg_done"), s("own"), s("act_in"), s("act_out")
        hot_ready, counted, slots_hot, tabled = s("hot_ready"), s("counted"), s("slots_hot"), s("tabled")

        with nc.Block() as block:
            @block.sync
            def _(sp):
                norm.sync_load(sp)
                wide = dict(allow_slow_non_contiguous=True)
                sp.dma_start(w_sb[:, :, 0:GROUPS], w_group.rearrange("(p k) n -> p k n", k=KD)).then_inc(w_loaded, 16)
                sp.dma_start(w_sb[:, :, GROUPS:NL], w_router.rearrange("(p k) n -> p k n", k=KD)).then_inc(w_loaded, 16)
                sp.dma_start(b_sb[0:GROUPS, :], b_group.unsqueeze(1), **wide).then_inc(w_loaded, 16)
                sp.dma_start(b_sb[GROUPS:NL, :], b_router.unsqueeze(1), **wide).then_inc(w_loaded, 16)
                moe.load(sp, 0, 0)
                norm.sync_store(sp)
                moe.load(sp, 1, 0)
                moe.load(sp, 2, 0)
                for w in range(2):
                    sp.wait_ge(moe.hi_done[w], 2)
                    sp.wait_ge(moe.lo_done[w], 2)
                    moe.load(sp, w, 1)
                norm.sync_stored(sp)

            @block.gpsimd
            def _(pool):
                pool.memset(ones[:, :], 1.0).then_inc(made, 1)
                pool.iota(count_i[:, :], pattern=[[1, CAP]], base=0, channel_multiplier=0).then_inc(made, 1)
                pool.iota(token_i[:, :], pattern=[[P, NT]], base=0, channel_multiplier=1).then_inc(made, 1)
                pool.wait_ge(made, 1)
                pool.affine_select(out=below[:, :], in_=ones[:, :], compare_op=ALU.is_gt, fill=0.0, base=0,
                                   pattern=[[1, P]], channel_multiplier=-1).then_inc(made, 1)
                for w in range(2):
                    for piece in range(2):
                        moe.low_part(pool, w, 0, piece)

            @block.scalar
            def _(act):
                norm.scalar(act)
                act.wait_ge(w_loaded, 64)
                for n in range(2):
                    act.wait_ge(norm.used, 4 * (n + 1))
                    act.activation(lT[0:NL, n * HALF:(n + 1) * HALF], L_ps[0:NL, n, :], ACT.Identity, bias=b_sb[:, :])\
                       .then_inc(lT_ready, 1)
                act.wait_ge(act_in, 1)
                act.activation(gd[:, :, :], gd[:, :, :], ACT.Exp, bias=t.zero_col[:, :]).then_inc(act_out, 1)
                act.wait_ge(act_in, 2)
                act.activation(ex[:, :], diff[:, :], ACT.Exp, bias=t.zero_col[:, :]).then_inc(act_out, 1)
                for w in range(2):
                    act.wait_ge(moe.raw_loaded[w], 16)
                    for piece in range(2):
                        moe.high_part(act, w, piece)

            @block.tensor
            def _(pe):
                def logits(tt):
                    pe.wait_ge(norm.copied, tt + 1)
                    for k in range(KD):
                        last = pe.matmul(L_ps[0:NL, tt // 4, tt % 4 * P:(tt % 4 + 1) * P], w_sb[:, k, :],
                                         norm.tile_T(tt)[:, k, :], start=(k == 0), stop=(k == KD - 1))
                    last.then_inc(norm.used, 1)

                pe.wait_ge(w_loaded, 64)
                norm.turn(pe, 0)
                for tt in range(NT):
                    if tt + 1 < NT:
                        norm.turn(pe, tt + 1)
                    logits(tt)
                for n in range(2):
                    pe.wait_ge(lT_ready, n + 1)
                    for tt in range(4 * n, 4 * n + 4):
                        last = pe.transpose(R_ps[:, tt * NL:(tt + 1) * NL], lT[0:NL, tt * P:(tt + 1) * P], t.ident[0:NL, 0:NL])
                last.then_inc(lg_done, 1)
                pe.wait_ge(hot_ready, 1)
                pe.wait_ge(made, 4)
                pe.matmul(C_ps[:, 0:256], below[:, :], hots[:, :], start=True, stop=True)
                pe.matmul(C_ps[:, 256:512], ones[:, :], hots[:, :], start=True, stop=True).then_inc(counted, 1)
                pe.wait_ge(slots_hot, 1)
                for c in range(2 * NT):
                    last = pe.matmul(table_ps, place_hot[:, c, :], row_hot[:, c, :], start=(c == 0), stop=(c == 2 * NT - 1))
                last.then_inc(tabled, 1)

            @block.vector
            def _(dve):
                norm.vector(dve)
                own = Step(dve, own_s)
                tt_, ts_, red = dve.tensor_tensor, dve.tensor_scalar, dve.tensor_reduce
                dve.wait_ge(made, 4)
                own(dve.tensor_copy(count_up[:, :], count_i[:, :]))
                own(ts_(count_dn[:, :], count_up[:, :], -1.0, 64.0, ALU.mult, ALU.add))
                own(dve.tensor_copy(token[:, :], token_i[:, :]))
                own(ts_(steps_of[:, :], count_up[:, 1:STEPS + 1], float(CAP), None, ALU.mult))
                dve.wait_ge(lg_done, 1)
                own(dve.tensor_copy(lg[:, :, :], R_ps[:, 0:NT * NL].rearrange("p (a b) -> p a b", b=NL)))
                groups = lg[:, :, 0:GROUPS]
                over_g = lambda a: a.unsqueeze(2).broadcast_to((P, NT, GROUPS))
                over_e = lambda a: a.unsqueeze(2).broadcast_to((P, NT, EXPERTS))
                tiled = lambda a, n: a.unsqueeze(1).broadcast_to((P, NT, n))
                own(red(gm[:, :], groups, AX, ALU.max))
                tt_(gd[:, :, :], groups, over_g(gm[:, :]), ALU.subtract).then_inc(act_in, 1)
                own(tt_(gh[:, :, :], groups, over_g(gm[:, :]), ALU.is_equal))
                own(tt_(gs[:, :, :], gh[:, :, :], tiled(count_dn[:, 0:GROUPS], GROUPS), ALU.mult))
                own(red(gm[:, :], gs[:, :, :], AX, ALU.max))
                own(tt_(gh[:, :, :], gs[:, :, :], over_g(gm[:, :]), ALU.is_equal))
                own(ts_(gh[:, :, :], gh[:, :, :], -1.0, -MASKED, ALU.add, ALU.mult))
                own(tt_(le[:, :, :].rearrange("p a (g e) -> p a g e", g=GROUPS),
                        lg[:, :, GROUPS:NL].rearrange("p a (g e) -> p a g e", g=GROUPS),
                        gh[:, :, :].unsqueeze(3).broadcast_to((P, NT, GROUPS, PER_GROUP)), ALU.add))
                flat = lambda a: a[:, :, :].rearrange("p a b -> p (a b)")
                for c in range(TOP_K):
                    own(red(top[:, c, :], le[:, :, :], AX, ALU.max))
                    own(tt_(seen[:, :, :], le[:, :, :], over_e(top[:, c, :]), ALU.is_equal))
                    own(tt_(seen[:, :, :], seen[:, :, :], tiled(count_dn[:, 0:EXPERTS], EXPERTS), ALU.mult))
                    own(red(code[:, c, :], seen[:, :, :], AX, ALU.max))
                    own(tt_(hot[:, c, :].rearrange("p (a b) -> p a b", b=EXPERTS), seen[:, :, :], over_e(code[:, c, :]),
                            ALU.is_equal))
                    if c == 0:
                        own(dve.scalar_tensor_tensor(out=flat(le), in0=hot[:, 0, :], scalar=2 * MASKED, in1=flat(le),
                                                     op0=ALU.mult, op1=ALU.add))
                tt_(hots[:, :], hot[:, 0, :], hot[:, 1, :], ALU.add).then_inc(hot_ready, 1)
                tt_(diff[:, :], top[:, 1, :], top[:, 0, :], ALU.subtract).then_inc(act_in, 1)
                own(ts_(expert[:, :], code[:, :, :].rearrange("p a b -> p (a b)"), -1.0, 64.0, ALU.mult, ALU.add))
                own(dve.memset(base[:, 0, :], 0.0))
                dve.wait_ge(act_out, 2)
                own(red(gsum[:, :], gd[:, :, :], AX, ALU.add))
                own(dve.reciprocal(pg[:, :], gsum[:, :]))
                own(ts_(den[:, :], ex[:, :], 1.0, None, ALU.add))
                own(dve.reciprocal(den[:, :], den[:, :]))
                own(tt_(t.weight[:, 0, :], pg[:, :], den[:, :], ALU.mult))
                own(tt_(t.weight[:, 1, :], t.weight[:, 0, :], ex[:, :], ALU.mult))
                dve.wait_ge(counted, 1)
                own(dve.tensor_copy(flat(tot), C_ps[:, 256:512]))
                for a in range(NT):
                    own(tt_(base[:, a + 1, :], base[:, a, :], tot[:, a, :], ALU.add))
                own(tt_(pos[:, :], C_ps[:, 0:256], base[:, 0:NT, :].rearrange("p a b -> p (a b)"), ALU.add))
                twice = lambda a: a.unsqueeze(1).broadcast_to((P, 2, NT * EXPERTS))
                by_expert = pick[:, :, :].rearrange("p c (a b) -> p (c a) b", b=EXPERTS)
                own(tt_(pick[:, :, :], hot[:, :, :], twice(pos[:, :]), ALU.mult))
                own(red(place[:, :], by_expert, AX, ALU.add))
                total = base[:, NT, :]
                grid = over[:, :].rearrange("p (e j) -> p e j", j=STEPS)
                own(tt_(grid, total.unsqueeze(2).broadcast_to((P, EXPERTS, STEPS)),
                        steps_of[:, :].unsqueeze(1).broadcast_to((P, EXPERTS, STEPS)), ALU.is_gt))
                own(red(spare[:, :], grid, AX, ALU.add))
                source, target, shift = spare, run_a, 1
                while shift < EXPERTS:
                    own(dve.tensor_copy(target[:, 0:shift], source[:, 0:shift]))
                    own(tt_(target[:, shift:], source[:, shift:], source[:, 0:EXPERTS - shift], ALU.add))
                    source, target = target, (run_b if target is run_a else run_a)
                    shift *= 2
                running = source
                own(tt_(first[:, :], running[:, :], spare[:, :], ALU.subtract))
                own(tt_(pick[:, :, :].rearrange("p c (a b) -> p (c a) b", b=EXPERTS),
                        hot[:, :, :].rearrange("p c (a b) -> p (c a) b", b=EXPERTS),
                        first[:, :].unsqueeze(1).broadcast_to((P, 2 * NT, EXPERTS)), ALU.mult))
                own(red(extra0[:, :], by_expert, AX, ALU.add))
                ladder = stepped[:, :].rearrange("p (c j) -> p c j", j=STEPS)
                own(tt_(ladder, place[:, :].unsqueeze(2).broadcast_to((P, 2 * NT, STEPS)),
                        steps_of[:, :].unsqueeze(1).broadcast_to((P, 2 * NT, STEPS)), ALU.is_ge))
                own(red(more[:, :], ladder, AX, ALU.add))
                own(dve.scalar_tensor_tensor(out=place[:, :], in0=more[:, :], scalar=-float(CAP), in1=place[:, :],
                                             op0=ALU.mult, op1=ALU.add))
                own(tt_(row[:, :], extra0[:, :], more[:, :], ALU.add))
                own(ts_(row[:, :], row[:, :], float(EXPERTS - 1), None, ALU.add))
                own(tt_(row[:, :], row[:, :], expert[:, :], ALU.subtract))
                own(ts_(more[:, :], more[:, :], 0.0, None, ALU.is_gt))
                own(tt_(row[:, :], row[:, :], more[:, :], ALU.mult))
                own(tt_(row[:, :], row[:, :], expert[:, :], ALU.add))
                over_slots = lambda a, n: a.unsqueeze(2).broadcast_to((P, 2 * NT, n))
                own(tt_(row_hot[:, :, :], over_slots(row[:, :], CAP),
                        count_up[:, :].unsqueeze(1).broadcast_to((P, 2 * NT, CAP)), ALU.is_equal))
                for c in range(TOP_K):
                    half = row_hot[:, c * NT:(c + 1) * NT, 0:COLS]
                    own(tt_(half, half, token[:, :].unsqueeze(2).broadcast_to((P, NT, COLS)), ALU.mult))
                tt_(place_hot[:, :, :], over_slots(place[:, :], CAP),
                    count_up[:, :].unsqueeze(1).broadcast_to((P, 2 * NT, CAP)), ALU.is_equal).then_inc(slots_hot, 1)
                own(dve.scalar_tensor_tensor(out=slot_of_row[:, :], in0=row[:, :], scalar=float(CAP), in1=place[:, :],
                                             op0=ALU.mult, op1=ALU.add))
                own(dve.tensor_copy(t.out_slot[:, :], slot_of_row[:, :]))
                own(ts_(ctl_f[:, 0:1], running[:, EXPERTS - 1:EXPERTS], float(EXPERTS - 3), None, ALU.add))
                own(dve.tensor_copy(ctl_f[:, 1:1 + EXPERTS], count_up[:, 0:EXPERTS]))
                owners = owner_cmp[:, :].rearrange("p (b e) -> p b e", e=EXPERTS)
                own(tt_(owners, running[:, :].unsqueeze(1).broadcast_to((P, COLS - EXPERTS, EXPERTS)),
                        count_up[:, 0:COLS - EXPERTS].unsqueeze(2).broadcast_to((P, COLS - EXPERTS, EXPERTS)), ALU.is_le))
                own(red(ctl_f[:, 1 + EXPERTS:1 + COLS], owners, AX, ALU.add))
                own(ts_(ctl_f[:, 1 + EXPERTS:1 + COLS], ctl_f[:, 1 + EXPERTS:1 + COLS], float(EXPERTS - 1), None, ALU.min))
                own(dve.tensor_copy(moe.control[:, :], ctl_f[0:1, :]))
                dve.wait_ge(tabled, 1)
                own(dve.tensor_copy(moe.table[:, :], L_ps[0:CAP, 0, 0:COLS]))



def differential_attention(t, gain, w_qkv, w_o, lam, subln, lambda_init):
    nc = t.nc
    HEADS = 8
    VD = 2 * HEAD
    QK = HEADS * 2 * HEAD
    SPAN = 2 * T - P
    with ExitStack() as ctx:
        sb = lambda *a: ctx.enter_context(nc.sbuf_tensor(*a))
        S = ctx.enter_context(nc.psum_tensor("a1_S", [P, 4, HALF], F32))
        TB = ctx.enter_context(nc.psum_tensor("a1_T", [P, 2, HALF], F32))
        O = ctx.enter_context(nc.psum_tensor("a1_O", [P, 2, HALF], F32))
        w_sb = sb("a1_w", [P, KD, 3 * P], F32)
        q_parts, k_hi, k_lo = (sb(f"a1_{n}", [P, 2, T], F32R) for n in ("q_parts", "k_hi", "k_lo"))
        v_rows = sb("a1_v_rows", [P, NT, VD], F32)
        probs = sb("a1_probs", [P, 2, 2, T], F32)
        norm = Norm(t, "a1n", gain, sb, S, Combined(t, "a1", t.dram[1], [probs[:, i // 2, i % 2, :] for i in range(4)]))
        mixed = sb("a1_mixed", [P, 2, T], F32)
        mixT = sb("a1_mixT", [P, 2, KD * P], F32)
        bias = sb("a1_bias", [P, SPAN], F32)
        o_rows = sb("a1_o_rows", [P, NT, HEADS, VD], F32)
        square = sb("a1_square", [P, HEADS * VD], F32)
        lam_b = sb("a1_lam", [P, 4, HEAD], F32)
        lam_2 = sb("a1_lam_2", [P, 2, HEAD], F32)
        lam_s = sb("a1_lam_s", [P, 2], F32)
        lam_neg = sb("a1_lam_neg", [P, 1], F32)
        sub_g = sb("a1_sub_g", [P, 1], F32)
        top2, neg2, sum2 = (sb(f"a1_{n}", [P, 2, 2], F32) for n in ("top2", "neg2", "sum2"))
        inv2 = sb("a1_inv2", [P, 4, 2], F32)
        ratio = sb("a1_ratio", [P, 2], F32)
        o_ss, o_rms, o_rstd = (sb(f"a1_{n}", [P, NT, HEADS], F32) for n in ("o_ss", "o_rms", "o_rstd"))
        out_proj = OutProjection(t, "a1o", w_o, None, norm.hnT, S, None)

        w_loaded, lam_loaded = t.sem("a1_w_loaded"), t.sem("a1_lam_loaded")
        proj_done, hi_ready, parts_ready, v_ready = (t.sem(f"a1_{n}") for n in ("proj_done", "hi_ready", "parts_ready", "v_ready"))
        scores, scores_seen, biased = t.sem("a1_scores"), t.sem("a1_scores_seen"), t.sem("a1_biased")
        stats, exp_done, mixed_ready = t.sem("a1_stats"), t.sem("a1_exp_done"), t.sem("a1_mixed_ready")
        m_turned, mixT_ready, pv_done, o_ready = t.sem("a1_m_turned"), t.sem("a1_mixT_ready"), t.sem("a1_pv_done"), t.sem("a1_o_ready")
        dve_own, prep, iota_done = t.sem("a1_dve_own"), t.sem("a1_prep"), t.sem("a1_iota")
        lam_in, lam_out = t.sem("a1_lam_in"), t.sem("a1_lam_out")
        rms_in, rms_out, scaled, o_turned, oT_ready = (t.sem(f"a1_{n}") for n in ("rms_in", "rms_out", "scaled", "o_turned", "oT_ready"))

        with nc.Block() as block:
            @block.sync
            def _(sp):
                norm.sync_load(sp)
                sp.dma_start(lam_b[:, :, :], lam.unsqueeze(0).broadcast_to((P, 4, HEAD))).then_inc(lam_loaded, 16)
                sp.dma_start(sub_g[:, :], subln.unsqueeze(1), allow_slow_non_contiguous=True).then_inc(lam_loaded, 16)

                def load_weights(h):
                    for at, col in ((0, h * P), (P, QK + h * P), (2 * P, 2 * QK + h * P)):
                        sp.dma_start(w_sb[:, :, at:at + P],
                                     w_qkv.rearrange("(p k) n -> p k n", k=KD)[:, :, bass.ds(col, P)])\
                          .then_inc(w_loaded, 16)

                load_weights(0)
                with sp.Fori(1, HEADS) as h:
                    sp.wait_ge(proj_done, 6 * h)
                    load_weights(h)
                sp.wait_ge(proj_done, 6 * HEADS)
                out_proj.sync_load(sp)

            @block.gpsimd
            def _(pool):
                pool.iota(bias[:, :].bitcast(I32), pattern=[[-1, SPAN]], base=T - P, channel_multiplier=1).then_inc(iota_done, 1)
                norm.source.gather(pool)

            @block.scalar
            def _(act):
                norm.scalar(act)
                act.wait_ge(lam_in, 1)
                act.activation(lam_s[:, :], lam_s[:, :], ACT.Exp, bias=t.zero_col[:, :]).then_inc(lam_out, 1)
                with act.Fori(0, HEADS) as h:
                    for o in range(6):
                        act.wait_ge(proj_done, 6 * h + o + 1)
                        j, n = divmod(o, 2)
                        cols = slice(n * HALF, (n + 1) * HALF)
                        if j == 0:
                            for c, part in enumerate(HALVES):
                                last = act.mul(q_parts[part, c, cols], S[part, o % 4, :], Q_SCALE)
                            last.then_inc(hi_ready, 1)
                        elif j == 1:
                            for c, part in enumerate(HALVES):
                                for there in HALVES:
                                    last = act.copy(k_hi[there, c, cols], S[part, o % 4, :])
                            last.then_inc(hi_ready, 1)
                        else:
                            act.copy(v_rows[:, 4 * n:4 * n + 4, :], S[:, o % 4, :].rearrange("p (a b) -> p a b", b=VD))\
                               .then_inc(v_ready, 1)

                    def exponentials(i):
                        n = NT * h + i
                        act.wait_ge(stats, n + 1)
                        for c in range(2):
                            row = probs[:, i % 2, c, :]
                            last = act.activation(row, row, ACT.Exp, bias=neg2[:, i % 2, c:c + 1],
                                                  accum_out=sum2[:, i % 2, c:c + 1])
                        last.then_inc(exp_done, 1)

                    exponentials(0)
                    for i in range(NT):
                        if i + 1 < NT:
                            exponentials(i + 1)
                        n = NT * h + i
                        if i >= 2:
                            act.wait_ge(pv_done, n - 1)
                        for b in range(2):
                            act.wait_ge(m_turned, 2 * n + b + 1)
                            act.copy(mixT[:, i % 2, b * HALF:(b + 1) * HALF], TB[:, b, :]).then_inc(mixT_ready, 1)
                act.wait_ge(rms_in, 1)
                act.activation(o_rms[:, :, :], o_ss[:, :, :], ACT.Sqrt, bias=t.zero_col[:, :]).then_inc(rms_out, 1)
                for tt in range(NT):
                    for b in range(2):
                        act.wait_ge(o_turned, 2 * tt + b + 1)
                        if tt >= 2:
                            act.wait_ge(out_proj.done, 2 * (tt - 1))
                        act.activation(mixT[:, tt % 2, b * HALF:(b + 1) * HALF], TB[:, b, :], ACT.Copy,
                                       scale=sub_g[:, :]).then_inc(oT_ready, 1)

            @block.vector
            def _(dve):
                norm.vector(dve)
                own = Step(dve, prep)
                dve.wait_ge(iota_done, 1)
                wide = mixed[:, :, :].rearrange("p a b -> p (a b)")[:, 0:SPAN]
                own(dve.tensor_copy(wide, bias[:, :].bitcast(I32)))
                own(dve.tensor_scalar(bias[:, :], wide, -1.0, None, ALU.mult))
                own(dve.tensor_tensor(bias[:, :], bias[:, :], wide, ALU.max))
                own(dve.tensor_scalar(bias[:, :], bias[:, :], -2.0 ** (-8.0 / HEADS), None, ALU.mult))
                dve.wait_ge(lam_loaded, 32)
                own(dve.tensor_tensor(lam_2[:, :, :], lam_b[:, 0:4:2, :], lam_b[:, 1:4:2, :], ALU.mult))
                own(dve.tensor_reduce(lam_s[:, :], lam_2[:, :, :], AX, ALU.add))
                own(dve.tensor_scalar(sub_g[:, :], sub_g[:, :], 1.0 - lambda_init, None, ALU.mult))
                dve.tensor_copy(lam_neg[:, :], lam_s[:, 0:1]).then_inc(lam_in, 1)
                dve.wait_ge(lam_out, 1)
                own(dve.tensor_tensor(lam_neg[:, :], lam_s[:, 1:2], lam_s[:, 0:1], ALU.subtract))
                own(dve.tensor_scalar(lam_neg[:, :], lam_neg[:, :], -lambda_init, None, ALU.add))
                prepared = own.n
                OWN = 2 * NT + 1
                with dve.Fori(0, HEADS) as h:
                    own = Step(dve, dve_own, OWN * h)
                    for o in range(4):
                        dve.wait_ge(hi_ready, 4 * h + o + 1)
                        j, n = divmod(o, 2)
                        cols = slice(n * HALF, (n + 1) * HALF)
                        for c, part in enumerate(HALVES):
                            if j == 0:
                                last = dve.scalar_tensor_tensor(out=q_parts[HALVES[1 - c], c, cols], in0=S[part, o, :],
                                                                scalar=Q_SCALE, in1=q_parts[part, c, cols].bitcast(F32),
                                                                op0=ALU.mult, op1=ALU.subtract)
                            else:
                                for there in HALVES:
                                    last = dve.tensor_tensor(k_lo[there, c, cols], S[part, o, :],
                                                             k_hi[part, c, cols].bitcast(F32), ALU.subtract)
                        last.then_inc(parts_ready, 1)

                    def biased_scores(i):
                        n = NT * h + i
                        if i >= 2:
                            dve.wait_ge(mixed_ready, n - 1)
                        for c in range(2):
                            wait_apart(dve, scores, 2 * n + c + 1, scores_seen)
                            at = T - P - i * P
                            dve.tensor_tensor_reduce(probs[:, i % 2, c, :].rearrange("p (a b) -> p a b", a=2),
                                                     S[:, 2 * c:2 * c + 2, :],
                                                     bias[:, at:at + T].rearrange("p (a b) -> p a b", a=2), 1.0, MASKED,
                                                     ALU.add, ALU.max, top2[:, i % 2, c:c + 1]).then_inc(biased, 1)
                        dve.wait_ge(biased, 2 * n + 2)
                        dve.tensor_scalar(neg2[:, i % 2, :], top2[:, i % 2, :], -1.0, None, ALU.mult).then_inc(stats, 1)

                    def mix(i):
                        n = NT * h + i
                        dve.wait_ge(exp_done, n + 1)
                        own(dve.reciprocal(inv2[:, i % 4, :], sum2[:, i % 2, :]))
                        own(dve.scalar_tensor_tensor(out=ratio[:, i % 2:i % 2 + 1], in0=inv2[:, i % 4, 1:2],
                                                     scalar=lam_neg[:, :], in1=sum2[:, i % 2, 0:1],
                                                     op0=ALU.mult, op1=ALU.mult))
                        if i >= 2:
                            dve.wait_ge(m_turned, 2 * (n - 1))
                        dve.scalar_tensor_tensor(out=mixed[:, i % 2, :], in0=probs[:, i % 2, 1, :],
                                                 scalar=ratio[:, i % 2:i % 2 + 1], in1=probs[:, i % 2, 0, :],
                                                 op0=ALU.mult, op1=ALU.add).then_inc(mixed_ready, 1)

                    def head_out(i):
                        dve.wait_ge(pv_done, NT * h + i + 1)
                        dve.tensor_scalar(o_rows[:, i, bass.ds(h, 1), :].rearrange("p a b -> p (a b)"), O[:, i % 2, 0:VD],
                                          inv2[:, i % 4, 0:1], None, ALU.mult).then_inc(o_ready, 1)

                    biased_scores(0)
                    for i in range(NT):
                        if i + 1 < NT:
                            biased_scores(i + 1)
                        if i >= 2:
                            head_out(i - 2)
                        mix(i)
                    head_out(NT - 2)
                    head_out(NT - 1)
                    own(dve.tensor_scalar(bias[:, :], bias[:, :], 2.0 ** (-8.0 / HEADS), None, ALU.mult))
                    assert own.n == OWN
                own = Step(dve, prep, prepared)
                dve.wait_ge(o_ready, NT * HEADS)
                for tt in range(NT):
                    own(dve.tensor_tensor(square[:, :], o_rows[:, tt, :, :].rearrange("p a b -> p (a b)"),
                                          o_rows[:, tt, :, :].rearrange("p a b -> p (a b)"), ALU.mult))
                    own(dve.tensor_reduce(o_ss[:, tt, :], square[:, :].rearrange("p (a b) -> p a b", b=VD), AX, ALU.add))
                dve.tensor_scalar(o_ss[:, :, :], o_ss[:, :, :], 1.0 / VD, SUBLN_EPS, ALU.mult, ALU.add).then_inc(rms_in, 1)
                dve.wait_ge(rms_out, 1)
                own(dve.reciprocal(o_rstd[:, :, :], o_rms[:, :, :]))

                def scale(tt):
                    dve.tensor_tensor(o_rows[:, tt, :, :], o_rows[:, tt, :, :],
                                      o_rstd[:, tt, :].unsqueeze(2).broadcast_to((P, HEADS, VD)), ALU.mult).then_inc(scaled, 1)
                scale(0)
                for tt in range(NT):
                    if tt + 1 < NT:
                        scale(tt + 1)
                    out_proj.vector(dve, tt)

            @block.tensor
            def _(pe):
                norm.tensor(pe)
                with pe.Fori(0, HEADS) as h:
                    pe.wait_ge(w_loaded, 48 * h + 48)
                    for o in range(6):
                        j, n = divmod(o, 2)
                        if o >= 4:
                            pe.wait_ge(parts_ready, 4 * h + o - 3)
                        if j < 2:
                            for k in range(KD):
                                last = pe.matmul(S[:, o % 4, :], w_sb[:, k, j * P:(j + 1) * P],
                                                 norm.hnT[:, k, n * HALF:(n + 1) * HALF], start=(k == 0), stop=(k == KD - 1))
                        else:
                            for a in range(4):
                                tt = 4 * n + a
                                for k in range(KD):
                                    last = pe.matmul(S[:, o % 4, a * P:(a + 1) * P], norm.hnT[:, k, tt * P:(tt + 1) * P],
                                                     w_sb[:, k, 2 * P:3 * P], start=(k == 0), stop=(k == KD - 1))
                        last.then_inc(proj_done, 1)
                    pe.wait_ge(parts_ready, 4 * h + 4)
                    pe.wait_ge(v_ready, 2 * h + 2)

                    def head_scores(i):
                        n = NT * h + i
                        for c in range(2):
                            if i >= 1:
                                pe.wait_ge(biased, 2 * (n - 1) + c + 1)
                            for b in range(2):
                                for k_part in (k_hi, k_lo):
                                    last = pe.matmul(S[:, 2 * c + b, :], q_parts[:, c, i * P:(i + 1) * P],
                                                     k_part[:, c, b * HALF:(b + 1) * HALF],
                                                     start=(k_part is k_hi), stop=(k_part is k_lo))
                            last.then_inc(scores, 1)

                    def product(i):
                        n = NT * h + i
                        pe.wait_ge(mixed_ready, n + 1)
                        for b in range(2):
                            if i >= 1:
                                pe.wait_ge(mixT_ready, 2 * (n - 1) + b + 1)
                            for a in range(4):
                                k = 4 * b + a
                                last = pe.transpose(TB[:, b, a * P:(a + 1) * P], mixed[:, i % 2, k * P:(k + 1) * P],
                                                    t.ident[:, :])
                            last.then_inc(m_turned, 1)
                        if i >= 2:
                            pe.wait_ge(o_ready, n - 1)
                        for k in range(KD):
                            if k % 4 == 0:
                                pe.wait_ge(mixT_ready, 2 * n + k // 4 + 1)
                            last = pe.matmul(O[:, i % 2, 0:VD], mixT[:, i % 2, k * P:(k + 1) * P], v_rows[:, k, :],
                                             start=(k == 0), stop=(k == KD - 1))
                        last.then_inc(pv_done, 1)

                    head_scores(0)
                    head_scores(1)
                    for i in range(NT):
                        if i + 2 < NT:
                            head_scores(i + 2)
                        product(i)
                pe.wait_ge(out_proj.loaded, 16)
                for tt in range(NT):
                    pe.wait_ge(scaled, tt + 1)
                    for b in range(2):
                        if tt >= 1:
                            pe.wait_ge(oT_ready, 2 * (tt - 1) + b + 1)
                        for a in range(4):
                            last = pe.transpose(TB[:, b, a * P:(a + 1) * P], o_rows[:, tt, 4 * b + a, :], t.ident[:, :])
                        last.then_inc(o_turned, 1)
                    pe.wait_ge(oT_ready, 2 * tt + 2)
                    out_proj.tensor(pe, tt, mixT[:, tt % 2, :].rearrange("p (k n) -> p k n", k=KD))


def final_norm(t, gain, out):
    nc = t.nc
    BUFS = 8
    with ExitStack() as ctx:
        sb = lambda *a: ctx.enter_context(nc.sbuf_tensor(*a))
        back = sb("f_back", [P, BUFS, D], F32)
        source = Combined(t, "f", t.dram[1], [back[:, i, :] for i in range(BUFS)])
        gain_b, junk = sb("f_gain", [P, D], F32), sb("f_junk", [P, D], F32)
        rows = sb("f_rows", [P, NT, D], F32)
        ssq, rms, rstd = sb("f_ssq", [P, NT], F32), sb("f_rms", [P, NT], F32), sb("f_rstd", [P, NT], F32)
        gain_loaded, squared, rms_ready, chain, ready, stored = (
            t.sem(f"f_{n}") for n in ("gain_loaded", "squared", "rms_ready", "chain", "ready", "stored"))
        with nc.Block() as block:
            @block.sync
            def _(sp):
                sp.dma_start(gain_b[:, :], gain.broadcast_to((P, D))).then_inc(gain_loaded, 16)
                for tt in range(NT):
                    sp.wait_ge(ready, tt + 1)
                    sp.dma_start(out[0, tt * P:(tt + 1) * P, :], rows[:, tt, :]).then_inc(stored, 16)
                sp.wait_ge(stored, 16 * NT)

            @block.gpsimd
            def _(pool):
                source.gather(pool)

            @block.scalar
            def _(act):
                for tt in range(NT):
                    source.complete(act, tt)
                    if tt:
                        act.wait_ge(squared, tt)
                    act.activation(junk[:, :], t.x[:, tt, :], ACT.Square, bias=t.zero_col[:, :],
                                   accum_out=ssq[:, tt:tt + 1]).then_inc(squared, 1)
                    act.wait_ge(squared, tt + 1)
                    act.activation(rms[:, tt:tt + 1], ssq[:, tt:tt + 1], ACT.Sqrt, bias=t.eps_col[:, :],
                                   scale=1.0 / D).then_inc(rms_ready, 1)

            @block.vector
            def _(dve):
                source.add(dve, 0)
                for tt in range(NT):
                    if tt + 1 < NT:
                        source.add(dve, tt + 1)
                    dve.wait_ge(rms_ready, tt + 1)
                    dve.reciprocal(rstd[:, tt:tt + 1], rms[:, tt:tt + 1]).then_inc(chain, 1)
                    if tt == 0:
                        dve.wait_ge(gain_loaded, 16)
                    dve.wait_ge(chain, tt + 1)
                    dve.scalar_tensor_tensor(out=rows[:, tt, :], in0=t.x[:, tt, :], scalar=rstd[:, tt:tt + 1],
                                             in1=gain_b[:, :], op0=ALU.mult, op1=ALU.mult).then_inc(ready, 1)


class Experts:

    def __init__(self, t, name, w_gate, w_up, w_down, dram, ctx):
        nc = t.nc
        sb = lambda *a: ctx.enter_context(nc.sbuf_tensor(*a))
        self.t, self.name = t, name
        self.weights = (w_gate, w_up, w_down)
        self.hn_rows, self.out_rows = dram
        self.raw = [sb(f"{name}_raw_{w}", [P, KD * HIDDEN], F32) for w in ("gate", "up", "down")]
        self.table = sb(f"{name}_table", [CAP, COLS], I32)
        self.control = sb(f"{name}_control", [1, COLS + 1], I32)
        s = lambda what: t.sem(f"{name}_{what}")
        names = ("gate", "up", "down")
        self.raw_loaded, self.hi_done, self.lo_done = ([s(f"{w}_{n}") for w in names] for n in ("loaded", "hi_done", "lo_done"))
        self.hi, self.lo = ([sb(f"{name}_{n}_{w}", [P, KD * HIDDEN], F32R) for w in names[:2]] for n in ("hi", "lo"))

    def load(self, sp, w, expert):
        k = KH if w == 2 else KD
        sp.dma_start(self.raw[w][:, :], self.weights[w][expert].rearrange("(p k) n -> p (k n)", k=k)
                     if isinstance(expert, int) else
                     self.weights[w][bass.ds(expert, 1)].rearrange("e (p k) n -> p (e k n)", k=k))\
          .then_inc(self.raw_loaded[w], 16)

    def high_part(self, act, w, piece):
        cut = slice(piece * PIECE, (piece + 1) * PIECE)
        act.copy(self.hi[w][:, cut], self.raw[w][:, cut]).then_inc(self.hi_done[w], 1)

    def low_part(self, eng, w, b, piece):
        eng.wait_ge(self.hi_done[w], 2 * b + piece + 1)
        cut = slice(piece * PIECE, (piece + 1) * PIECE)
        eng.tensor_tensor(self.lo[w][:, cut], self.raw[w][:, cut], self.hi[w][:, cut].bitcast(F32), ALU.subtract)\
           .then_inc(self.lo_done[w], 1)

    def run(self):
        t, nc, name = self.t, self.t.nc, self.name
        with ExitStack() as ctx:
            sb = lambda *a: ctx.enter_context(nc.sbuf_tensor(*a))
            ps = lambda *a: ctx.enter_context(nc.psum_tensor(*a))
            self.hi.append(sb(f"{name}_hi_down", [P, KH * D], F32R))
            self.lo.append(sb(f"{name}_lo_down", [P, KH * D], F32R))
            hi, lo, hi_done, lo_done = self.hi, self.lo, self.hi_done, self.lo_done
            pick = sb(f"{name}_pick", [CAP, 1], I32)
            xg = sb(f"{name}_xg", [CAP, D], F32)
            x_hi, x_lo = sb(f"{name}_x_hi", [P, KD * CAP], F32R), sb(f"{name}_x_lo", [P, KD * CAP], F32R)
            gated = sb(f"{name}_gated", [CAP, HIDDEN], F32)
            hid = sb(f"{name}_hid", [CAP, HIDDEN], F32)
            h_hi, h_lo = sb(f"{name}_h_hi", [P, KH * CAP], F32R), sb(f"{name}_h_lo", [P, KH * CAP], F32R)
            y = sb(f"{name}_y", [CAP, D], F32)
            G, U, HT = ps(f"{name}_G", [P, HALF], F32), ps(f"{name}_U", [P, HALF], F32), ps(f"{name}_HT", [P, HALF], F32)
            Y, XT = ps(f"{name}_Y", [P, 2, HALF], F32), ps(f"{name}_XT", [P, 2, HALF], F32)
            s = lambda what: t.sem(f"{name}_{what}")
            gate_done, up_done, down_done = s("gate_done"), s("up_done"), s("down_done")
            picked, gathered, x_turned, x_hi_done, x_lo_done = s("picked"), s("gathered"), s("x_turned"), s("x_hi"), s("x_lo")
            gated_done, hid_done, h_turned, h_hi_done, h_lo_done = s("gated"), s("hid"), s("h_turned"), s("h_hi"), s("h_lo")
            pick_seen = s("pick_seen")
            y_act, y_dve, y_stored = s("y_act"), s("y_dve"), s("y_stored")

            def steady_blocks(eng):
                return eng.value_load(self.control[0:1, 0:1], min_val=EXPERTS - 3, max_val=ROWS - 3)

            def in_turn(eng, step):
                last = steady_blocks(eng) + 2
                step(0, True, False)
                step(1, False, False)
                with eng.Fori(2, last) as b:
                    step(b, False, False)
                step(last, False, True)
                return last

            with nc.Block() as block:
                @block.sync
                def _(sp):
                    def load(w, b, expert):
                        sp.wait_ge(hi_done[w], 2 * b)
                        sp.wait_ge(lo_done[w], 2 * b)
                        self.load(sp, w, expert)

                    def expert_of(b):
                        return sp.value_load(self.control[0:1, bass.ds(b + 1, 1)], min_val=0, max_val=EXPERTS - 1)

                    last = steady_blocks(sp) + 2
                    with sp.Fori(1, last) as b:
                        following, expert = expert_of(b + 1), expert_of(b)
                        for w in range(2):
                            load(w, b + 1, following)
                        load(2, b, expert)
                    load(2, last, expert_of(last))

                @block.gpsimd
                def _(pool):
                    def gather(b, first):
                        if not first:
                            pool.wait_ge(x_turned, b)
                        pool.tensor_copy(pick[:, :], self.table[:, b:b + 1] if first else self.table[:, bass.ds(b, 1)])\
                            .then_inc(picked, 1)
                        wait_apart(pool, picked, b + 1, pick_seen)
                        pool.indirect_dma_start(out=xg[:, :], out_offset=None, in_=self.hn_rows,
                                                in_offset=bass.IndirectOffsetOnAxis(pick[:, :], 0)).then_inc(gathered, 16)

                    def store(b):
                        pool.wait_ge(y_act, b + 1)
                        pool.wait_ge(y_dve, b + 1)
                        rows = self.out_rows.rearrange("(r c) n -> r c n", c=CAP)
                        pool.dma_start(rows[b] if isinstance(b, int) else rows[bass.ds(b, 1)].rearrange("r c n -> (r c) n"),
                                       y[:, :]).then_inc(y_stored, 16)

                    def step(b, first, last):
                        if not last:
                            gather(b + 1, False)
                        if not first:
                            store(b - 1)
                    gather(0, True)
                    last = in_turn(pool, step)
                    store(last)
                    pool.wait_ge(y_stored, 16 * (last + 1))

                def times(pe, out, left, right, K, n, N):
                    (l_hi, l_lo), (r_hi, r_lo) = left, right
                    for k in range(K):
                        rows = slice(k * CAP, (k + 1) * CAP)
                        cols = slice(k * N + n * HALF, k * N + (n + 1) * HALF)
                        pe.matmul(out, l_hi[:, rows], r_hi[:, cols], start=(k == 0), stop=False)
                        pe.matmul(out, l_lo[:, rows], r_hi[:, cols], start=False, stop=False)
                        last = pe.matmul(out, l_hi[:, rows], r_lo[:, cols], start=False, stop=(k == K - 1))
                    return last

                @block.tensor
                def _(pe):
                    def turn_x(b):
                        pe.wait_ge(gathered, 16 * (b + 1))
                        wait_count(pe, x_lo_done, 2 * b)
                        for half in range(2):
                            for k in range(4):
                                kk = 4 * half + k
                                last = pe.transpose(XT[:, half, k * CAP:(k + 1) * CAP], xg[:, kk * P:(kk + 1) * P],
                                                    t.ident[0:CAP, 0:CAP])
                        last.then_inc(x_turned, 1)

                    def turn_h(b):
                        pe.wait_ge(hid_done, b + 1)
                        wait_count(pe, h_lo_done, b)
                        for k in range(KH):
                            last = pe.transpose(HT[:, k * CAP:(k + 1) * CAP], hid[:, k * P:(k + 1) * P],
                                                t.ident[0:CAP, 0:CAP])
                        last.then_inc(h_turned, 1)

                    def down(b):
                        pe.wait_ge(h_lo_done, b + 1)
                        pe.wait_ge(lo_done[2], 2 * b + 2)
                        wait_count(pe, y_act, b)
                        wait_count(pe, y_dve, b)
                        for n in range(2):
                            times(pe, Y[0:CAP, n, :], (h_hi, h_lo), (hi[2], lo[2]), KH, n, D).then_inc(down_done, 1)

                    def step(b, first, last):
                        pe.wait_ge(x_lo_done, 2 * b + 2)
                        pe.wait_ge(lo_done[0], 2 * b + 2)
                        if not first:
                            pe.wait_ge(gated_done, b)
                        times(pe, G[0:CAP, :], (x_hi, x_lo), (hi[0], lo[0]), KD, 0, HIDDEN).then_inc(gate_done, 1)
                        if not first:
                            turn_h(b - 1)
                        pe.wait_ge(lo_done[1], 2 * b + 2)
                        if not first:
                            pe.wait_ge(hid_done, b)
                        times(pe, U[0:CAP, :], (x_hi, x_lo), (hi[1], lo[1]), KD, 0, HIDDEN).then_inc(up_done, 1)
                        if not last:
                            turn_x(b + 1)
                        if not first:
                            down(b - 1)
                    turn_x(0)
                    last = in_turn(pe, step)
                    turn_h(last)
                    down(last)

                @block.scalar
                def _(act):
                    def split(w, b, piece):
                        if piece == 0:
                            act.wait_ge(self.raw_loaded[w], 16 * (b + 1))
                            wait_count(act, *((gate_done, b), (up_done, b), (down_done, 2 * b))[w])
                        self.high_part(act, w, piece)

                    def x_part(b):
                        act.wait_ge(x_turned, b + 1)
                        for half in range(2):
                            act.copy(x_hi[:, half * 4 * CAP:(half + 1) * 4 * CAP], XT[:, half, 0:4 * CAP]).then_inc(x_hi_done, 1)

                    def step(b, first, last):
                        act.wait_ge(gate_done, b + 1)
                        wait_count(act, hid_done, b)
                        act.activation(gated[:, :], G[0:CAP, :], ACT.Silu, bias=t.zero_col[0:CAP, :]).then_inc(gated_done, 1)
                        if not first:
                            act.wait_ge(h_turned, b)
                            act.copy(h_hi[:, :], HT[:, 0:KH * CAP]).then_inc(h_hi_done, 1)
                        if not last:
                            split(0, b + 1, 0)
                            split(0, b + 1, 1)
                            x_part(b + 1)
                            split(1, b + 1, 0)
                            split(1, b + 1, 1)
                        if not first:
                            act.wait_ge(down_done, 2 * b - 1)
                            wait_count(act, y_stored, 16 * (b - 1))
                            act.copy(y[:, 0:HALF], Y[0:CAP, 0, :]).then_inc(y_act, 1)
                        split(2, b, 0)
                        split(2, b, 1)

                    x_part(0)
                    last = in_turn(act, step)
                    act.wait_ge(h_turned, last + 1)
                    act.copy(h_hi[:, :], HT[:, 0:KH * CAP]).then_inc(h_hi_done, 1)
                    act.wait_ge(down_done, 2 * last + 1)
                    act.wait_ge(y_stored, 16 * last)
                    act.copy(y[:, 0:HALF], Y[0:CAP, 0, :]).then_inc(y_act, 1)

                @block.vector
                def _(dve):
                    def split(w, b, piece):
                        self.low_part(dve, w, b, piece)

                    def x_part(b):
                        for half in range(2):
                            dve.wait_ge(x_hi_done, 2 * b + half + 1)
                            cut = slice(half * 4 * CAP, (half + 1) * 4 * CAP)
                            dve.tensor_tensor(x_lo[:, cut], XT[:, half, 0:4 * CAP], x_hi[:, cut].bitcast(F32), ALU.subtract)\
                               .then_inc(x_lo_done, 1)

                    def h_part(b):
                        dve.wait_ge(h_hi_done, b + 1)
                        dve.tensor_tensor(h_lo[:, :], HT[:, 0:KH * CAP], h_hi[:, :].bitcast(F32), ALU.subtract)\
                           .then_inc(h_lo_done, 1)

                    def y_part(b):
                        dve.wait_ge(down_done, 2 * b + 2)
                        wait_count(dve, y_stored, 16 * b)
                        dve.tensor_copy(y[:, HALF:D], Y[0:CAP, 1, :]).then_inc(y_dve, 1)

                    def step(b, first, last):
                        if not first:
                            h_part(b - 1)
                        if not last:
                            split(0, b + 1, 0)
                            split(0, b + 1, 1)
                        dve.wait_ge(up_done, b + 1)
                        dve.tensor_tensor(hid[:, :].rearrange("q (k p) -> q p k", k=KH), gated[:, :]
                                          .rearrange("q (p k) -> q p k", k=KH), U[0:CAP, :]
                                          .rearrange("q (p k) -> q p k", k=KH), ALU.mult).then_inc(hid_done, 1)
                        if not last:
                            x_part(b + 1)
                            split(1, b + 1, 0)
                            split(1, b + 1, 1)
                        if not first:
                            y_part(b - 1)
                        split(2, b, 0)
                        split(2, b, 1)

                    x_part(0)
                    last = in_turn(dve, step)
                    h_part(last)
                    y_part(last)



def mixture(t, name, args, layer):
    with ExitStack() as ctx:
        moe = Experts(t, name, args["moe_w_gate"][layer], args["moe_w_up"][layer], args["moe_w_down"][layer],
                      t.dram, ctx)
        route(t, f"{name}r", args["norm_ffn"][layer:layer + 1, :], args["moe_w_group"][layer],
              args["moe_b_group"][layer], args["moe_w_router"][layer], args["moe_b_router"][layer], moe)
        moe.run()


def program(nc, args, out, stages=99):
    with ExitStack() as stack:
        t = Trunk(nc, stack)
        dram = lambda n, shape, dt: nc.dram_tensor(n, shape, dt, kind="Internal").ap()
        t.dram = (dram("hn_rows", (T, D), F32), dram("out_rows", (ROWS * CAP, D), F32))
        setup(t, args["x"])
        if stages >= 1:
            windowed_attention(t, args["norm_mix"][0:1, :], args["swa_w_qkv"][0], args["swa_w_o"][0],
                               args["swa_sink"][0:1, :])
        if stages >= 2:
            mixture(t, "m0", args, 0)
            t.clear_semaphores()
        if stages >= 3:
            differential_attention(t, args["norm_mix"][1:2, :], args["diff_w_qkv"][0], args["diff_w_o"][0],
                                   args["diff_lambda"][0], args["diff_subln"][0], 0.8 - 0.6 * math.exp(-0.3))
        if stages >= 4:
            mixture(t, "m1", args, 1)
        if stages >= 5:
            return final_norm(t, args["final_norm"].unsqueeze(0), out)
        stored = t.sem("out_stored")
        with nc.Block() as block:
            @block.sync
            def _(sp):
                for tt in range(NT):
                    sp.dma_start(out[0, tt * P:(tt + 1) * P, :], t.x[:, tt, :]).then_inc(stored, 16)
                sp.wait_ge(stored, 16 * NT)


_INS = ("x", "norm_mix", "norm_ffn", "swa_w_qkv", "swa_w_o", "swa_sink", "diff_w_qkv", "diff_w_o", "diff_lambda",
        "diff_subln", "moe_w_group", "moe_b_group", "moe_w_router", "moe_b_router", "moe_w_gate", "moe_w_up",
        "moe_w_down", "final_norm")


def kernel(**inputs):
    import numpy as np
    import concourse.bacc as bacc
    from concourse.bass_utils import run_bass_kernel_spmd

    nc = bacc.Bacc("TRN2", target_bir_lowering=False, num_devices=1)
    arrays, args = {}, {}
    for name in _INS:
        a = np.ascontiguousarray(inputs[name])
        arrays[f"in_{name}_dram"] = a
        args[name] = nc.dram_tensor(f"in_{name}_dram", a.shape, mybir.dt.from_np(a.dtype), kind="ExternalInput").ap()
    out = nc.dram_tensor("out_0_dram", (1, T, D), F32, kind="ExternalOutput").ap()
    program(nc, args, out)
    r = run_bass_kernel_spmd(nc, [arrays], core_ids=[0])
    return r.results[0]["out_0_dram"]
```

```python
import math
from contextlib import ExitStack

import concourse.bass as bass
from concourse import mybir

F32 = mybir.dt.float32
F32R = mybir.dt.float32r
I32 = mybir.dt.int32
ALU = mybir.AluOpType
ACT = mybir.ActivationFunctionType
AX = mybir.AxisListType.X

P = 128
T = 1024
D = 1024
NT = T // P
KD = D // P
HALF = 512
HEAD = 64
Q_SCALE = HEAD ** -0.5
NORM_EPS = 1e-6
SUBLN_EPS = 1e-5
MASKED = -1e30
HALVES = (slice(0, 64), slice(64, 128))

GROUPS = 4
PER_GROUP = 8
EXPERTS = GROUPS * PER_GROUP
HIDDEN = 512
KH = HIDDEN // P
TOP_K = 2
CAP = 96
SPARE = T * TOP_K // CAP
ROWS = EXPERTS + SPARE
COLS = ROWS + 2
STEPS = T // CAP
PIECE = KD * HIDDEN // 2


class Step:

    def __init__(self, eng, sem, base=0):
        self.eng, self.sem, self.base, self.n = eng, sem, base, 0

    def __call__(self, instruction):
        self.n += 1
        instruction.then_inc(self.sem, 1)
        self.eng.wait_ge(self.sem, self.base + self.n)


def wait_count(eng, sem, count):
    if not (isinstance(count, int) and count == 0):
        eng.wait_ge(sem, count)


def wait_apart(eng, sem, count, passed):
    eng.wait_ge(sem, count)
    eng.sem_inc(passed, 1)


class Trunk:
    def __init__(self, nc, stack):
        self.nc, self.stack, self.used = nc, stack, []

    def sem(self, name):
        handle = self.nc.alloc_semaphore(name=name)
        self.used.append(handle)
        return handle

    def clear_semaphores(self):
        numbers = sorted(h.num for h in self.used)
        spans = []
        for n in numbers:
            if spans and spans[-1][1] == n:
                spans[-1][1] = n + 1
            else:
                spans.append([n, n + 1])
        with self.nc.Block() as block:
            @block.gpsimd
            def _(pool):
                for a, b in spans:
                    pool.sem_clear(range(a, b))
        for h in self.used:
            self.nc.release_semaphore(h)
        self.used = []


def setup(t):
    nc = t.nc
    keep = t.stack.enter_context
    t.x = keep(nc.sbuf_tensor("x_res", [P, NT, D], F32))
    t.ident = keep(nc.sbuf_tensor("ident", [P, P], F32))
    t.zero_col = keep(nc.sbuf_tensor("zero_col", [P, 1], F32))
    t.eps_col = keep(nc.sbuf_tensor("eps_col", [P, 1], F32))
    t.weight = keep(nc.sbuf_tensor("choice_weight", [P, 2, NT], F32))
    t.out_slot = keep(nc.sbuf_tensor("choice_slot", [P, 2 * NT], I32))
    made = t.sem("const_made")
    with nc.Block() as block:
        @block.gpsimd
        def _(pool):
            pool.memset(t.ident[:, :], 0.0).then_inc(made, 1)
            pool.memset(t.zero_col[:, :], 0.0)
            pool.memset(t.eps_col[:, :], NORM_EPS)
            pool.wait_ge(made, 1)
            pool.affine_select(out=t.ident[:, :], in_=t.ident[:, :], compare_op=ALU.not_equal, fill=1.0,
                               base=0, pattern=[[-1, P]], channel_multiplier=1).then_inc(made, 1)


class Resident:

    def complete(self, eng, tt):
        pass

    def add(self, dve, tt):
        pass


class Loaded(Resident):

    def __init__(self, t, x_rows):
        self.t, self.x_rows = t, x_rows
        self.loaded = [t.sem(f"x_loaded_{i}") for i in range(NT // 2)]

    def load(self, sp):
        for i, loaded in enumerate(self.loaded):
            sp.dma_start(self.t.x[:, 2 * i:2 * i + 2, :], self.x_rows[2 * i * P:2 * (i + 1) * P, :]
                         .rearrange("(a p) n -> p a n", p=P)).then_inc(loaded, 16)

    def complete(self, eng, tt):
        eng.wait_ge(self.loaded[tt // 2], 16)


class Combined:

    def __init__(self, t, name, out_rows, buffers):
        self.t, self.out_rows, self.buffers = t, out_rows, buffers
        self.gathered = [t.sem(f"{name}_back_{i}") for i in range(len(buffers))]
        self.added = t.sem(f"{name}_added")

    def gather(self, pool):
        bufs = len(self.buffers)
        for m in range(2 * NT):
            tt, c = divmod(m, 2)
            if m >= bufs:
                pool.wait_ge(self.added, m - bufs + 1)
            pool.indirect_dma_start(out=self.buffers[m % bufs], out_offset=None, in_=self.out_rows,
                                    in_offset=bass.IndirectOffsetOnAxis(self.t.out_slot[:, c * NT + tt:c * NT + tt + 1], 0))\
                .then_inc(self.gathered[m % bufs], 16)

    def add(self, dve, tt):
        bufs = len(self.buffers)
        for c in range(TOP_K):
            m = 2 * tt + c
            dve.wait_ge(self.gathered[m % bufs], 16 * (m // bufs + 1))
            if c:
                dve.wait_ge(self.added, m)
            dve.scalar_tensor_tensor(out=self.t.x[:, tt, :], in0=self.buffers[m % bufs],
                                     scalar=self.t.weight[:, c, tt:tt + 1], in1=self.t.x[:, tt, :],
                                     op0=ALU.mult, op1=ALU.add).then_inc(self.added, 1)

    def complete(self, eng, tt):
        eng.wait_ge(self.added, 2 * (tt + 1))


class Norm:

    def __init__(self, t, name, gain, sb, banks, source, tiles_T=0, rows_dram=None, bufs=2):
        self.t, self.gain, self.banks, self.source, self.rows_dram = t, gain, banks, source, rows_dram
        self.tiles_T, self.bufs = tiles_T, bufs
        self.gain_b = sb(f"{name}_gain", [P, D], F32)
        self.scratch = sb(f"{name}_rows", [P, 1 + bufs, D], F32)
        self.junk, self.hn = self.scratch[:, 0, :], self.scratch[:, 1:1 + bufs, :]
        self.ssq = sb(f"{name}_ssq", [P, NT], F32)
        self.rms = sb(f"{name}_rms", [P, NT], F32)
        self.rstd = sb(f"{name}_rstd", [P, NT], F32)
        if tiles_T:
            self.hnT = sb(f"{name}_hnT", [P, KD, tiles_T * P], F32)
        else:
            self.hi, self.lo = sb(f"{name}_hi", [P, KD, T], F32R), sb(f"{name}_lo", [P, KD, T], F32R)
        s = lambda what: t.sem(f"{name}_{what}")
        self.gain_loaded, self.squared, self.rms_ready, self.chain = s("gain_loaded"), s("squared"), s("rms_ready"), s("chain")
        self.hn_ready, self.turned, self.copied, self.used = s("hn_ready"), s("turned"), s("copied"), s("used")
        self.banks_read = self.copied if tiles_T else s("banks_read")
        self.rows_stored = [s(f"rows_stored_{i}") for i in range(bufs)] if rows_dram is not None else []

    def tile_T(self, tt):
        at = tt % self.tiles_T
        return self.hnT[:, :, at * P:(at + 1) * P]

    def turned_tile(self, tt):
        return self.banks[:, 2 * (tt % 2):2 * (tt % 2) + 2, :].rearrange("p b (k n) -> p (b k) n", k=4)

    def low_part(self, dve, tt):
        dve.wait_ge(self.copied, tt + 1)
        cols = slice(tt * P, (tt + 1) * P)
        dve.tensor_tensor(self.lo[:, :, cols], self.turned_tile(tt), self.hi[:, :, cols].bitcast(F32), ALU.subtract)\
           .then_inc(self.banks_read, 1)

    def sync_free(self, sp):
        sp.wait_ge(self.squared, NT)
        sp.wait_ge(self.turned, NT)

    def sync_load(self, sp):
        sp.dma_start(self.gain_b[:, :], self.gain.broadcast_to((P, D))).then_inc(self.gain_loaded, 16)

    def sync_store(self, sp):
        for tt in range(NT):
            sp.wait_ge(self.hn_ready, tt + 1)
            sp.dma_start(self.rows_dram[tt * P:(tt + 1) * P, :], self.hn[:, tt % self.bufs, :])\
              .then_inc(self.rows_stored[tt % self.bufs], 16)

    def sync_stored(self, sp):
        for stored in self.rows_stored:
            sp.wait_ge(stored, 16 * NT // self.bufs)

    def scalar(self, act, meanwhile=()):
        for tt in range(NT + 2):
            if tt < NT:
                self.source.complete(act, tt)
                if tt:
                    act.wait_ge(self.squared, tt)
                act.activation(self.junk, self.t.x[:, tt, :], ACT.Square, bias=self.t.zero_col[:, :],
                               accum_out=self.ssq[:, tt:tt + 1]).then_inc(self.squared, 1)
                act.wait_ge(self.squared, tt + 1)
                act.activation(self.rms[:, tt:tt + 1], self.ssq[:, tt:tt + 1], ACT.Sqrt, bias=self.t.eps_col[:, :],
                               scale=1.0 / D).then_inc(self.rms_ready, 1)
            if 0 <= tt - NT // 2 - 1 < len(meanwhile):
                meanwhile[tt - NT // 2 - 1]()
            if tt >= 2:
                done = tt - 2
                act.wait_ge(self.turned, done + 1)
                if self.tiles_T and done >= self.tiles_T:
                    act.wait_ge(self.used, done - self.tiles_T + 1)
                act.copy(self.tile_T(done) if self.tiles_T else self.hi[:, :, done * P:(done + 1) * P],
                         self.turned_tile(done)).then_inc(self.copied, 1)

    def vector(self, dve, meanwhile=()):
        self.source.add(dve, 0)
        for tt in range(NT):
            if tt + 1 < NT:
                self.source.add(dve, tt + 1)
            dve.wait_ge(self.rms_ready, tt + 1)
            dve.reciprocal(self.rstd[:, tt:tt + 1], self.rms[:, tt:tt + 1]).then_inc(self.chain, 1)
            if tt == 0:
                dve.wait_ge(self.gain_loaded, 16)
            else:
                if tt >= self.bufs:
                    dve.wait_ge(self.turned, tt - self.bufs + 1)
                    if self.rows_dram is not None:
                        dve.wait_ge(self.rows_stored[tt % self.bufs], 16 * (tt // self.bufs))
            dve.wait_ge(self.chain, tt + 1)
            dve.scalar_tensor_tensor(
                out=self.hn[:, tt % self.bufs, :].rearrange("q (k p) -> q p k", k=KD),
                in0=self.t.x[:, tt, :].rearrange("q (p k) -> q p k", k=KD), scalar=self.rstd[:, tt:tt + 1],
                in1=self.gain_b[:, :].rearrange("q (p k) -> q p k", k=KD), op0=ALU.mult, op1=ALU.mult)\
               .then_inc(self.hn_ready, 1)
            if not self.tiles_T and tt >= 2:
                self.low_part(dve, tt - 2)
            if 0 < tt - NT // 2 <= len(meanwhile):
                meanwhile[tt - NT // 2 - 1]()
        if not self.tiles_T:
            self.low_part(dve, NT - 2)
            self.low_part(dve, NT - 1)

    def turn(self, pe, tt):
        pe.wait_ge(self.hn_ready, tt + 1)
        if tt >= 2:
            pe.wait_ge(self.banks_read, tt - 1)
        for k in range(KD):
            last = pe.transpose(self.banks[:, 2 * (tt % 2) + k // 4, k % 4 * P:(k % 4 + 1) * P],
                                self.hn[:, tt % self.bufs, k * P:(k + 1) * P], self.t.ident[:, :])
        last.then_inc(self.turned, 1)


def three_passes(pe, out, left, right, first, last):
    pe.matmul(out, left[0], right[0], start=first, stop=False)
    pe.matmul(out, left[1], right[0], start=False, stop=False)
    return pe.matmul(out, left[0], right[1], start=False, stop=last)


class Projections:
    COLS = 3 * P

    def __init__(self, t, name, w_qkv, columns, norm, first_raw, sb, order):
        self.order, self.used_at = order, [order.index((j, 1)) + 1 for j in range(3)]
        self.w_qkv, self.columns, self.norm = w_qkv.rearrange("(p k) n -> p k n", k=KD), columns, norm
        shaped = lambda a: a.rearrange("p (k n) -> p k n", n=self.COLS)
        self.first_raw, self.raw = shaped(first_raw), shaped(norm.scratch[:, :, :].rearrange("p a b -> p (a b)"))
        self.hi, self.lo = (sb(f"{name}_{n}", [P, KD, self.COLS], F32R) for n in ("w_hi", "w_lo"))
        self.loaded, self.hi_done, self.lo_done, self.done = (t.sem(f"{name}_w_{n}") for n in ("loaded", "hi", "lo", "used"))

    def load(self, sp, step):
        raw = self.first_raw if isinstance(step, int) and step == 0 else self.raw
        at = 0
        for column, n in self.columns(step):
            sp.dma_start(raw[:, :, at:at + n], self.w_qkv[:, :, bass.ds(column, n)]).then_inc(self.loaded, 16)
            at += n

    def sync(self, sp, steps):
        self.norm.sync_free(sp)
        with sp.Fori(1, steps) as step:
            sp.wait_ge(self.lo_done, 3 * step)
            self.load(sp, step)

    def high_part(self, act, step, j):
        first = isinstance(step, int) and step == 0
        if j == 0:
            act.wait_ge(self.loaded, 48 * step + 48)
        if not first:
            act.wait_ge(self.done, 6 * step - 6 + self.used_at[j])
        raw, cols = self.first_raw if first else self.raw, slice(j * P, (j + 1) * P)
        act.copy(self.hi[:, :, cols], raw[:, :, cols]).then_inc(self.hi_done, 1)

    def low_part(self, dve, step, j):
        first = isinstance(step, int) and step == 0
        dve.wait_ge(self.hi_done, 3 * step + j + 1)
        raw, cols = self.first_raw if first else self.raw, slice(j * P, (j + 1) * P)
        dve.tensor_tensor(self.lo[:, :, cols], raw[:, :, cols], self.hi[:, :, cols].bitcast(F32), ALU.subtract)\
           .then_inc(self.lo_done, 1)

    def tensor(self, pe, out, step, o, first):
        j, n = self.order[o]
        if first and o == 0:
            for tt in range(NT - 2):
                self.norm.turn(pe, tt)
        if first and o == 1:
            self.norm.turn(pe, NT - 2)
            self.norm.turn(pe, NT - 1)
        if first and (o == 0 or (n == 1 and self.order[o - 1][1] == 0 and o < 4)):
            pe.wait_ge(self.norm.banks_read, (n + 1) * NT // 2)
        if n == 0:
            pe.wait_ge(self.lo_done, 3 * step + j + 1)
        cols, rows = slice(j * P, (j + 1) * P), slice(n * HALF, (n + 1) * HALF)
        for k in range(KD):
            last = three_passes(pe, out, (self.hi[:, k, cols], self.lo[:, k, cols]),
                                (self.norm.hi[:, k, rows], self.norm.lo[:, k, rows]), k == 0, k == KD - 1)
        last.then_inc(self.done, 1)


class OutProjection:

    def __init__(self, t, name, w_o, x_rows, projections, steps, banks):
        self.t, self.w_o, self.x_rows, self.banks = t, w_o, x_rows, banks
        self.projections, self.norm, self.steps = projections, projections.norm, steps
        self.w_hi, self.w_lo = self.norm.hi, self.norm.lo
        self.o_hi, self.o_lo = (a[:, :, :].rearrange("p a b -> p (a b)")[:, 0:2 * T].rearrange("p (b n) -> p b n", b=2)
                                for a in (projections.hi, projections.lo))
        s = lambda what: t.sem(f"{name}_{what}")
        self.w_hi_done, self.w_lo_done = s("wo_hi"), s("wo_lo")
        self.o_hi_done, self.o_lo_done, self.done, self.added = s("o_hi"), s("o_lo"), s("wo_done"), s("wo_added")
        self.landed = [s(f"landed_{i}") for i in range(3)]

    def staged(self, m):
        return self.norm.scratch[:, m % 3, :]

    def wait_staged(self, eng, m):
        eng.wait_ge(self.landed[m % 3], 16 * (m // 3 + 1))

    def sync(self, sp):
        sp.wait_ge(self.projections.lo_done, 3 * self.steps)
        for m in range(KD + NT):
            if m >= 3:
                sp.wait_ge(*((self.w_lo_done, m - 2) if m - 3 < KD else (self.added, 2 * (m - 2 - KD))))
            rows, at = (self.w_o, m) if m < KD else (self.x_rows, m - KD)
            sp.dma_start(self.staged(m), rows[at * P:(at + 1) * P, :]).then_inc(self.landed[m % 3], 16)

    def high_weights(self, act, k):
        if k == 0:
            act.wait_ge(self.projections.done, 6 * self.steps)
        self.wait_staged(act, k)
        act.copy(self.w_hi[:, k, :], self.staged(k)).then_inc(self.w_hi_done, 1)

    def low_weights(self, pool, k):
        pool.wait_ge(self.w_hi_done, k + 1)
        pool.tensor_tensor(self.w_lo[:, k, :], self.staged(k), self.w_hi[:, k, :].bitcast(F32), ALU.subtract)\
            .then_inc(self.w_lo_done, 1)

    def tensor(self, pe, tt):
        pe.wait_ge(self.o_lo_done, 2 * tt + 2)
        for k in range(KD):
            if tt == 0:
                pe.wait_ge(self.w_lo_done, k + 1)
            rows = slice(k * P, (k + 1) * P)
            for n in range(2):
                if k == 0 and tt >= 2:
                    pe.wait_ge(self.added, 2 * (tt - 2) + n + 1)
                cols = slice(n * HALF, (n + 1) * HALF)
                last = three_passes(pe, self.banks[:, 2 * (tt % 2) + n, :],
                                    (self.o_hi[:, tt % 2, rows], self.o_lo[:, tt % 2, rows]),
                                    (self.w_hi[:, k, cols], self.w_lo[:, k, cols]), k == 0, k == KD - 1)
        last.then_inc(self.done, 1)

    def vector(self, dve, tt):
        self.wait_staged(dve, KD + tt)
        dve.wait_ge(self.done, tt + 1)
        for n in range(2):
            cols = slice(n * HALF, (n + 1) * HALF)
            dve.tensor_tensor(self.t.x[:, tt, cols], self.banks[:, 2 * (tt % 2) + n, :], self.staged(KD + tt)[:, cols],
                              ALU.add).then_inc(self.added, 1)


def windowed_attention(t, gain, w_qkv, w_o, sink, x_rows):
    nc = t.nc
    KV = 4
    QH = 4
    NQ = KV * QH
    WIN = 3 * P
    blocks = [(max(i - 1, 0), min(i + 1, NT - 1)) for i in range(NT)]
    tiles = [b - a + 1 for a, b in blocks]
    before = [sum(tiles[:i]) for i in range(NT)]
    TILES = sum(tiles)
    with ExitStack() as ctx:
        sb = lambda *a: ctx.enter_context(nc.sbuf_tensor(*a))
        S = ctx.enter_context(nc.psum_tensor("a0_S", [P, 4, HALF], F32))
        TO = ctx.enter_context(nc.psum_tensor("a0_TO", [P, 4, HALF], F32))
        TB, O = TO[:, 0:2, :], TO[:, 2:4, :]
        norm = Norm(t, "a0n", gain, sb, TO, Loaded(t, x_rows))
        q_parts = sb("a0_q_parts", [P, QH, T], F32R)
        k_hi, k_lo = sb("a0_k_hi", [P, T], F32R), sb("a0_k_lo", [P, T], F32R)
        v_rows = sb("a0_v_rows", [P, NT, 2, HEAD], F32)
        probs = sb("a0_probs", [P, 3, QH, WIN], F32)
        pT = sb("a0_pT", [P, 2, 3, QH * P], F32)
        kvT = pT[:, 0, 0:2, :].rearrange("p a b -> p (a b)")
        bias = sb("a0_bias", [P, QH, WIN], F32)
        dist = sb("a0_dist", [P, WIN], F32)
        far = sb("a0_far", [P, WIN], F32)
        sinks = sb("a0_sinks", [P, NQ], F32)
        sink4 = sb("a0_sink4", [P, QH], F32)
        top4 = sb("a0_top4", [P, 2, QH], F32)
        neg4 = sb("a0_neg4", [P, 2, QH], F32)
        snk4 = sb("a0_snk4", [P, 2, QH], F32)
        sum4 = sb("a0_sum4", [P, 2, QH], F32)
        exs4 = sb("a0_exs4", [P, 2, QH], F32)
        inv4 = sb("a0_inv4", [P, 2, QH], F32)
        oT = t.x[:, :, :].rearrange("p a (k n) -> p a k n", k=KD)
        projections = Projections(t, "a0", w_qkv, lambda g: ((g * (QH * HEAD), QH * HEAD), (NQ * HEAD + g * HEAD, HEAD),
                                                             ((NQ + KV) * HEAD + g * HEAD, HEAD)),
                                  norm, probs[:, 0:2, :, :].rearrange("p a b c -> p (a b c)"), sb,
                                  ((0, 0), (1, 0), (2, 0), (0, 1), (1, 1), (2, 1)))
        out_proj = OutProjection(t, "a0o", w_o, x_rows, projections, KV, S)
        zero_rows = norm.gain_b[0:CAP, :]

        sink_loaded = t.sem("a0_sink_loaded")
        projected = lambda o: S[:, o, :] if o < 4 else O[:, o - 4, :]
        proj_done, hi_ready, parts_ready = projections.done, t.sem("a0_hi_ready"), t.sem("a0_parts_ready")
        v_turned, v_rows_ready = t.sem("a0_v_turned"), t.sem("a0_v_rows_ready")
        scores, scores_seen, biased = t.sem("a0_scores"), t.sem("a0_scores_seen"), t.sem("a0_biased")
        stats, exp_done, probs_ready = t.sem("a0_stats"), t.sem("a0_exp_done"), t.sem("a0_probs_ready")
        p_turned, pT_ready = t.sem("a0_p_turned"), t.sem("a0_pT_ready")
        pv_done, oT_ready = t.sem("a0_pv_done"), t.sem("a0_oT_ready")
        spare_zeroed = t.sem("spare_zeroed")
        dve_own, prep, zeroed, iota_done = t.sem("a0_dve_own"), t.sem("a0_prep"), t.sem("a0_zeroed"), t.sem("a0_iota")

        with nc.Block() as block:
            @block.sync
            def _(sp):
                norm.sync_load(sp)
                norm.source.load(sp)
                sp.dma_start(sinks[:, :], sink.broadcast_to((P, NQ))).then_inc(sink_loaded, 16)

                projections.load(sp, 0)
                projections.sync(sp, KV)
                sp.wait_ge(zeroed, 1)
                spare_rows = t.dram[1].rearrange("(r c) n -> r c n", c=CAP)[EXPERTS:ROWS]
                sp.dma_start(spare_rows.rearrange("r c n -> c r n"), zero_rows.unsqueeze(1)
                             .broadcast_to((CAP, SPARE, D))).then_inc(spare_zeroed, 16)
                out_proj.sync(sp)
                sp.wait_ge(spare_zeroed, 16)

            @block.gpsimd
            def _(pool):
                pool.iota(dist[:, :].bitcast(I32), pattern=[[-1, WIN]], base=P, channel_multiplier=1).then_inc(iota_done, 1)
                pool.wait_ge(norm.hn_ready, NT)
                pool.memset(zero_rows, 0.0).then_inc(zeroed, 1)
                for k in range(KD):
                    out_proj.low_weights(pool, k)

            @block.scalar
            def _(act):
                norm.scalar(act, [lambda j=j: projections.high_part(act, 0, j) for j in range(3)])

                def group(g, last_group):
                    def exponentials(i):
                        n = 8 * g + i
                        act.wait_ge(stats, n + 1)
                        for h in range(QH):
                            row = probs[:, i % 3, h, 0:tiles[i] * P]
                            act.activation(row, row, ACT.Exp, bias=neg4[:, i % 2, h:h + 1],
                                           accum_out=sum4[:, i % 2, h:h + 1])
                        act.activation(exs4[:, i % 2, :], snk4[:, i % 2, :], ACT.Exp, bias=t.zero_col[:, :])\
                           .then_inc(exp_done, 1)

                    for o in range(6):
                        act.wait_ge(proj_done, 6 * g + o + 1)
                        (j, n), out = projections.order[o], projected(o)
                        cols = slice(n * HALF, (n + 1) * HALF)
                        if j < 2:
                            for e, part in enumerate(HALVES):
                                last = act.mul(q_parts[part, 2 * j + e, cols], out[part], Q_SCALE)
                            last.then_inc(hi_ready, 1)
                        else:
                            for there in HALVES:
                                act.copy(k_hi[there, cols], out[0:64])
                            act.copy(kvT[:, cols], out).then_inc(hi_ready, 1)
                        if n == 1 and j < 2 and not last_group:
                            projections.high_part(act, g + 1, j)
                        if o == 4:
                            exponentials(0)

                    for i in range(NT):
                        if i + 1 < NT:
                            exponentials(i + 1)
                        if last_group:
                            out_proj.high_weights(act, i)
                        n = 8 * g + i
                        if i >= 2:
                            act.wait_ge(pv_done, n - 1)
                        for j in range(tiles[i]):
                            c = TILES * g + before[i] + j
                            act.wait_ge(p_turned, c + 1)
                            act.copy(pT[:, i % 2, j, :], TB[:, (before[i] + j) % 2, :]).then_inc(pT_ready, 1)
                        if i == 3 and not last_group:
                            projections.high_part(act, g + 1, 2)

                with act.Fori(0, KV - 1) as g:
                    group(g, False)
                group(KV - 1, True)
                for tt in range(NT):
                    act.wait_ge(oT_ready, (KV - 1) * NT + tt + 1)
                    if tt >= 2:
                        act.wait_ge(out_proj.done, tt - 1)
                    for b in range(2):
                        act.copy(out_proj.o_hi[:, tt % 2, b * HALF:(b + 1) * HALF].rearrange("p (k n) -> p k n", k=4),
                                 oT[:, tt, 4 * b:4 * b + 4, :]).then_inc(out_proj.o_hi_done, 1)

            @block.vector
            def _(dve):
                norm.vector(dve, [lambda j=j: projections.low_part(dve, 0, j) for j in range(3)])
                own = Step(dve, prep)
                dve.wait_ge(iota_done, 1)
                own(dve.tensor_copy(far[:, :], dist[:, :].bitcast(I32)))
                own(dve.tensor_scalar(dist[:, :], far[:, :], -1.0, None, ALU.mult))
                own(dve.tensor_tensor(dist[:, :], dist[:, :], far[:, :], ALU.max))
                own(dve.tensor_scalar(far[:, :], dist[:, :], float(P), MASKED, ALU.is_gt, ALU.mult))
                for h in range(QH):
                    last = dve.scalar_tensor_tensor(out=bias[:, h, :], in0=dist[:, :], scalar=-2.0 ** (-8.0 * (h + 1) / NQ),
                                                    in1=far[:, :], op0=ALU.mult, op1=ALU.add)
                own(last)
                dve.wait_ge(sink_loaded, 16)
                OWN = 2 + 4 * NT

                def o_part(tt):
                    for b in range(2):
                        dve.wait_ge(out_proj.o_hi_done, 2 * tt + b + 1)
                        part = slice(b * HALF, (b + 1) * HALF)
                        dve.tensor_tensor(out_proj.o_lo[:, tt % 2, part].rearrange("p (k n) -> p k n", k=4),
                                          oT[:, tt, 4 * b:4 * b + 4, :],
                                          out_proj.o_hi[:, tt % 2, part].bitcast(F32).rearrange("p (k n) -> p k n", k=4),
                                          ALU.subtract).then_inc(out_proj.o_lo_done, 1)

                def group(g, last_group):
                    own = Step(dve, dve_own, OWN * g)
                    own(dve.tensor_copy(sink4[:, :], sinks[:, bass.ds(g * QH, QH)]))
                    def value_rows(b):
                        dve.wait_ge(v_turned, 2 * g + b + 1)
                        source = TB[:, b, :].rearrange("p (a c) -> p a c", c=P)[:, :, HEAD:P]
                        for copy in range(2):
                            last = dve.tensor_copy(v_rows[:, 4 * b:4 * b + 4, copy, :], source)
                        last.then_inc(v_rows_ready, 1)

                    def masked_scores(i):
                        n = 8 * g + i
                        first = P if i == 0 else 0
                        width = tiles[i] * P
                        if i >= 3:
                            dve.wait_ge(p_turned, TILES * g + before[i - 2])
                        for h in range(QH):
                            wait_apart(dve, scores, 4 * n + h + 1, scores_seen)
                            dve.tensor_tensor_reduce(probs[:, i % 3, h, 0:width], S[:, h, 0:width],
                                                     bias[:, h, first:first + width], 1.0, MASKED,
                                                     ALU.add, ALU.max, top4[:, i % 2, h:h + 1]).then_inc(biased, 1)
                        dve.wait_ge(biased, 4 * n + 4)
                        own(dve.tensor_tensor(top4[:, i % 2, :], top4[:, i % 2, :], sink4[:, :], ALU.max))
                        own(dve.tensor_scalar(neg4[:, i % 2, :], top4[:, i % 2, :], -1.0, None, ALU.mult))
                        dve.tensor_tensor(snk4[:, i % 2, :], sink4[:, :], top4[:, i % 2, :], ALU.subtract).then_inc(stats, 1)

                    def normalise(i):
                        n = 8 * g + i
                        dve.wait_ge(exp_done, n + 1)
                        own(dve.tensor_tensor(sum4[:, i % 2, :], sum4[:, i % 2, :], exs4[:, i % 2, :], ALU.add))
                        own(dve.reciprocal(inv4[:, i % 2, :], sum4[:, i % 2, :]))
                        for h in range(QH):
                            row = probs[:, i % 3, h, 0:tiles[i] * P]
                            last = dve.tensor_scalar(row, row, inv4[:, i % 2, h:h + 1], None, ALU.mult)
                        last.then_inc(probs_ready, 1)

                    def heads_out(i):
                        dve.wait_ge(pv_done, 8 * g + i + 1)
                        out = O[:, i % 2, :].rearrange("p (h n) -> p h n", h=QH)
                        for e, part in enumerate((slice(0, 64), slice(64, 128))):
                            last = dve.tensor_copy(oT[part, i, bass.ds(2 * g, 2), :], out[part, e:QH:2, :])
                        last.then_inc(oT_ready, 1)

                    for o in range(6):
                        dve.wait_ge(hi_ready, 6 * g + o + 1)
                        (j, n), out = projections.order[o], projected(o)
                        cols = slice(n * HALF, (n + 1) * HALF)
                        for e, part in enumerate(HALVES):
                            if j < 2:
                                q = q_parts[:, 2 * j + e, cols]
                                last = dve.scalar_tensor_tensor(out=q[HALVES[1 - e]], in0=out[part], scalar=Q_SCALE,
                                                                in1=q[part].bitcast(F32), op0=ALU.mult, op1=ALU.subtract)
                            else:
                                last = dve.tensor_tensor(k_lo[part, cols], out[0:64],
                                                         k_hi[0:64, cols].bitcast(F32), ALU.subtract)
                        last.then_inc(parts_ready, 1)
                        if n == 1 and j < 2 and not last_group:
                            projections.low_part(dve, g + 1, j)
                        if o == 4:
                            masked_scores(0)
                            value_rows(0)
                            normalise(0)
                    for i in range(NT):
                        if i + 1 < NT:
                            masked_scores(i + 1)
                        if i == 0:
                            value_rows(1)
                        else:
                            normalise(i)
                        if i >= 1:
                            heads_out(i - 1)
                        if i == 4 and not last_group:
                            projections.low_part(dve, g + 1, 2)
                    if last_group:
                        o_part(0)
                        o_part(1)
                    heads_out(NT - 1)
                    own(dve.tensor_scalar(bias[:, :, :], bias[:, :, :], 2.0 ** (-8.0 * QH / NQ), None, ALU.mult))
                    assert own.n == OWN

                with dve.Fori(0, KV - 1) as g:
                    group(g, False)
                group(KV - 1, True)

                for tt in range(NT):
                    if 1 < tt + 1 < NT:
                        o_part(tt + 1)
                    out_proj.vector(dve, tt)

            @block.tensor
            def _(pe):
                def group(g, first_group):
                    def value_rows(b):
                        pe.wait_ge(hi_ready, 6 * g + 3 + 3 * b)
                        for a in range(4):
                            last = pe.transpose(TB[:, b, a * P:(a + 1) * P], kvT[:, (4 * b + a) * P:(4 * b + a + 1) * P],
                                                t.ident[:, :])
                        last.then_inc(v_turned, 1)

                    def head_scores(i):
                        n = 8 * g + i
                        a, b = blocks[i]
                        if i == 0:
                            pe.wait_ge(parts_ready, 6 * g + 4)
                        if i == 3:
                            pe.wait_ge(parts_ready, 6 * g + 6)
                        for h in range(QH):
                            if i >= 1:
                                pe.wait_ge(biased, 4 * (n - 1) + h + 1)
                            for k_part in (k_hi, k_lo):
                                last = pe.matmul(S[:, h, 0:tiles[i] * P], q_parts[:, h, i * P:(i + 1) * P],
                                                 k_part[:, a * P:(b + 1) * P], start=(k_part is k_hi), stop=(k_part is k_lo))
                            last.then_inc(scores, 1)

                    def product(i):
                        n = 8 * g + i
                        pe.wait_ge(probs_ready, n + 1)

                        def turn(j):
                            c = TILES * g + before[i] + j
                            if before[i] + j >= 2:
                                pe.wait_ge(pT_ready, c - 1)
                            for h in range(QH):
                                last = pe.transpose(TB[:, (before[i] + j) % 2, h * P:(h + 1) * P],
                                                    probs[:, i % 3, h, j * P:(j + 1) * P], t.ident[:, :])
                            last.then_inc(p_turned, 1)

                        def times_v(j):
                            c = TILES * g + before[i] + j
                            pe.wait_ge(pT_ready, c + 1)
                            return pe.matmul(O[:, i % 2, :],
                                             v_rows[:, blocks[i][0] + j, :, :].rearrange("p a b -> p (a b)"),
                                             pT[:, i % 2, j, :], start=(j == 0), stop=(j == tiles[i] - 1))

                        turn(0)
                        turn(1)
                        if i >= 2:
                            pe.wait_ge(oT_ready, n - 1)
                        times_v(0)
                        if tiles[i] == 3:
                            turn(2)
                            times_v(1)
                        times_v(tiles[i] - 1).then_inc(pv_done, 1)

                    for o in range(6):
                        (j, n), out = projections.order[o], projected(o)
                        if o == 4:
                            pe.wait_ge(parts_ready, 6 * g + 1)
                        projections.tensor(pe, out, g, o, first_group)
                        if o == 4:
                            head_scores(0)
                            value_rows(0)
                    head_scores(1)
                    value_rows(1)
                    for i in range(NT):
                        if i + 2 < NT:
                            head_scores(i + 2)
                        if i == 0:
                            pe.wait_ge(v_rows_ready, 2 * g + 2)
                        product(i)

                group(0, True)
                with pe.Fori(1, KV) as g:
                    group(g, False)
                for tt in range(NT):
                    out_proj.tensor(pe, tt)


def route(t, name, gain, w_group, b_group, w_router, b_router, moe):
    nc = t.nc
    NL = GROUPS + EXPERTS
    with ExitStack() as ctx:
        sb = lambda *a: ctx.enter_context(nc.sbuf_tensor(*a))
        ps = lambda *a: ctx.enter_context(nc.psum_tensor(*a))
        turn_banks = ps(f"{name}_T", [P, 4, HALF], F32)
        L_ps = ps(f"{name}_L", [P, 2, HALF], F32)
        R_ps = ps(f"{name}_R", [P, HALF], F32)
        C_ps = ps(f"{name}_C", [P, HALF], F32)
        table_ps = L_ps[0:CAP, 0, 0:CAP]
        norm = Norm(t, f"{name}n", gain, sb, turn_banks, Resident(), 2, moe.hn_rows, 4)
        w_sb = sb(f"{name}_w", [P, KD, NL], F32)
        b_sb = sb(f"{name}_b", [NL, 1], F32)
        lT = norm.junk
        lg = sb(f"{name}_lg", [P, NT, NL], F32)
        below = sb(f"{name}_below", [P, P], F32)
        ones = sb(f"{name}_ones", [P, P], F32)
        count_i = sb(f"{name}_count_i", [P, CAP], I32)
        count_up = sb(f"{name}_count_up", [P, CAP], F32)
        count_dn = sb(f"{name}_count_dn", [P, CAP], F32)
        token_i = sb(f"{name}_token_i", [P, NT], I32)
        token = sb(f"{name}_token", [P, NT], F32)
        place_hot = norm.hnT[:, :, :].rearrange("p a b -> p (a b)")[:, 0:2 * NT * CAP].rearrange("p (c n) -> p c n", n=CAP)
        row_hot = sb(f"{name}_row_hot", [P, 2 * NT, CAP], F32)
        v = lambda what, *shape: sb(f"{name}_{what}", [P, *shape], F32)
        gm, gh, gs = v("gm", NT), v("gh", NT, GROUPS), v("gs", NT, GROUPS)
        gd, gsum, pg = v("gd", NT, GROUPS), v("gsum", NT), v("pg", NT)
        le = v("le", NT, EXPERTS)
        top = v("top", 2, NT)
        seen = v("seen", NT, EXPERTS)
        code = v("code", 2, NT)
        hot = v("hot", 2, NT * EXPERTS)
        hots = v("hots", NT * EXPERTS)
        diff, ex, den = v("diff", NT), v("ex", NT), v("den", NT)
        tot = v("tot", NT, EXPERTS)
        base = v("base", NT + 1, EXPERTS)
        pos = v("pos", NT * EXPERTS)
        pick = v("pick", 2, NT * EXPERTS)
        place, extra0, more = v("place", 2 * NT), v("extra0", 2 * NT), v("more", 2 * NT)
        over = v("over", EXPERTS * STEPS)
        spare, run_a, run_b, first = v("spare", EXPERTS), v("run_a", EXPERTS), v("run_b", EXPERTS), v("first", EXPERTS)
        stepped = v("stepped", 2 * NT * STEPS)
        expert, row, slot_of_row = (v(what, 2 * NT) for what in ("expert", "row", "slot_of_row"))
        owner_cmp, ctl_f = v("owner_cmp", (COLS - EXPERTS) * EXPERTS), v("ctl_f", COLS + 1)
        steps_of = v("steps_of", STEPS)

        s = lambda what: t.sem(f"{name}_{what}")
        w_loaded, made, lT_ready = s("w_loaded"), s("made"), s("lT_ready")
        lg_done, own_s, act_in, act_out = s("lg_done"), s("own"), s("act_in"), s("act_out")
        hot_ready, counted, slots_hot, tabled = s("hot_ready"), s("counted"), s("slots_hot"), s("tabled")

        with nc.Block() as block:
            @block.sync
            def _(sp):
                norm.sync_load(sp)
                wide = dict(allow_slow_non_contiguous=True)
                sp.dma_start(w_sb[:, :, 0:GROUPS], w_group.rearrange("(p k) n -> p k n", k=KD)).then_inc(w_loaded, 16)
                sp.dma_start(w_sb[:, :, GROUPS:NL], w_router.rearrange("(p k) n -> p k n", k=KD)).then_inc(w_loaded, 16)
                sp.dma_start(b_sb[0:GROUPS, :], b_group.unsqueeze(1), **wide).then_inc(w_loaded, 16)
                sp.dma_start(b_sb[GROUPS:NL, :], b_router.unsqueeze(1), **wide).then_inc(w_loaded, 16)
                moe.load(sp, 0, 0)
                norm.sync_store(sp)
                moe.load(sp, 1, 0)
                moe.load(sp, 2, 0)
                for w in range(2):
                    sp.wait_ge(moe.hi_done[w], 2)
                    sp.wait_ge(moe.lo_done[w], 2)
                    moe.load(sp, w, 1)
                norm.sync_stored(sp)

            @block.gpsimd
            def _(pool):
                pool.memset(ones[:, :], 1.0).then_inc(made, 1)
                pool.iota(count_i[:, :], pattern=[[1, CAP]], base=0, channel_multiplier=0).then_inc(made, 1)
                pool.iota(token_i[:, :], pattern=[[P, NT]], base=0, channel_multiplier=1).then_inc(made, 1)
                pool.wait_ge(made, 1)
                pool.affine_select(out=below[:, :], in_=ones[:, :], compare_op=ALU.is_gt, fill=0.0, base=0,
                                   pattern=[[1, P]], channel_multiplier=-1).then_inc(made, 1)
                for w in range(2):
                    for piece in range(2):
                        moe.low_part(pool, w, 0, piece)

            @block.scalar
            def _(act):
                norm.scalar(act)
                act.wait_ge(w_loaded, 64)
                for n in range(2):
                    act.wait_ge(norm.used, 4 * (n + 1))
                    act.activation(lT[0:NL, n * HALF:(n + 1) * HALF], L_ps[0:NL, n, :], ACT.Identity, bias=b_sb[:, :])\
                       .then_inc(lT_ready, 1)
                act.wait_ge(act_in, 1)
                act.activation(gd[:, :, :], gd[:, :, :], ACT.Exp, bias=t.zero_col[:, :]).then_inc(act_out, 1)
                act.wait_ge(act_in, 2)
                act.activation(ex[:, :], diff[:, :], ACT.Exp, bias=t.zero_col[:, :]).then_inc(act_out, 1)
                for w in range(2):
                    act.wait_ge(moe.raw_loaded[w], 16)
                    for piece in range(2):
                        moe.high_part(act, w, piece)

            @block.tensor
            def _(pe):
                def logits(tt):
                    pe.wait_ge(norm.copied, tt + 1)
                    for k in range(KD):
                        last = pe.matmul(L_ps[0:NL, tt // 4, tt % 4 * P:(tt % 4 + 1) * P], w_sb[:, k, :],
                                         norm.tile_T(tt)[:, k, :], start=(k == 0), stop=(k == KD - 1))
                    last.then_inc(norm.used, 1)

                pe.wait_ge(w_loaded, 64)
                norm.turn(pe, 0)
                for tt in range(NT):
                    if tt + 1 < NT:
                        norm.turn(pe, tt + 1)
                    logits(tt)
                for n in range(2):
                    pe.wait_ge(lT_ready, n + 1)
                    for tt in range(4 * n, 4 * n + 4):
                        last = pe.transpose(R_ps[:, tt * NL:(tt + 1) * NL], lT[0:NL, tt * P:(tt + 1) * P], t.ident[0:NL, 0:NL])
                last.then_inc(lg_done, 1)
                pe.wait_ge(hot_ready, 1)
                pe.wait_ge(made, 4)
                pe.matmul(C_ps[:, 0:256], below[:, :], hots[:, :], start=True, stop=True)
                pe.matmul(C_ps[:, 256:512], ones[:, :], hots[:, :], start=True, stop=True).then_inc(counted, 1)
                pe.wait_ge(slots_hot, 1)
                for c in range(2 * NT):
                    last = pe.matmul(table_ps, place_hot[:, c, :], row_hot[:, c, :], start=(c == 0), stop=(c == 2 * NT - 1))
                last.then_inc(tabled, 1)

            @block.vector
            def _(dve):
                norm.vector(dve)
                own = Step(dve, own_s)
                tt_, ts_, red = dve.tensor_tensor, dve.tensor_scalar, dve.tensor_reduce
                dve.wait_ge(made, 4)
                own(dve.tensor_copy(count_up[:, :], count_i[:, :]))
                own(ts_(count_dn[:, :], count_up[:, :], -1.0, 64.0, ALU.mult, ALU.add))
                own(dve.tensor_copy(token[:, :], token_i[:, :]))
                own(ts_(steps_of[:, :], count_up[:, 1:STEPS + 1], float(CAP), None, ALU.mult))
                dve.wait_ge(lg_done, 1)
                own(dve.tensor_copy(lg[:, :, :], R_ps[:, 0:NT * NL].rearrange("p (a b) -> p a b", b=NL)))
                groups = lg[:, :, 0:GROUPS]
                over_g = lambda a: a.unsqueeze(2).broadcast_to((P, NT, GROUPS))
                over_e = lambda a: a.unsqueeze(2).broadcast_to((P, NT, EXPERTS))
                tiled = lambda a, n: a.unsqueeze(1).broadcast_to((P, NT, n))
                own(red(gm[:, :], groups, AX, ALU.max))
                tt_(gd[:, :, :], groups, over_g(gm[:, :]), ALU.subtract).then_inc(act_in, 1)
                own(tt_(gh[:, :, :], groups, over_g(gm[:, :]), ALU.is_equal))
                own(tt_(gs[:, :, :], gh[:, :, :], tiled(count_dn[:, 0:GROUPS], GROUPS), ALU.mult))
                own(red(gm[:, :], gs[:, :, :], AX, ALU.max))
                own(tt_(gh[:, :, :], gs[:, :, :], over_g(gm[:, :]), ALU.is_equal))
                own(ts_(gh[:, :, :], gh[:, :, :], -1.0, -MASKED, ALU.add, ALU.mult))
                own(tt_(le[:, :, :].rearrange("p a (g e) -> p a g e", g=GROUPS),
                        lg[:, :, GROUPS:NL].rearrange("p a (g e) -> p a g e", g=GROUPS),
                        gh[:, :, :].unsqueeze(3).broadcast_to((P, NT, GROUPS, PER_GROUP)), ALU.add))
                flat = lambda a: a[:, :, :].rearrange("p a b -> p (a b)")
                for c in range(TOP_K):
                    own(red(top[:, c, :], le[:, :, :], AX, ALU.max))
                    own(tt_(seen[:, :, :], le[:, :, :], over_e(top[:, c, :]), ALU.is_equal))
                    own(tt_(seen[:, :, :], seen[:, :, :], tiled(count_dn[:, 0:EXPERTS], EXPERTS), ALU.mult))
                    own(red(code[:, c, :], seen[:, :, :], AX, ALU.max))
                    own(tt_(hot[:, c, :].rearrange("p (a b) -> p a b", b=EXPERTS), seen[:, :, :], over_e(code[:, c, :]),
                            ALU.is_equal))
                    if c == 0:
                        own(dve.scalar_tensor_tensor(out=flat(le), in0=hot[:, 0, :], scalar=2 * MASKED, in1=flat(le),
                                                     op0=ALU.mult, op1=ALU.add))
                tt_(hots[:, :], hot[:, 0, :], hot[:, 1, :], ALU.add).then_inc(hot_ready, 1)
                tt_(diff[:, :], top[:, 1, :], top[:, 0, :], ALU.subtract).then_inc(act_in, 1)
                own(ts_(expert[:, :], code[:, :, :].rearrange("p a b -> p (a b)"), -1.0, 64.0, ALU.mult, ALU.add))
                own(dve.memset(base[:, 0, :], 0.0))
                dve.wait_ge(act_out, 2)
                own(red(gsum[:, :], gd[:, :, :], AX, ALU.add))
                own(dve.reciprocal(pg[:, :], gsum[:, :]))
                own(ts_(den[:, :], ex[:, :], 1.0, None, ALU.add))
                own(dve.reciprocal(den[:, :], den[:, :]))
                own(tt_(t.weight[:, 0, :], pg[:, :], den[:, :], ALU.mult))
                own(tt_(t.weight[:, 1, :], t.weight[:, 0, :], ex[:, :], ALU.mult))
                dve.wait_ge(counted, 1)
                own(dve.tensor_copy(flat(tot), C_ps[:, 256:512]))
                for a in range(NT):
                    own(tt_(base[:, a + 1, :], base[:, a, :], tot[:, a, :], ALU.add))
                own(tt_(pos[:, :], C_ps[:, 0:256], base[:, 0:NT, :].rearrange("p a b -> p (a b)"), ALU.add))
                twice = lambda a: a.unsqueeze(1).broadcast_to((P, 2, NT * EXPERTS))
                by_expert = pick[:, :, :].rearrange("p c (a b) -> p (c a) b", b=EXPERTS)
                own(tt_(pick[:, :, :], hot[:, :, :], twice(pos[:, :]), ALU.mult))
                own(red(place[:, :], by_expert, AX, ALU.add))
                total = base[:, NT, :]
                grid = over[:, :].rearrange("p (e j) -> p e j", j=STEPS)
                own(tt_(grid, total.unsqueeze(2).broadcast_to((P, EXPERTS, STEPS)),
                        steps_of[:, :].unsqueeze(1).broadcast_to((P, EXPERTS, STEPS)), ALU.is_gt))
                own(red(spare[:, :], grid, AX, ALU.add))
                source, target, shift = spare, run_a, 1
                while shift < EXPERTS:
                    own(dve.tensor_copy(target[:, 0:shift], source[:, 0:shift]))
                    own(tt_(target[:, shift:], source[:, shift:], source[:, 0:EXPERTS - shift], ALU.add))
                    source, target = target, (run_b if target is run_a else run_a)
                    shift *= 2
                running = source
                own(tt_(first[:, :], running[:, :], spare[:, :], ALU.subtract))
                own(tt_(pick[:, :, :].rearrange("p c (a b) -> p (c a) b", b=EXPERTS),
                        hot[:, :, :].rearrange("p c (a b) -> p (c a) b", b=EXPERTS),
                        first[:, :].unsqueeze(1).broadcast_to((P, 2 * NT, EXPERTS)), ALU.mult))
                own(red(extra0[:, :], by_expert, AX, ALU.add))
                ladder = stepped[:, :].rearrange("p (c j) -> p c j", j=STEPS)
                own(tt_(ladder, place[:, :].unsqueeze(2).broadcast_to((P, 2 * NT, STEPS)),
                        steps_of[:, :].unsqueeze(1).broadcast_to((P, 2 * NT, STEPS)), ALU.is_ge))
                own(red(more[:, :], ladder, AX, ALU.add))
                own(dve.scalar_tensor_tensor(out=place[:, :], in0=more[:, :], scalar=-float(CAP), in1=place[:, :],
                                             op0=ALU.mult, op1=ALU.add))
                own(tt_(row[:, :], extra0[:, :], more[:, :], ALU.add))
                own(ts_(row[:, :], row[:, :], float(EXPERTS - 1), None, ALU.add))
                own(tt_(row[:, :], row[:, :], expert[:, :], ALU.subtract))
                own(ts_(more[:, :], more[:, :], 0.0, None, ALU.is_gt))
                own(tt_(row[:, :], row[:, :], more[:, :], ALU.mult))
                own(tt_(row[:, :], row[:, :], expert[:, :], ALU.add))
                over_slots = lambda a, n: a.unsqueeze(2).broadcast_to((P, 2 * NT, n))
                own(tt_(row_hot[:, :, :], over_slots(row[:, :], CAP),
                        count_up[:, :].unsqueeze(1).broadcast_to((P, 2 * NT, CAP)), ALU.is_equal))
                for c in range(TOP_K):
                    half = row_hot[:, c * NT:(c + 1) * NT, 0:COLS]
                    own(tt_(half, half, token[:, :].unsqueeze(2).broadcast_to((P, NT, COLS)), ALU.mult))
                tt_(place_hot[:, :, :], over_slots(place[:, :], CAP),
                    count_up[:, :].unsqueeze(1).broadcast_to((P, 2 * NT, CAP)), ALU.is_equal).then_inc(slots_hot, 1)
                own(dve.scalar_tensor_tensor(out=slot_of_row[:, :], in0=row[:, :], scalar=float(CAP), in1=place[:, :],
                                             op0=ALU.mult, op1=ALU.add))
                own(dve.tensor_copy(t.out_slot[:, :], slot_of_row[:, :]))
                own(ts_(ctl_f[:, 0:1], running[:, EXPERTS - 1:EXPERTS], float(EXPERTS - 3), None, ALU.add))
                own(dve.tensor_copy(ctl_f[:, 1:1 + EXPERTS], count_up[:, 0:EXPERTS]))
                owners = owner_cmp[:, :].rearrange("p (b e) -> p b e", e=EXPERTS)
                own(tt_(owners, running[:, :].unsqueeze(1).broadcast_to((P, COLS - EXPERTS, EXPERTS)),
                        count_up[:, 0:COLS - EXPERTS].unsqueeze(2).broadcast_to((P, COLS - EXPERTS, EXPERTS)), ALU.is_le))
                own(red(ctl_f[:, 1 + EXPERTS:1 + COLS], owners, AX, ALU.add))
                own(ts_(ctl_f[:, 1 + EXPERTS:1 + COLS], ctl_f[:, 1 + EXPERTS:1 + COLS], float(EXPERTS - 1), None, ALU.min))
                own(dve.tensor_copy(moe.control[:, :], ctl_f[0:1, :]))
                dve.wait_ge(tabled, 1)
                own(dve.tensor_copy(moe.table[:, :], L_ps[0:CAP, 0, 0:COLS]))



def differential_attention(t, gain, w_qkv, w_o, lam, subln, lambda_init, x_rows):
    nc = t.nc
    HEADS = 8
    VD = 2 * HEAD
    QK = HEADS * 2 * HEAD
    SPAN = 2 * T - P
    with ExitStack() as ctx:
        sb = lambda *a: ctx.enter_context(nc.sbuf_tensor(*a))
        S = ctx.enter_context(nc.psum_tensor("a1_S", [P, 4, HALF], F32))
        TO = ctx.enter_context(nc.psum_tensor("a1_TO", [P, 4, HALF], F32))
        TB, O = TO[:, 0:2, :], TO[:, 2:4, :]
        q_parts, k_hi, k_lo = (sb(f"a1_{n}", [P, 2, T], F32R) for n in ("q_parts", "k_hi", "k_lo"))
        v_rows = sb("a1_v_rows", [P, NT, VD], F32)
        probs = sb("a1_probs", [P, 2, 2, T], F32)
        norm = Norm(t, "a1n", gain, sb, TO, Combined(t, "a1", t.dram[1], [probs[:, i // 2, i % 2, :] for i in range(4)]))
        mix = sb("a1_mix", [P, 4, T], F32)
        mixed, mixT = mix[:, 0:2, :], mix[:, 2:4, :]
        bias = sb("a1_bias", [P, SPAN], F32)
        o_rows = t.x[:, :, :].rearrange("p a (b c) -> p a b c", c=VD)
        o_square = norm.gain_b[:, 0:VD]
        sub_eps = sb("a1_sub_eps", [P, 1], F32)
        vT = mixT[:, 1, :]
        lam_b = sb("a1_lam", [P, 4, HEAD], F32)
        lam_2 = sb("a1_lam_2", [P, 2, HEAD], F32)
        lam_s = sb("a1_lam_s", [P, 2], F32)
        lam_neg = sb("a1_lam_neg", [P, 1], F32)
        sub_g = sb("a1_sub_g", [P, 1], F32)
        top2, neg2, sum2 = (sb(f"a1_{n}", [P, 2, 2], F32) for n in ("top2", "neg2", "sum2"))
        inv2 = sb("a1_inv2", [P, 4, 2], F32)
        ratio = sb("a1_ratio", [P, 2], F32)
        o_ss, o_rms, o_rstd = (sb(f"a1_{n}", [P, NT, HEADS], F32) for n in ("o_ss", "o_rms", "o_rstd"))
        projections = Projections(t, "a1", w_qkv, lambda h: ((h * P, P), (QK + h * P, P), (2 * QK + h * P, P)), norm,
                                  mix[:, 0:3, :].rearrange("p a b -> p (a b)"), sb,
                                  ((0, 0), (1, 0), (0, 1), (1, 1), (2, 0), (2, 1)))
        out_proj = OutProjection(t, "a1o", w_o, x_rows, projections, HEADS, S)

        lam_loaded, x_stored = t.sem("a1_lam_loaded"), t.sem("a1_x_stored")
        projected = lambda o: S[:, o, :] if o < 4 else O[:, o - 4, :]
        proj_done, hi_ready, parts_ready = projections.done, t.sem("a1_hi_ready"), t.sem("a1_parts_ready")
        vT_ready, v_turned, v_rows_ready = (t.sem(f"a1_{n}") for n in ("vT_ready", "v_turned", "v_rows_ready"))
        scores, scores_seen, biased = t.sem("a1_scores"), t.sem("a1_scores_seen"), t.sem("a1_biased")
        stats, exp_done, mixed_ready = t.sem("a1_stats"), t.sem("a1_exp_done"), t.sem("a1_mixed_ready")
        m_turned, mixT_ready, pv_done, o_ready = t.sem("a1_m_turned"), t.sem("a1_mixT_ready"), t.sem("a1_pv_done"), t.sem("a1_o_ready")
        dve_own, prep, iota_done = t.sem("a1_dve_own"), t.sem("a1_prep"), t.sem("a1_iota")
        lam_in, lam_out = t.sem("a1_lam_in"), t.sem("a1_lam_out")
        o_squared, rms_out, scaled, o_turned = (t.sem(f"a1_{n}") for n in ("o_squared", "rms_out", "scaled", "o_turned"))

        with nc.Block() as block:
            @block.sync
            def _(sp):
                norm.sync_load(sp)
                sp.dma_start(lam_b[:, :, :], lam.unsqueeze(0).broadcast_to((P, 4, HEAD))).then_inc(lam_loaded, 16)
                sp.dma_start(sub_g[:, :], subln.unsqueeze(1), allow_slow_non_contiguous=True).then_inc(lam_loaded, 16)

                norm.source.complete(sp, 1)
                projections.load(sp, 0)
                norm.source.complete(sp, NT - 1)
                for tt in range(NT):
                    sp.dma_start(x_rows[tt * P:(tt + 1) * P, :], t.x[:, tt, :]).then_inc(x_stored, 16)
                projections.sync(sp, HEADS)
                out_proj.sync(sp)

            @block.gpsimd
            def _(pool):
                norm.source.gather(pool)
                pool.iota(bias[:, :].bitcast(I32), pattern=[[-1, SPAN]], base=T - P, channel_multiplier=1).then_inc(iota_done, 1)
                pool.memset(sub_eps[:, :], SUBLN_EPS).then_inc(iota_done, 1)
                for k in range(KD):
                    out_proj.low_weights(pool, k)

            @block.scalar
            def _(act):
                norm.scalar(act, [lambda j=j: projections.high_part(act, 0, j) for j in range(3)])
                act.wait_ge(lam_in, 1)
                act.activation(lam_s[:, :], lam_s[:, :], ACT.Exp, bias=t.zero_col[:, :]).then_inc(lam_out, 1)
                def head(h, last_head):
                    def exponentials(i):
                        n = NT * h + i
                        act.wait_ge(stats, n + 1)
                        for c in range(2):
                            row = probs[:, i % 2, c, :]
                            last = act.activation(row, row, ACT.Exp, bias=neg2[:, i % 2, c:c + 1],
                                                  accum_out=sum2[:, i % 2, c:c + 1])
                        last.then_inc(exp_done, 1)

                    def output_square(i):
                        act.wait_ge(o_ready, NT * h + i + 1)
                        if i >= 1:
                            act.wait_ge(o_squared, NT * h + i)
                        act.activation(o_square, o_rows[:, i, bass.ds(h, 1), :].rearrange("p a b -> p (a b)"), ACT.Square,
                                       bias=t.zero_col[:, :], accum_out=o_ss[:, i, bass.ds(h, 1)]).then_inc(o_squared, 1)

                    for o in range(6):
                        act.wait_ge(proj_done, 6 * h + o + 1)
                        (j, n), out = projections.order[o], projected(o)
                        cols = slice(n * HALF, (n + 1) * HALF)
                        if j == 0:
                            for c, part in enumerate(HALVES):
                                last = act.mul(q_parts[part, c, cols], out[part], Q_SCALE)
                            last.then_inc(hi_ready, 1)
                        elif j == 1:
                            for c, part in enumerate(HALVES):
                                for there in HALVES:
                                    last = act.copy(k_hi[there, c, cols], out[part])
                            last.then_inc(hi_ready, 1)
                        else:
                            act.copy(vT[:, cols], out).then_inc(vT_ready, 1)
                            act.wait_ge(v_turned, 2 * h + n + 1)
                            act.copy(v_rows[:, 4 * n:4 * n + 4, :], TB[:, n, :].rearrange("p (a b) -> p a b", b=VD))\
                               .then_inc(v_rows_ready, 1)
                        if n == 1 and j < 2 and not last_head:
                            projections.high_part(act, h + 1, j)
                        if o == 4:
                            exponentials(0)

                    for i in range(NT):
                        if i + 1 < NT:
                            exponentials(i + 1)
                        if last_head:
                            out_proj.high_weights(act, i)
                        n = NT * h + i
                        if i >= 2:
                            act.wait_ge(pv_done, n - 1)
                        for b in range(2):
                            act.wait_ge(m_turned, 2 * n + b + 1)
                            act.copy(mixT[:, i % 2, b * HALF:(b + 1) * HALF], TB[:, b, :]).then_inc(mixT_ready, 1)
                        if i == 3 and not last_head:
                            projections.high_part(act, h + 1, 2)
                        if i >= 3:
                            output_square(i - 3)
                    for i in range(NT - 3, NT):
                        output_square(i)
                    act.wait_ge(o_squared, NT * h + NT)

                with act.Fori(0, HEADS - 1) as h:
                    head(h, False)
                head(HEADS - 1, True)
                act.activation(o_rms[:, :, :], o_ss[:, :, :], ACT.Sqrt, bias=sub_eps[:, :], scale=1.0 / VD).then_inc(rms_out, 1)
                for tt in range(NT):
                    for b in range(2):
                        act.wait_ge(o_turned, 2 * tt + b + 1)
                        if tt >= 2:
                            act.wait_ge(out_proj.done, tt - 1)
                        act.activation(out_proj.o_hi[:, tt % 2, b * HALF:(b + 1) * HALF], TB[:, b, :], ACT.Copy,
                                       scale=sub_g[:, :]).then_inc(out_proj.o_hi_done, 1)

            @block.vector
            def _(dve):
                norm.vector(dve, [lambda j=j: projections.low_part(dve, 0, j) for j in range(3)])
                dve.wait_ge(projections.lo_done, 3)
                own = Step(dve, prep)
                dve.wait_ge(iota_done, 2)
                wide = mixed[:, :, :].rearrange("p a b -> p (a b)")[:, 0:SPAN]
                own(dve.tensor_copy(wide, bias[:, :].bitcast(I32)))
                own(dve.tensor_scalar(bias[:, :], wide, -1.0, None, ALU.mult))
                own(dve.tensor_tensor(bias[:, :], bias[:, :], wide, ALU.max))
                own(dve.tensor_scalar(bias[:, :], bias[:, :], -2.0 ** (-8.0 / HEADS), None, ALU.mult))
                dve.wait_ge(lam_loaded, 32)
                own(dve.tensor_tensor(lam_2[:, :, :], lam_b[:, 0:4:2, :], lam_b[:, 1:4:2, :], ALU.mult))
                own(dve.tensor_reduce(lam_s[:, :], lam_2[:, :, :], AX, ALU.add))
                own(dve.tensor_scalar(sub_g[:, :], sub_g[:, :], 1.0 - lambda_init, None, ALU.mult))
                dve.tensor_copy(lam_neg[:, :], lam_s[:, 0:1]).then_inc(lam_in, 1)
                dve.wait_ge(lam_out, 1)
                own(dve.tensor_tensor(lam_neg[:, :], lam_s[:, 1:2], lam_s[:, 0:1], ALU.subtract))
                own(dve.tensor_scalar(lam_neg[:, :], lam_neg[:, :], -lambda_init, None, ALU.add))
                prepared = own.n
                dve.wait_ge(x_stored, 16 * NT)
                OWN = 2 * NT + 1

                def head(h, last_head):
                    own = Step(dve, dve_own, OWN * h)
                    def biased_scores(i):
                        n = NT * h + i
                        if i >= 2:
                            dve.wait_ge(mixed_ready, n - 1)
                        for c in range(2):
                            wait_apart(dve, scores, 2 * n + c + 1, scores_seen)
                            at = T - P - i * P
                            dve.tensor_tensor_reduce(probs[:, i % 2, c, :].rearrange("p (a b) -> p a b", a=2),
                                                     S[:, 2 * c:2 * c + 2, :],
                                                     bias[:, at:at + T].rearrange("p (a b) -> p a b", a=2), 1.0, MASKED,
                                                     ALU.add, ALU.max, top2[:, i % 2, c:c + 1]).then_inc(biased, 1)
                        dve.wait_ge(biased, 2 * n + 2)
                        dve.tensor_scalar(neg2[:, i % 2, :], top2[:, i % 2, :], -1.0, None, ALU.mult).then_inc(stats, 1)

                    def mix(i):
                        n = NT * h + i
                        dve.wait_ge(exp_done, n + 1)
                        own(dve.reciprocal(inv2[:, i % 4, :], sum2[:, i % 2, :]))
                        own(dve.scalar_tensor_tensor(out=ratio[:, i % 2:i % 2 + 1], in0=inv2[:, i % 4, 1:2],
                                                     scalar=lam_neg[:, :], in1=sum2[:, i % 2, 0:1],
                                                     op0=ALU.mult, op1=ALU.mult))
                        if i >= 2:
                            dve.wait_ge(m_turned, 2 * (n - 1))
                        dve.scalar_tensor_tensor(out=mixed[:, i % 2, :], in0=probs[:, i % 2, 1, :],
                                                 scalar=ratio[:, i % 2:i % 2 + 1], in1=probs[:, i % 2, 0, :],
                                                 op0=ALU.mult, op1=ALU.add).then_inc(mixed_ready, 1)

                    def head_out(i):
                        dve.wait_ge(pv_done, NT * h + i + 1)
                        dve.tensor_scalar(o_rows[:, i, bass.ds(h, 1), :].rearrange("p a b -> p (a b)"), O[:, i % 2, 0:VD],
                                          inv2[:, i % 4, 0:1], None, ALU.mult).then_inc(o_ready, 1)

                    for o in range(6):
                        (j, n), out = projections.order[o], projected(o)
                        if j < 2:
                            dve.wait_ge(hi_ready, 4 * h + o + 1)
                        cols = slice(n * HALF, (n + 1) * HALF)
                        for c, part in enumerate(HALVES):
                            if j == 0:
                                last = dve.scalar_tensor_tensor(out=q_parts[HALVES[1 - c], c, cols], in0=out[part],
                                                                scalar=Q_SCALE, in1=q_parts[part, c, cols].bitcast(F32),
                                                                op0=ALU.mult, op1=ALU.subtract)
                            elif j == 1:
                                for there in HALVES:
                                    last = dve.tensor_tensor(k_lo[there, c, cols], out[part],
                                                             k_hi[part, c, cols].bitcast(F32), ALU.subtract)
                        if j < 2:
                            last.then_inc(parts_ready, 1)
                        if n == 1 and j < 2 and not last_head:
                            projections.low_part(dve, h + 1, j)
                        if o == 4:
                            biased_scores(0)
                            mix(0)

                    for i in range(NT):
                        if i + 1 < NT:
                            biased_scores(i + 1)
                        if i >= 2:
                            head_out(i - 2)
                        if i > 0:
                            mix(i)
                        if i == 4 and not last_head:
                            projections.low_part(dve, h + 1, 2)
                    head_out(NT - 2)
                    head_out(NT - 1)
                    own(dve.tensor_scalar(bias[:, :], bias[:, :], 2.0 ** (-8.0 / HEADS), None, ALU.mult))
                    assert own.n == OWN

                with dve.Fori(0, HEADS - 1) as h:
                    head(h, False)
                head(HEADS - 1, True)
                own = Step(dve, prep, prepared)
                dve.wait_ge(rms_out, 1)
                own(dve.reciprocal(o_rstd[:, :, :], o_rms[:, :, :]))

                def scale(tt):
                    dve.tensor_tensor(o_rows[:, tt, :, :], o_rows[:, tt, :, :],
                                      o_rstd[:, tt, :].unsqueeze(2).broadcast_to((P, HEADS, VD)), ALU.mult).then_inc(scaled, 1)

                def o_part(tt):
                    for b in range(2):
                        dve.wait_ge(out_proj.o_hi_done, 2 * tt + b + 1)
                        part = slice(b * HALF, (b + 1) * HALF)
                        dve.scalar_tensor_tensor(out=out_proj.o_lo[:, tt % 2, part], in0=TB[:, b, :], scalar=sub_g[:, :],
                                                 in1=out_proj.o_hi[:, tt % 2, part].bitcast(F32),
                                                 op0=ALU.mult, op1=ALU.subtract).then_inc(out_proj.o_lo_done, 1)
                scale(0)
                scale(1)
                o_part(0)
                for tt in range(NT):
                    if tt + 2 < NT:
                        scale(tt + 2)
                    if tt + 1 < NT:
                        o_part(tt + 1)
                    out_proj.vector(dve, tt)

            @block.tensor
            def _(pe):
                def head(h, first_head):
                    def value_rows(b):
                        pe.wait_ge(vT_ready, 2 * h + b + 1)
                        for a in range(4):
                            last = pe.transpose(TB[:, b, a * P:(a + 1) * P], vT[:, (4 * b + a) * P:(4 * b + a + 1) * P],
                                                t.ident[:, :])
                        last.then_inc(v_turned, 1)

                    def head_scores(i):
                        n = NT * h + i
                        for c in range(2):
                            if i >= 1:
                                pe.wait_ge(biased, 2 * (n - 1) + c + 1)
                            for b in range(2):
                                for k_part in (k_hi, k_lo):
                                    last = pe.matmul(S[:, 2 * c + b, :], q_parts[:, c, i * P:(i + 1) * P],
                                                     k_part[:, c, b * HALF:(b + 1) * HALF],
                                                     start=(k_part is k_hi), stop=(k_part is k_lo))
                            last.then_inc(scores, 1)

                    def product(i):
                        n = NT * h + i
                        pe.wait_ge(mixed_ready, n + 1)
                        for b in range(2):
                            if i >= 1:
                                pe.wait_ge(mixT_ready, 2 * (n - 1) + b + 1)
                            for a in range(4):
                                k = 4 * b + a
                                last = pe.transpose(TB[:, b, a * P:(a + 1) * P], mixed[:, i % 2, k * P:(k + 1) * P],
                                                    t.ident[:, :])
                            last.then_inc(m_turned, 1)
                        if i >= 2:
                            pe.wait_ge(o_ready, n - 1)
                        for k in range(KD):
                            if k % 4 == 0:
                                pe.wait_ge(mixT_ready, 2 * n + k // 4 + 1)
                            last = pe.matmul(O[:, i % 2, 0:VD], mixT[:, i % 2, k * P:(k + 1) * P], v_rows[:, k, :],
                                             start=(k == 0), stop=(k == KD - 1))
                        last.then_inc(pv_done, 1)

                    for o in range(6):
                        (j, n), out = projections.order[o], projected(o)
                        if o == 4:
                            pe.wait_ge(parts_ready, 4 * h + 1)
                        projections.tensor(pe, out, h, o, first_head)
                        if o == 4:
                            pe.wait_ge(parts_ready, 4 * h + 4)
                            head_scores(0)
                            value_rows(0)

                    head_scores(1)
                    value_rows(1)
                    for i in range(NT):
                        if i + 2 < NT:
                            head_scores(i + 2)
                        if i == 0:
                            pe.wait_ge(v_rows_ready, 2 * h + 2)
                        product(i)

                head(0, True)
                with pe.Fori(1, HEADS) as h:
                    head(h, False)

                def turn_o(tt):
                    pe.wait_ge(scaled, tt + 1)
                    for b in range(2):
                        if tt >= 1:
                            pe.wait_ge(out_proj.o_lo_done, 2 * (tt - 1) + b + 1)
                        for a in range(4):
                            last = pe.transpose(TB[:, b, a * P:(a + 1) * P], o_rows[:, tt, 4 * b + a, :], t.ident[:, :])
                        last.then_inc(o_turned, 1)

                turn_o(0)
                for tt in range(NT):
                    if tt + 1 < NT:
                        turn_o(tt + 1)
                    out_proj.tensor(pe, tt)


def final_norm(t, gain, out):
    nc = t.nc
    BUFS = 8
    with ExitStack() as ctx:
        sb = lambda *a: ctx.enter_context(nc.sbuf_tensor(*a))
        back = sb("f_back", [P, BUFS, D], F32)
        source = Combined(t, "f", t.dram[1], [back[:, i, :] for i in range(BUFS)])
        gain_b, junk = sb("f_gain", [P, D], F32), sb("f_junk", [P, D], F32)
        rows = sb("f_rows", [P, NT, D], F32)
        ssq, rms, rstd = sb("f_ssq", [P, NT], F32), sb("f_rms", [P, NT], F32), sb("f_rstd", [P, NT], F32)
        gain_loaded, squared, rms_ready, chain, ready, stored = (
            t.sem(f"f_{n}") for n in ("gain_loaded", "squared", "rms_ready", "chain", "ready", "stored"))
        with nc.Block() as block:
            @block.sync
            def _(sp):
                sp.dma_start(gain_b[:, :], gain.broadcast_to((P, D))).then_inc(gain_loaded, 16)
                for tt in range(NT):
                    sp.wait_ge(ready, tt + 1)
                    sp.dma_start(out[0, tt * P:(tt + 1) * P, :], rows[:, tt, :]).then_inc(stored, 16)
                sp.wait_ge(stored, 16 * NT)

            @block.gpsimd
            def _(pool):
                source.gather(pool)

            @block.scalar
            def _(act):
                for tt in range(NT):
                    source.complete(act, tt)
                    if tt:
                        act.wait_ge(squared, tt)
                    act.activation(junk[:, :], t.x[:, tt, :], ACT.Square, bias=t.zero_col[:, :],
                                   accum_out=ssq[:, tt:tt + 1]).then_inc(squared, 1)
                    act.wait_ge(squared, tt + 1)
                    act.activation(rms[:, tt:tt + 1], ssq[:, tt:tt + 1], ACT.Sqrt, bias=t.eps_col[:, :],
                                   scale=1.0 / D).then_inc(rms_ready, 1)

            @block.vector
            def _(dve):
                source.add(dve, 0)
                for tt in range(NT):
                    if tt + 1 < NT:
                        source.add(dve, tt + 1)
                    dve.wait_ge(rms_ready, tt + 1)
                    dve.reciprocal(rstd[:, tt:tt + 1], rms[:, tt:tt + 1]).then_inc(chain, 1)
                    if tt == 0:
                        dve.wait_ge(gain_loaded, 16)
                    dve.wait_ge(chain, tt + 1)
                    dve.scalar_tensor_tensor(out=rows[:, tt, :], in0=t.x[:, tt, :], scalar=rstd[:, tt:tt + 1],
                                             in1=gain_b[:, :], op0=ALU.mult, op1=ALU.mult).then_inc(ready, 1)


class Experts:

    def __init__(self, t, name, w_gate, w_up, w_down, dram, ctx):
        nc = t.nc
        sb = lambda *a: ctx.enter_context(nc.sbuf_tensor(*a))
        self.t, self.name = t, name
        self.weights = (w_gate, w_up, w_down)
        self.hn_rows, self.out_rows = dram
        self.raw = [sb(f"{name}_raw_{w}", [P, KD * HIDDEN], F32) for w in ("gate", "up", "down")]
        self.table = sb(f"{name}_table", [CAP, COLS], I32)
        self.control = sb(f"{name}_control", [1, COLS + 1], I32)
        s = lambda what: t.sem(f"{name}_{what}")
        names = ("gate", "up", "down")
        self.raw_loaded, self.hi_done, self.lo_done = ([s(f"{w}_{n}") for w in names] for n in ("loaded", "hi_done", "lo_done"))
        self.hi, self.lo = ([sb(f"{name}_{n}_{w}", [P, KD * HIDDEN], F32R) for w in names[:2]] for n in ("hi", "lo"))

    def load(self, sp, w, expert, to=None):
        to = w if to is None else to
        k = KH if w == 2 else KD
        sp.dma_start(self.raw[to][:, :], self.weights[w][expert].rearrange("(p k) n -> p (k n)", k=k)
                     if isinstance(expert, int) else
                     self.weights[w][bass.ds(expert, 1)].rearrange("e (p k) n -> p (e k n)", k=k))\
          .then_inc(self.raw_loaded[to], 16)

    def high_part(self, act, w, piece):
        cut = slice(piece * PIECE, (piece + 1) * PIECE)
        act.copy(self.hi[w][:, cut], self.raw[w][:, cut]).then_inc(self.hi_done[w], 1)

    def low_part(self, eng, w, b, piece):
        eng.wait_ge(self.hi_done[w], 2 * b + piece + 1)
        cut = slice(piece * PIECE, (piece + 1) * PIECE)
        eng.tensor_tensor(self.lo[w][:, cut], self.raw[w][:, cut], self.hi[w][:, cut].bitcast(F32), ALU.subtract)\
           .then_inc(self.lo_done[w], 1)

    def run(self):
        t, nc, name = self.t, self.t.nc, self.name
        with ExitStack() as ctx:
            sb = lambda *a: ctx.enter_context(nc.sbuf_tensor(*a))
            ps = lambda *a: ctx.enter_context(nc.psum_tensor(*a))
            self.hi.append(sb(f"{name}_hi_down", [P, KH * D], F32R))
            self.lo.append(sb(f"{name}_lo_down", [P, KH * D], F32R))
            hi, lo, hi_done, lo_done = self.hi, self.lo, self.hi_done, self.lo_done
            pick = sb(f"{name}_pick", [CAP, 1], I32)
            xg = sb(f"{name}_xg", [CAP, D], F32)
            x_hi, x_lo = sb(f"{name}_x_hi", [P, KD * CAP], F32R), sb(f"{name}_x_lo", [P, KD * CAP], F32R)
            gated = sb(f"{name}_gated", [CAP, HIDDEN], F32)
            hid = sb(f"{name}_hid", [CAP, HIDDEN], F32)
            h_hi, h_lo = sb(f"{name}_h_hi", [P, KH * CAP], F32R), sb(f"{name}_h_lo", [P, KH * CAP], F32R)
            y = sb(f"{name}_y", [CAP, D], F32)
            G, U, HT = ps(f"{name}_G", [P, HALF], F32), ps(f"{name}_U", [P, HALF], F32), ps(f"{name}_HT", [P, HALF], F32)
            Y, XT = ps(f"{name}_Y", [P, 2, HALF], F32), ps(f"{name}_XT", [P, 2, HALF], F32)
            s = lambda what: t.sem(f"{name}_{what}")
            gate_done, up_done, down_done = s("gate_done"), s("up_done"), s("down_done")
            picked, gathered, x_turned, x_hi_done, x_lo_done = s("picked"), s("gathered"), s("x_turned"), s("x_hi"), s("x_lo")
            gated_done, hid_done, h_turned, h_hi_done, h_lo_done = s("gated"), s("hid"), s("h_turned"), s("h_hi"), s("h_lo")
            pick_seen = s("pick_seen")
            y_act, y_dve, y_stored = s("y_act"), s("y_dve"), s("y_stored")

            def steady_blocks(eng):
                return eng.value_load(self.control[0:1, 0:1], min_val=EXPERTS - 3, max_val=ROWS - 3)

            def in_turn(eng, step):
                last = steady_blocks(eng) + 2
                step(0, True, False)
                step(1, False, False)
                with eng.Fori(2, last) as b:
                    step(b, False, False)
                step(last, False, True)
                return last

            with nc.Block() as block:
                @block.sync
                def _(sp):
                    def load(w, b, expert):
                        sp.wait_ge(hi_done[w], 2 * b)
                        sp.wait_ge(lo_done[w], 2 * b)
                        self.load(sp, w, expert)

                    def expert_of(b):
                        return sp.value_load(self.control[0:1, bass.ds(b + 1, 1)], min_val=0, max_val=EXPERTS - 1)

                    last = steady_blocks(sp) + 2
                    load(2, 1, 1)
                    load(0, 2, expert_of(2))
                    load(1, 2, expert_of(2))
                    with sp.Fori(2, last) as b:
                        following, expert = expert_of(b + 1), expert_of(b)
                        for w in range(2):
                            load(w, b + 1, following)
                        load(2, b, expert)
                    sp.wait_ge(hi_done[0], 2 * last + 2)
                    sp.wait_ge(lo_done[0], 2 * last + 2)
                    self.load(sp, 2, expert_of(last), 0)

                @block.gpsimd
                def _(pool):
                    def gather(b, first):
                        if not first:
                            pool.wait_ge(x_turned, b)
                        pool.tensor_copy(pick[:, :], self.table[:, b:b + 1] if first else self.table[:, bass.ds(b, 1)])\
                            .then_inc(picked, 1)
                        wait_apart(pool, picked, b + 1, pick_seen)
                        pool.indirect_dma_start(out=xg[:, :], out_offset=None, in_=self.hn_rows,
                                                in_offset=bass.IndirectOffsetOnAxis(pick[:, :], 0)).then_inc(gathered, 16)

                    def store(b):
                        pool.wait_ge(y_act, b + 1)
                        pool.wait_ge(y_dve, b + 1)
                        rows = self.out_rows.rearrange("(r c) n -> r c n", c=CAP)
                        pool.dma_start(rows[b] if isinstance(b, int) else rows[bass.ds(b, 1)].rearrange("r c n -> (r c) n"),
                                       y[:, :]).then_inc(y_stored, 16)

                    def step(b, first, last):
                        if not last:
                            gather(b + 1, False)
                        if not first:
                            store(b - 1)
                    gather(0, True)
                    last = in_turn(pool, step)
                    store(last)
                    pool.wait_ge(y_stored, 16 * (last + 1))

                def times(pe, out, left, right, K, n, N):
                    (l_hi, l_lo), (r_hi, r_lo) = left, right
                    for k in range(K):
                        rows = slice(k * CAP, (k + 1) * CAP)
                        cols = slice(k * N + n * HALF, k * N + (n + 1) * HALF)
                        pe.matmul(out, l_hi[:, rows], r_hi[:, cols], start=(k == 0), stop=False)
                        pe.matmul(out, l_lo[:, rows], r_hi[:, cols], start=False, stop=False)
                        last = pe.matmul(out, l_hi[:, rows], r_lo[:, cols], start=False, stop=(k == K - 1))
                    return last

                @block.tensor
                def _(pe):
                    def turn_x(b):
                        pe.wait_ge(gathered, 16 * (b + 1))
                        wait_count(pe, x_lo_done, 2 * b)
                        for half in range(2):
                            for k in range(4):
                                kk = 4 * half + k
                                last = pe.transpose(XT[:, half, k * CAP:(k + 1) * CAP], xg[:, kk * P:(kk + 1) * P],
                                                    t.ident[0:CAP, 0:CAP])
                        last.then_inc(x_turned, 1)

                    def turn_h(b):
                        pe.wait_ge(hid_done, b + 1)
                        wait_count(pe, h_lo_done, b)
                        for k in range(KH):
                            last = pe.transpose(HT[:, k * CAP:(k + 1) * CAP], hid[:, k * P:(k + 1) * P],
                                                t.ident[0:CAP, 0:CAP])
                        last.then_inc(h_turned, 1)

                    def down(b, last=False):
                        w = 0 if last else 2
                        pe.wait_ge(h_lo_done, b + 1)
                        pe.wait_ge(lo_done[w], 2 * b + (4 if last else 2))
                        wait_count(pe, y_act, b)
                        wait_count(pe, y_dve, b)
                        for n in range(2):
                            times(pe, Y[0:CAP, n, :], (h_hi, h_lo), (hi[w], lo[w]), KH, n, D).then_inc(down_done, 1)

                    def step(b, first, last):
                        pe.wait_ge(x_lo_done, 2 * b + 2)
                        pe.wait_ge(lo_done[0], 2 * b + 2)
                        if not first:
                            pe.wait_ge(gated_done, b)
                        times(pe, G[0:CAP, :], (x_hi, x_lo), (hi[0], lo[0]), KD, 0, HIDDEN).then_inc(gate_done, 1)
                        if not first:
                            turn_h(b - 1)
                        pe.wait_ge(lo_done[1], 2 * b + 2)
                        if not first:
                            pe.wait_ge(hid_done, b)
                        times(pe, U[0:CAP, :], (x_hi, x_lo), (hi[1], lo[1]), KD, 0, HIDDEN).then_inc(up_done, 1)
                        if not last:
                            turn_x(b + 1)
                        if not first:
                            down(b - 1)
                    turn_x(0)
                    last = in_turn(pe, step)
                    turn_h(last)
                    down(last, True)

                @block.scalar
                def _(act):
                    def split(w, b, piece):
                        if piece == 0:
                            act.wait_ge(self.raw_loaded[w], 16 * (b + 1))
                            wait_count(act, *((gate_done, b), (up_done, b), (down_done, 2 * b))[w])
                        self.high_part(act, w, piece)

                    def x_part(b):
                        act.wait_ge(x_turned, b + 1)
                        for half in range(2):
                            act.copy(x_hi[:, half * 4 * CAP:(half + 1) * 4 * CAP], XT[:, half, 0:4 * CAP]).then_inc(x_hi_done, 1)

                    def step(b, first, last):
                        act.wait_ge(gate_done, b + 1)
                        wait_count(act, hid_done, b)
                        act.activation(gated[:, :], G[0:CAP, :], ACT.Silu, bias=t.zero_col[0:CAP, :]).then_inc(gated_done, 1)
                        if not first:
                            act.wait_ge(h_turned, b)
                            act.copy(h_hi[:, :], HT[:, 0:KH * CAP]).then_inc(h_hi_done, 1)
                        if not last:
                            split(0, b + 1, 0)
                            split(0, b + 1, 1)
                            x_part(b + 1)
                            split(1, b + 1, 0)
                            split(1, b + 1, 1)
                        else:
                            split(0, b + 1, 0)
                            split(0, b + 1, 1)
                        if not first:
                            act.wait_ge(down_done, 2 * b - 1)
                            wait_count(act, y_stored, 16 * (b - 1))
                            act.copy(y[:, 0:HALF], Y[0:CAP, 0, :]).then_inc(y_act, 1)
                        if not (first or last):
                            split(2, b, 0)
                            split(2, b, 1)

                    split(2, 0, 0)
                    split(2, 0, 1)
                    x_part(0)
                    last = in_turn(act, step)
                    act.wait_ge(h_turned, last + 1)
                    act.copy(h_hi[:, :], HT[:, 0:KH * CAP]).then_inc(h_hi_done, 1)
                    act.wait_ge(down_done, 2 * last + 1)
                    act.wait_ge(y_stored, 16 * last)
                    act.copy(y[:, 0:HALF], Y[0:CAP, 0, :]).then_inc(y_act, 1)

                @block.vector
                def _(dve):
                    def split(w, b, piece):
                        self.low_part(dve, w, b, piece)

                    def x_part(b):
                        for half in range(2):
                            dve.wait_ge(x_hi_done, 2 * b + half + 1)
                            cut = slice(half * 4 * CAP, (half + 1) * 4 * CAP)
                            dve.tensor_tensor(x_lo[:, cut], XT[:, half, 0:4 * CAP], x_hi[:, cut].bitcast(F32), ALU.subtract)\
                               .then_inc(x_lo_done, 1)

                    def h_part(b):
                        dve.wait_ge(h_hi_done, b + 1)
                        dve.tensor_tensor(h_lo[:, :], HT[:, 0:KH * CAP], h_hi[:, :].bitcast(F32), ALU.subtract)\
                           .then_inc(h_lo_done, 1)

                    def y_part(b):
                        dve.wait_ge(down_done, 2 * b + 2)
                        wait_count(dve, y_stored, 16 * b)
                        dve.tensor_copy(y[:, HALF:D], Y[0:CAP, 1, :]).then_inc(y_dve, 1)

                    def step(b, first, last):
                        if not first:
                            h_part(b - 1)
                        if not last:
                            split(0, b + 1, 0)
                            split(0, b + 1, 1)
                        dve.wait_ge(up_done, b + 1)
                        dve.tensor_tensor(hid[:, :].rearrange("q (k p) -> q p k", k=KH), gated[:, :]
                                          .rearrange("q (p k) -> q p k", k=KH), U[0:CAP, :]
                                          .rearrange("q (p k) -> q p k", k=KH), ALU.mult).then_inc(hid_done, 1)
                        if not last:
                            x_part(b + 1)
                            split(1, b + 1, 0)
                            split(1, b + 1, 1)
                        else:
                            split(0, b + 1, 0)
                            split(0, b + 1, 1)
                        if not first:
                            y_part(b - 1)
                        if not (first or last):
                            split(2, b, 0)
                            split(2, b, 1)

                    split(2, 0, 0)
                    split(2, 0, 1)
                    x_part(0)
                    last = in_turn(dve, step)
                    h_part(last)
                    y_part(last)



def mixture(t, name, args, layer):
    with ExitStack() as ctx:
        moe = Experts(t, name, args["moe_w_gate"][layer], args["moe_w_up"][layer], args["moe_w_down"][layer],
                      t.dram, ctx)
        route(t, f"{name}r", args["norm_ffn"][layer:layer + 1, :], args["moe_w_group"][layer],
              args["moe_b_group"][layer], args["moe_w_router"][layer], args["moe_b_router"][layer], moe)
        moe.run()


def program(nc, args, out, stages=99):
    with ExitStack() as stack:
        t = Trunk(nc, stack)
        dram = lambda n, shape, dt: nc.dram_tensor(n, shape, dt, kind="Internal").ap()
        t.dram = (dram("hn_rows", (T, D), F32), dram("out_rows", (ROWS * CAP, D), F32))
        setup(t)
        if stages >= 1:
            windowed_attention(t, args["norm_mix"][0:1, :], args["swa_w_qkv"][0], args["swa_w_o"][0],
                               args["swa_sink"][0:1, :], args["x"][0])
        if stages >= 2:
            mixture(t, "m0", args, 0)
            t.clear_semaphores()
        if stages >= 3:
            differential_attention(t, args["norm_mix"][1:2, :], args["diff_w_qkv"][0], args["diff_w_o"][0],
                                   args["diff_lambda"][0], args["diff_subln"][0], 0.8 - 0.6 * math.exp(-0.3), dram("x_rows", (T, D), F32))
        if stages >= 4:
            mixture(t, "m1", args, 1)
        if stages >= 5:
            return final_norm(t, args["final_norm"].unsqueeze(0), out)
        stored = t.sem("out_stored")
        with nc.Block() as block:
            @block.sync
            def _(sp):
                for tt in range(NT):
                    sp.dma_start(out[0, tt * P:(tt + 1) * P, :], t.x[:, tt, :]).then_inc(stored, 16)
                sp.wait_ge(stored, 16 * NT)


_INS = ("x", "norm_mix", "norm_ffn", "swa_w_qkv", "swa_w_o", "swa_sink", "diff_w_qkv", "diff_w_o", "diff_lambda",
        "diff_subln", "moe_w_group", "moe_b_group", "moe_w_router", "moe_b_router", "moe_w_gate", "moe_w_up",
        "moe_w_down", "final_norm")


def kernel(**inputs):
    import numpy as np
    import concourse.bacc as bacc
    from concourse.bass_utils import run_bass_kernel_spmd

    nc = bacc.Bacc("TRN2", target_bir_lowering=False, num_devices=1)
    arrays, args = {}, {}
    for name in _INS:
        a = np.ascontiguousarray(inputs[name])
        arrays[f"in_{name}_dram"] = a
        args[name] = nc.dram_tensor(f"in_{name}_dram", a.shape, mybir.dt.from_np(a.dtype), kind="ExternalInput").ap()
    out = nc.dram_tensor("out_0_dram", (1, T, D), F32, kind="ExternalOutput").ap()
    program(nc, args, out)
    r = run_bass_kernel_spmd(nc, [arrays], core_ids=[0])
    return r.results[0]["out_0_dram"]
```
